# Optimizing a Trainium2 kernel written in Bass

```python
import math
import jax, jax.numpy as jnp
from jax import lax
import numpy as np

D_MODEL = 1024
BATCH = 1
SEQ = 512
DEPTH = 1

S5_WIDTH = D_MODEL // 2
S5_GROUP = 16
S5_GROUPS = S5_WIDTH // S5_GROUP
S5_STATE = 64
DT_MIN = 1e-3
DT_MAX = 1e-1
RET_HEADS = 4
RET_DK = D_MODEL // 8
RET_DV = 2 * RET_DK
RET_QK_WIDTH = RET_HEADS * RET_DK
RET_V_WIDTH = RET_HEADS * RET_DV
RET_CHUNK = 128
ROPE_BASE = 10000.0
N_EXPERTS = 32
TOP_K = 4
D_FF = D_MODEL
SWIGLU_ALPHA = 1.702
SWIGLU_LIMIT = 7.0
MOE_BLOCK = 128
NORM_EPS = 1e-5
IN_WIDTH = S5_WIDTH + 2 * RET_QK_WIDTH + 2 * RET_V_WIDTH + 2 * D_MODEL
SPLIT_POINTS = (
    S5_WIDTH,
    S5_WIDTH + RET_QK_WIDTH,
    S5_WIDTH + 2 * RET_QK_WIDTH,
    S5_WIDTH + 2 * RET_QK_WIDTH + RET_V_WIDTH,
    S5_WIDTH + 2 * RET_QK_WIDTH + 2 * RET_V_WIDTH,
    S5_WIDTH + 2 * RET_QK_WIDTH + 2 * RET_V_WIDTH + D_MODEL,
)

kernel_name = "hybrid_s5_retention_gated_moe"

F32 = jnp.float32

def rms_norm(x, g):
    xf = x.astype(F32)
    y = xf * lax.rsqrt(jnp.mean(xf * xf, axis=-1, keepdims=True) + NORM_EPS)
    return (y * g.astype(F32)).astype(x.dtype)

def s5_mixer(u, lam_re, lam_im, log_dt, b_re, b_im, c_re, c_im, d_skip, w_glu, b_glu):
    bsz, seqlen, _ = u.shape
    dt = jnp.exp(log_dt.astype(F32))[:, None]
    lr, li = lam_re.astype(F32), lam_im.astype(F32)
    mag = jnp.exp(lr * dt)
    abar_re, abar_im = mag * jnp.cos(li * dt), mag * jnp.sin(li * dt)
    nr, ni = abar_re - 1.0, abar_im
    den = lr * lr + li * li
    f_re = (nr * lr + ni * li) / den
    f_im = (ni * lr - nr * li) / den
    ug = jnp.swapaxes(u, 0, 1).reshape(seqlen, bsz, S5_GROUPS, S5_GROUP).astype(F32)
    bu_re = jnp.einsum('lbgc,gnc->lbgn', ug, b_re.astype(F32))
    bu_im = jnp.einsum('lbgc,gnc->lbgn', ug, b_im.astype(F32))
    x_re = f_re * bu_re - f_im * bu_im
    x_im = f_re * bu_im + f_im * bu_re
    a_re = jnp.broadcast_to(abar_re[None, None], (seqlen, 1, S5_GROUPS, S5_STATE))
    a_im = jnp.broadcast_to(abar_im[None, None], (seqlen, 1, S5_GROUPS, S5_STATE))

    def combine(e1, e2):
        a1r, a1i, b1r, b1i = e1
        a2r, a2i, b2r, b2i = e2
        return (a2r * a1r - a2i * a1i,
                a2r * a1i + a2i * a1r,
                a2r * b1r - a2i * b1i + b2r,
                a2r * b1i + a2i * b1r + b2i)

    _, _, s_re, s_im = lax.associative_scan(combine, (a_re, a_im, x_re, x_im), axis=0)
    y = (jnp.einsum('lbgn,gcn->lbgc', s_re, c_re.astype(F32))
         - jnp.einsum('lbgn,gcn->lbgc', s_im, c_im.astype(F32)))
    y = jnp.swapaxes(y.reshape(seqlen, bsz, S5_WIDTH), 0, 1).astype(u.dtype) + d_skip * u
    z = jax.nn.gelu(y)
    return z * jax.nn.sigmoid(z @ w_glu + b_glu)

def rotary(x, positions):
    half = x.shape[-1] // 2
    inv_freq = ROPE_BASE ** (-jnp.arange(half, dtype=F32) / half)
    ang = positions.astype(F32)[..., None, None] * inv_freq
    cos, sin = jnp.cos(ang), jnp.sin(ang)
    x1, x2 = x[..., :half].astype(F32), x[..., half:].astype(F32)
    return jnp.concatenate([x1 * cos - x2 * sin, x2 * cos + x1 * sin], axis=-1).astype(x.dtype)

def retention(q, k, v):
    bsz, seqlen = q.shape[:2]
    n_chunks = seqlen // RET_CHUNK
    dt = q.dtype
    log_g = jnp.log1p(-(2.0 ** (-5.0 - jnp.arange(RET_HEADS, dtype=F32))))
    pos = jnp.arange(RET_CHUNK, dtype=F32)
    rel = pos[:, None] - pos[None, :]
    intra = jnp.where(rel >= 0, jnp.exp(log_g[:, None, None] * jnp.maximum(rel, 0.0)), 0.0).astype(dt)
    q_decay = jnp.exp(log_g[:, None] * (pos + 1.0)).astype(dt)
    k_decay = jnp.exp(log_g[:, None] * (RET_CHUNK - 1.0 - pos)).astype(dt)
    chunk_decay = jnp.exp(log_g * RET_CHUNK).astype(dt)

    def to_chunks(t):
        return t.reshape(bsz, n_chunks, RET_CHUNK, RET_HEADS, t.shape[-1]).transpose(1, 0, 3, 2, 4)

    def step(state, chunk):
        qc, kc, vc = chunk
        scores = jnp.einsum('bhid,bhjd->bhij', qc, kc) * intra
        inner = jnp.einsum('bhij,bhjv->bhiv', scores, vc)
        cross = jnp.einsum('bhid,bhdv->bhiv', qc * q_decay[:, :, None], state)
        state = chunk_decay[:, None, None] * state + jnp.einsum('bhjd,bhjv->bhdv', kc * k_decay[:, :, None], vc)
        return state, inner + cross

    state0 = jnp.zeros((bsz, RET_HEADS, RET_DK, RET_DV), dt)
    _, out = lax.scan(step, state0, (to_chunks(q), to_chunks(k), to_chunks(v)))
    return out.transpose(1, 0, 3, 2, 4).reshape(bsz, seqlen, RET_HEADS, RET_DV)

def head_group_norm(y, g):
    yf = y.astype(F32)
    mu = jnp.mean(yf, axis=-1, keepdims=True)
    var = jnp.mean(jnp.square(yf - mu), axis=-1, keepdims=True)
    yn = (yf - mu) * lax.rsqrt(var + NORM_EPS)
    yn = yn.reshape(y.shape[0], y.shape[1], RET_V_WIDTH) * g.astype(F32)
    return yn.astype(y.dtype)

def clamped_swiglu(gu):
    x_glu = jnp.minimum(gu[..., ::2], SWIGLU_LIMIT)
    x_lin = jnp.clip(gu[..., 1::2], -SWIGLU_LIMIT, SWIGLU_LIMIT)
    return x_glu * jax.nn.sigmoid(SWIGLU_ALPHA * x_glu) * (x_lin + 1.0)

def moe_ffn(h, router_w, router_b, w1, b1, w2, b2):
    bsz, seqlen, d = h.shape
    n_tok = bsz * seqlen
    ht = h.reshape(n_tok, d)
    logits = ht.astype(F32) @ router_w.astype(F32) + router_b.astype(F32)
    top_vals, top_idx = lax.top_k(logits, TOP_K)
    gates = jax.nn.softmax(top_vals, axis=-1)
    n_assign = n_tok * TOP_K
    flat_e = top_idx.reshape(n_assign)
    flat_tok = jnp.arange(n_assign, dtype=jnp.int32) // TOP_K
    order = jnp.argsort(flat_e)
    e_sorted = flat_e[order]
    tok_sorted = flat_tok[order]
    gate_sorted = gates.reshape(n_assign)[order]
    counts = jnp.bincount(flat_e, length=N_EXPERTS)
    padded = (counts + MOE_BLOCK - 1) // MOE_BLOCK * MOE_BLOCK
    start = jnp.cumsum(counts) - counts
    pend = jnp.cumsum(padded)
    pstart = pend - padded
    dest = pstart[e_sorted] + jnp.arange(n_assign, dtype=jnp.int32) - start[e_sorted]
    n_blocks = (n_assign + MOE_BLOCK - 1) // MOE_BLOCK + N_EXPERTS
    n_rows = n_blocks * MOE_BLOCK
    x_rows = jnp.zeros((n_rows, d), h.dtype).at[dest].set(ht[tok_sorted])
    block_start = jnp.arange(n_blocks, dtype=pend.dtype) * MOE_BLOCK
    block_expert = jnp.minimum(jnp.searchsorted(pend, block_start, side='right'), N_EXPERTS - 1)

    def expert_block(args):
        xb, e = args
        gu = xb @ w1[e] + b1[e]
        return clamped_swiglu(gu) @ w2[e] + b2[e]

    y_rows = lax.map(expert_block, (x_rows.reshape(n_blocks, MOE_BLOCK, d), block_expert))
    y_rows = y_rows.reshape(n_rows, d)
    y = jax.ops.segment_sum(y_rows[dest] * gate_sorted[:, None].astype(h.dtype), tok_sorted,
                            num_segments=n_tok)
    return y.reshape(bsz, seqlen, d)

def setup_inputs(seed: int = 0) -> dict:
    key = jax.random.key(seed)
    ks = jax.random.split(key, 24)
    L = DEPTH
    G, N, W = S5_GROUPS, S5_STATE, S5_WIDTH

    def nrm(k, shape, scale):
        return jax.random.normal(k, shape, F32) * scale

    x = nrm(ks[0], (BATCH, SEQ, D_MODEL), 1.0)
    positions = jnp.broadcast_to(jnp.arange(SEQ, dtype=jnp.int32)[None, :], (BATCH, SEQ))
    norm_mix_g = 1.0 + nrm(ks[1], (L, D_MODEL), 0.02)
    w_in = nrm(ks[2], (L, D_MODEL, IN_WIDTH), D_MODEL ** -0.5)
    s5_lambda_re = -0.5 + nrm(ks[3], (L, G, N), 0.01)
    s5_lambda_im = math.pi * jnp.arange(N, dtype=F32) + nrm(ks[4], (L, G, N), 0.01)
    s5_log_dt = jax.random.uniform(ks[5], (L, G), F32, math.log(DT_MIN), math.log(DT_MAX))
    s5_b_re = nrm(ks[6], (L, G, N, S5_GROUP), (2 * S5_GROUP) ** -0.5)
    s5_b_im = nrm(ks[7], (L, G, N, S5_GROUP), (2 * S5_GROUP) ** -0.5)
    s5_c_re = nrm(ks[8], (L, G, S5_GROUP, N), (2 * N) ** -0.5)
    s5_c_im = nrm(ks[9], (L, G, S5_GROUP, N), (2 * N) ** -0.5)
    s5_d = nrm(ks[10], (L, W), 1.0)
    s5_w_glu = nrm(ks[11], (L, W, W), W ** -0.5)
    s5_b_glu = nrm(ks[12], (L, W), 0.01)
    ret_gn_g = 1.0 + nrm(ks[13], (L, RET_V_WIDTH), 0.02)
    w_branch_s5 = nrm(ks[14], (L, W, D_MODEL), W ** -0.5)
    w_branch_ret = nrm(ks[15], (L, RET_V_WIDTH, D_MODEL), RET_V_WIDTH ** -0.5)
    w_out = nrm(ks[16], (L, D_MODEL, D_MODEL), D_MODEL ** -0.5)
    norm_ffn_g = 1.0 + nrm(ks[17], (L, D_MODEL), 0.02)
    router_w = nrm(ks[18], (L, D_MODEL, N_EXPERTS), D_MODEL ** -0.5)
    router_b = nrm(ks[19], (L, N_EXPERTS), 0.01)
    expert_w1 = nrm(ks[20], (L, N_EXPERTS, D_MODEL, 2 * D_FF), D_MODEL ** -0.5)
    expert_b1 = nrm(ks[21], (L, N_EXPERTS, 2 * D_FF), 0.01)
    expert_w2 = nrm(ks[22], (L, N_EXPERTS, D_FF, D_MODEL), D_FF ** -0.5)
    k23a, k23b = jax.random.split(ks[23])
    expert_b2 = nrm(k23a, (L, N_EXPERTS, D_MODEL), 0.01)
    norm_final_g = 1.0 + nrm(k23b, (D_MODEL,), 0.02)
    return {"x": x, "positions": positions, "norm_mix_g": norm_mix_g, "w_in": w_in,
            "s5_lambda_re": s5_lambda_re, "s5_lambda_im": s5_lambda_im, "s5_log_dt": s5_log_dt,
            "s5_b_re": s5_b_re, "s5_b_im": s5_b_im, "s5_c_re": s5_c_re, "s5_c_im": s5_c_im,
            "s5_d": s5_d, "s5_w_glu": s5_w_glu, "s5_b_glu": s5_b_glu, "ret_gn_g": ret_gn_g,
            "w_branch_s5": w_branch_s5, "w_branch_ret": w_branch_ret, "w_out": w_out,
            "norm_ffn_g": norm_ffn_g, "router_w": router_w, "router_b": router_b,
            "expert_w1": expert_w1, "expert_b1": expert_b1, "expert_w2": expert_w2,
            "expert_b2": expert_b2, "norm_final_g": norm_final_g}

def reference(x, positions, norm_mix_g, w_in, s5_lambda_re, s5_lambda_im, s5_log_dt,
              s5_b_re, s5_b_im, s5_c_re, s5_c_im, s5_d, s5_w_glu, s5_b_glu, ret_gn_g,
              w_branch_s5, w_branch_ret, w_out, norm_ffn_g, router_w, router_b,
              expert_w1, expert_b1, expert_w2, expert_b2, norm_final_g):
    bsz, seqlen, _ = x.shape
    for layer in range(DEPTH):
        h = rms_norm(x, norm_mix_g[layer])
        proj = h @ w_in[layer]
        u_s5, q, k, v, g_ret, gate_a, gate_b = jnp.split(proj, SPLIT_POINTS, axis=-1)
        y_s5 = s5_mixer(u_s5, s5_lambda_re[layer], s5_lambda_im[layer], s5_log_dt[layer],
                        s5_b_re[layer], s5_b_im[layer], s5_c_re[layer], s5_c_im[layer],
                        s5_d[layer], s5_w_glu[layer], s5_b_glu[layer])
        y_a = y_s5 @ w_branch_s5[layer]
        q = rotary(q.reshape(bsz, seqlen, RET_HEADS, RET_DK), positions)
        k = rotary(k.reshape(bsz, seqlen, RET_HEADS, RET_DK), positions) * (RET_DK ** -0.5)
        v = v.reshape(bsz, seqlen, RET_HEADS, RET_DV)
        ret = head_group_norm(retention(q, k, v), ret_gn_g[layer])
        y_b = (jax.nn.silu(g_ret) * ret) @ w_branch_ret[layer]
        merged = jax.nn.sigmoid(gate_a) * y_a + jax.nn.sigmoid(gate_b) * y_b
        x = x + merged @ w_out[layer]
        h2 = rms_norm(x, norm_ffn_g[layer])
        x = x + moe_ffn(h2, router_w[layer], router_b[layer], expert_w1[layer],
                        expert_b1[layer], expert_w2[layer], expert_b2[layer])
    return rms_norm(x, norm_final_g)


_drawn_inputs = setup_inputs


def setup_inputs(seed=0):
    import zlib

    import numpy as np

    out = dict(_drawn_inputs(seed))
    spreads = {}
    factors = {'s5_lambda_re': 200.0,
     's5_b_glu': 7.111,
     'expert_b1': 8.0,
     'expert_b2': 8.0,
     'norm_final_g': 21.379,
     's5_lambda_im': 23.2,
     's5_log_dt': 27.736,
     's5_b_re': 27.992,
     's5_b_im': 26.848,
     's5_c_re': 29.16,
     's5_c_im': 8.0}
    for name, (base, spread) in spreads.items():
        noise = np.random.default_rng([zlib.crc32(name.encode()), seed]).standard_normal(out[name].shape)
        drawn = base * np.exp(spread * noise) if base else spread * noise
        out[name] = __import__('jax').numpy.asarray(drawn.astype(out[name].dtype))
    for name, factor in factors.items():
        out[name] = (out[name] * factor).astype(out[name].dtype)
    return out
```

```python
from contextlib import ExitStack

import numpy as np

import concourse.bass as bass
from concourse import mybir

F32 = mybir.dt.float32
I32 = mybir.dt.int32
U32 = mybir.dt.uint32
ALU = mybir.AluOpType
ACT = mybir.ActivationFunctionType
AX = mybir.AxisListType

P = 128
D = 1024
SEQ = 512
NT = SEQ // P
KD = D // P
S5W = 512
GRP = 16
NG = S5W // GRP
NS = 64
GP = NG // 2
BT = P // GRP
NB = SEQ // BT
HEADS, DK, DV = 4, 128, 256
E, TOPK, DFF = 32, 4, 1024
FT = DFF // P
NA = SEQ * TOPK
EPS = 1e-5
LIMIT, SIG_ALPHA = 7.0, 1.702

CH = 2048
CW = CH // KD
C_U, C_Q, C_K, C_V, C_G, C_GA, C_GB = 0, 2, 4, 6, 10, 14, 18
C_GLU, C_BS5, C_BRET, C_OUT = 22, 23, 25, 29
N_TRUNK = 33
RING_T = 4
RING = 12
EC = 12
W2C = 4
N_SMALL = 96
NO_SLOT = 1 << 13

PAR = {}
_at = 0
for _n, _w in (("norm_mix", KD), ("ret_gn", KD), ("d_skip", S5W // P), ("b_glu", S5W // P),
               ("lam_re", GP), ("lam_im", GP), ("log_dt", GP), ("router_b", E)):
    PAR[_n] = (_at, _w)
    _at += _w
N_PAR = _at
CST = {}
_at = 0
for _n, _w in (("ident", P), ("before", P), ("ones", P), ("expert_id", E), ("assign_id", NT * TOPK),
               ("inv_freq", 1), ("sin_sign", 1)):
    CST[_n] = (_at, _w)
    _at += _w
N_CST = _at

TWO_PI = 2 * np.pi
PI_1 = 6.28125
PI_2 = float(np.float32(int((TWO_PI - PI_1) * 2 ** 21) / 2 ** 21))
PI_3 = float(np.float32(TWO_PI - PI_1 - PI_2))
PI_IN = 3.1415925
ROUND = 1.5 * 2 ** 23

JOBS = []


def _jobs(name, n, engine):
    JOBS.extend((f"{name}{i}", engine) for i in range(n))


_jobs("xT", KD, "A")
_jobs("u", 4, "A")
_jobs("ua", BT, "A")
_jobs("ub", 4, "V")
_jobs("q", HEADS, "V")
_jobs("k", HEADS, "V")
_jobs("hT", 8, "A")
_jobs("kb", 2, "V")
_jobs("xs", 4, "V")
_jobs("v", 8, "A")
for _h in range(HEADS):
    JOBS.extend([(f"sc{_h * 4 + j}", "V") for j in range(4)] + [(f"in{_h * 2 + j}", "V") for j in range(2)])
_jobs("g", KD, "A")
_jobs("rT", KD, "V")
_jobs("ys", 4, "V")
_jobs("yc", BT, "A")
_jobs("yd", 4, "V")
_jobs("ga", KD, "A")
_jobs("gb", KD, "A")
_jobs("z", 4, "A")
_jobs("ya", KD, "V")
_jobs("yb", KD, "V")
_jobs("wo", 8, "V")
_jobs("h2T", KD, "A")
_jobs("lg", 1, "V")
_jobs("rk", 1, "V")
_jobs("gT", 1, "V")
_jobs("b2", 8, "V")
_jobs("tb", 1, "V")
LAST_USE = [f"{name}{i}" for name, ids in (
    ("u", (1, 3)), ("q", (1, 3)), ("k", (1, 3)), ("v", (1, 3, 5, 7)), ("g", (1, 3, 5, 7)), ("ga", (1, 3, 5, 7)),
    ("gb", (1, 3, 5, 7)), ("z", (3,)), ("ya", (3, 7)), ("yb", (1, 3, 5, 7)), ("wo", (1, 3, 5, 7))) for i in ids]
JOB = {name: n for n, (name, _) in enumerate(JOBS)}
EMPTIED = []
_c = {"A": 0, "V": 0}
for _name, _e in JOBS:
    _c[_e] += 1
    EMPTIED.append((_e, _c[_e]))


def build(nc, x, pos, wt, we, par, s5bc, b1, b2, rw, g_ffn, g_fin, cst, dmask, fill, out):
    h2_dram = nc.dram_tensor("h2_rows", (SEQ, D), F32).ap()
    y_dram = nc.dram_tensor("y_rows", (NA, D), F32).ap()
    slot_dram = nc.dram_tensor("slots", (E * SEQ, 1), I32).ap()

    with ExitStack() as ctx:
        def sb(name, shape, dt=F32):
            return ctx.enter_context(nc.sbuf_tensor(name, shape, dt))

        def sem(name):
            return ctx.enter_context(nc.semaphore(name))

        bank = [ctx.enter_context(nc.psum_tensor(f"bank{i}", [P, 512], F32)) for i in range(8)]

        ring = sb("ring", [P, RING, CH])
        big = [sb(f"big{i}", [P, 4096]) for i in range(6)]
        uT = sb("uT", [P, 4, SEQ])
        par_s = sb("par_s", [P, N_PAR])
        cst_s = sb("cst_s", [P, N_CST])

        def prm(name, i=None, n=1):
            a, w = PAR[name]
            return par_s[:, a:a + w] if i is None else par_s[:, a + i:a + i + n]

        def con(name):
            a, w = CST[name]
            return cst_s[:, a:a + w]

        ident, ones = con("ident"), con("ones")

        hT = big[0][:, :].rearrange("p (k t) -> p k t", k=KD)
        xn = big[1][:, :].rearrange("p (i d) -> p i d", i=NT)
        vt = xn
        gs = big[1][:, :].rearrange("p (k t) -> p k t", k=KD)
        qT = big[2][:, 0:2048].rearrange("p (h t) -> p h t", h=HEADS)
        kT = big[2][:, 2048:4096].rearrange("p (h t) -> p h t", h=HEADS)
        siga = big[2][:, :].rearrange("p (k t) -> p k t", k=KD)
        cosT, sinT = big[3][:, 0:SEQ], big[3][:, SEQ:2 * SEQ]
        rope_k = big[3][:, 1024:1536]
        rope_t = big[3][:, 1536:2048]
        sT = big[3][:, 0:2048].rearrange("p (j t) -> p j t", j=NT)
        decay = big[3][:, 2048:4096].rearrange("p (h t) -> p h t", h=HEADS)
        sigb = big[3][:, :].rearrange("p (k t) -> p k t", k=KD)
        ret = big[4][:, :].rearrange("p (i d) -> p i d", i=NT)
        rot_a, rot_b = big[4][:, 0:512], big[4][:, 512:1024]
        pos_i = big[4][:, 1024:1536].bitcast(I32)
        mg = big[4][:, :].rearrange("p (k t) -> p k t", k=KD)
        x2 = big[0][:, :].rearrange("p (i d) -> p i d", i=NT)
        h2 = big[1][:, :].rearrange("p (i d) -> p i d", i=NT)
        h2T = big[2][:, :].rearrange("p (k t) -> p k t", k=KD)

        s5a = ring[:, 6:8, :].rearrange("p a b -> p (a b)")
        s5b = ring[:, 8:10, :].rearrange("p a b -> p (a b)")
        pbr = s5a[:, 0:2048].rearrange("p (g m c) -> p g m c", g=GP, m=BT)
        pbi = s5a[:, 2048:4096].rearrange("p (g m c) -> p g m c", g=GP, m=BT)
        gre, gim = pbr, pbi
        yjr = s5a.rearrange("p (r c) -> p r c", r=BT)
        hTr = s5b[:, 0:2048].rearrange("p (g n) -> p g n", g=GP)
        hTi = s5b[:, 2048:4096].rearrange("p (g n) -> p g n", g=GP)
        m0T = s5b.rearrange("p (g n) -> p g n", g=NG)
        m0r = big[5][:, :].rearrange("p (r n) -> p r n", r=BT)
        ub = ring[:, 10, :].rearrange("p (g j) -> p g j", g=NG)
        xr = ring[:, 11, 0:1024].rearrange("p (g j) -> p g j", g=GP)
        xi = ring[:, 11, 1024:2048].rearrange("p (g j) -> p g j", g=GP)
        ujr = big[5][:, :].rearrange("p (g r c) -> p g r c", g=NG, r=BT)
        sc1 = big[5][:, 0:1024].rearrange("p (g j) -> p g j", g=GP)
        sc2 = big[5][:, 1024:2048].rearrange("p (g j) -> p g j", g=GP)
        ysb = big[5][:, 2048:4096].rearrange("p (g j) -> p g j", g=NG)
        zT = big[5][:, 0:2048].rearrange("p (k t) -> p k t", k=4)
        zg = big[5][:, 2048:4096].rearrange("p (k t) -> p k t", k=4)
        k7 = ring[:, 4, 0:512]
        s5in = ring[:, 4, 512:1536].rearrange("p (a n) -> p a n", a=4)
        s5p = ring[:, 4, 1536:1536 + 24 * GP].rearrange("p (a n) -> p a n", a=24)
        bb = ring[:, 5, 0:3 * GP * GRP].rearrange("p (a n) -> p a n", a=3)

        xe = big[1][:, :].rearrange("p (b d) -> p b d", b=NT)
        xeT = big[2][:, :].rearrange("p (k t) -> p k t", k=KD)
        aT = big[3][:, :].rearrange("p (k t) -> p k t", k=KD)
        ye = big[4][:, :].rearrange("p (b d) -> p b d", b=NT)
        tmp = big[5][:, :].rearrange("p (a b t) -> p a b t", a=4, b=2)
        g_t, l_t, sg_t, gs_t = (tmp[:, i] for i in range(4))
        yk = [big[i][:, :].rearrange("p (k d) -> p k d", k=TOPK) for i in (1, 2)]
        flat_u = uT[:, :, :].rearrange("p c t -> p (c t)")
        gvec = flat_u[:, 0:D]
        b2_s = flat_u[0:E, D:2 * D]

        ss = sb("ss", [P, 4 * NT])
        stat = sb("stat", [P, NT, 8])
        mv = sb("mv", [P, NT, 4])
        b1_s = sb("b1_s", [P, E, 2 * FT])
        b1e = sb("b1e", [P, 2 * FT])
        rw_s = sb("rw_s", [P, KD, E])
        at = [0]

        def tmp_tile(rows, *shape):
            n = int(np.prod(shape))
            ap = big[5][0:rows, at[0]:at[0] + n]
            at[0] += n
            names = "abc"[:len(shape)]
            if len(shape) == 1:
                return ap
            return ap.rearrange(f"p ({' '.join(names)}) -> p {' '.join(names)}", **dict(zip(names, shape)))

        lg, cum, hot, gte = (tmp_tile(P, NT, E) for _ in range(4))
        oneh, wrk = (tmp_tile(P, NT, TOPK, E) for _ in range(2))
        pairs, is_long = tmp_tile(1, E, E), sb("is_long", [1, E])[:, :]
        gTs, tabf = tmp_tile(E, SEQ), tmp_tile(E, SEQ)
        tabi = tmp_tile(E, SEQ).bitcast(I32)
        top_v = sb("top_v", [P, NT, 8])
        top_i = sb("top_i", [P, NT, 8], U32)
        top_f = sb("top_f", [P, NT, 8])
        gate = sb("gate", [P, NT, TOPK])
        negm = sb("negm", [P, NT])
        gsum = sb("gsum", [P, 2 * NT])
        rank = sb("rank", [P, NT * TOPK])
        dest = sb("dest", [P, NT * TOPK], U32)
        aid = sb("aid", [P, NT * TOPK], I32)
        cnt = sb("cnt", [1, E], I32)
        n_long = sb("n_long", [1, E], I32)
        put_i = sb("put_i", [P, NT, E], I32)
        get_e, put_e = sb("get_e", [P, NT], I32), sb("put_e", [P, NT], I32)
        get_i = sb("get_i", [P, NT, E], I32)

        landed = [sem(f"landed{i}") for i in range(RING)]
        bank_full = sem("bank_full")
        act_emptied, dve_emptied = sem("act_emptied"), sem("dve_emptied")
        act_chain, dve_chain, pool_chain = sem("act_chain"), sem("dve_chain"), sem("pool_chain")
        x_in, x_in2 = [sem(f"x_in{i}") for i in range(NT)], [sem(f"x_again{i}") for i in range(NT)]
        par_in, cst_in, pos_in, dec_in = sem("par_in"), sem("cst_in"), sem("pos_in"), sem("dec_in")
        moe_in, gf_in, gfin_in = sem("moe_in"), sem("gf_in"), sem("gfin_in")
        squares, rstd_ready, xn_ready = sem("squares"), sem("rstd_ready"), sem("xn_ready")
        rope_act = sem("rope_act")
        s5_act, s5_pool = sem("s5_act"), sem("s5_pool")
        pb_ready, g_ready, scan_done = sem("pb_ready"), sem("g_ready"), sem("scan_done")
        m0_zero, m0_in, m0_ready = sem("m0_zero"), sem("m0_in"), sem("m0_ready")
        gn_var, gn_rstd = sem("gn_var"), sem("gn_rstd")
        z_lin, z_ready, zg_ready = sem("z_lin"), sem("z_ready"), sem("zg_ready")
        h2_ready, h2_out = sem("h2_ready"), sem("h2_out")
        top_ready, gate_exp = sem("top_ready"), sem("gate_exp")
        hot_ready, gte_ready = sem("hot_ready"), sem("gte_ready")
        fill_in, dest_ready, slots_put, slots_in = sem("fill_in"), sem("dest_ready"), sem("slots_put"), sem("slots_in")
        tabf_ready = sem("tabf_ready")
        got = [sem(f"got{b}") for b in range(NT)]
        put = [sem(f"put{b}") for b in range(NT)]
        get_e_ready, put_e_ready = sem("get_e_ready"), sem("put_e_ready")
        index_seen = sem("index_seen")
        ye_free = sem("ye_free")
        xe_zero = sem("xe_zero")
        gu_full, gu_empty = sem("gu_full"), sem("gu_empty")
        glu_ready, sg_ready, gs_ready, act_ready = sem("glu_ready"), sem("sig_ready"), sem("gs_ready"), sem("act_ready")
        b1_ready, b1e_ready = sem("b1_ready"), sem("b1e_ready")
        t_full, t_empty = sem("rows_full"), sem("rows_empty")
        y_full, y_empty = sem("y_full"), sem("y_empty")
        angles, den_ready, neg_c, tab_ready = sem("angles"), sem("den_ready"), sem("neg_c"), sem("tab_ready")
        yk_in = [sem("yk_in0"), sem("yk_in1")]
        summed, fsq, frstd, fin_ready, out_done = sem("summed"), sem("fsq"), sem("frstd"), sem("fin_ready"), sem("out_done")
        dumped = sem("dumped")

        EMPT = {"A": act_emptied, "V": dve_emptied}

        def full(name):
            return bank_full, JOB[name] + 1

        def emptied(name):
            e, n = EMPTIED[JOB[name]]
            return EMPT[e], n

        def bk(name):
            return bank[JOB[name] % 8]

        def bc(ap, n):
            return ap.unsqueeze(2).to_broadcast([ap.shape[0], ap.shape[1], n])

        block = ctx.enter_context(nc.Block())

        @block.sync
        def _(sp):
            sp.dma_start(cst_s[:, :], cst).then_inc(cst_in, 16)
            for n in range(N_TRUNK):
                if n >= RING_T:
                    sp.wait_ge(*full(LAST_USE[n - RING_T]))
                sp.dma_start(ring[:, n % RING_T, :], wt[n]).then_inc(landed[n % RING_T], 16)
                if n == 1:
                    sp.dma_start(decay, dmask).then_inc(dec_in, 16)
            sp.wait_ge(*emptied("yd3"))
            for c in range(EC):
                slot = (RING_T + c) % RING
                if slot < RING_T:
                    last = max(n for n in range(N_TRUNK) if n % RING_T == slot)
                    sp.wait_ge(*full(LAST_USE[last]))
                sp.dma_start(ring[:, slot, :], we[0, c]).then_inc(landed[slot], 16)
            with sp.Fori(1, E) as e:
                for c in range(EC):
                    slot = (RING_T + c) % RING
                    if c < FT:
                        sp.wait_ge(gu_full, e * FT + (c + 1 - FT))
                    else:
                        sp.wait_ge(y_full, e * W2C + (c - FT + 1 - W2C))
                    sp.dma_start(ring[:, slot, :], we[bass.ds(e, 1), c].rearrange("o p n -> (o p) n"))\
                        .then_inc(landed[slot], 16)
            sp.wait_ge(ye_free, E)
            for i in range(NT):
                if i >= 2:
                    sp.wait_ge(summed, i - 1)
                sp.dma_start(yk[i % 2], y_dram.rearrange("(i p k) d -> i p k d", i=NT, p=P)[i])\
                    .then_inc(yk_in[i % 2], 16)
            for i in range(NT):
                sp.wait_ge(fin_ready, i + 1)
                sp.dma_start(out[i * P:(i + 1) * P, :], x2[:, i, :]).then_inc(out_done, 16)
            sp.wait_ge(out_done, 16 * NT)

        @block.gpsimd
        def _(pool):
            n_chain = [0]

            def step(ins):
                n_chain[0] += 1
                ins.then_inc(pool_chain, 1)
                pool.wait_ge(pool_chain, n_chain[0])

            TT = pool.tensor_tensor
            rs = ss[:, NT:2 * NT]
            mhalf = ss[:, 3 * NT:4 * NT]
            step(pool.memset(mhalf, -0.5))

            def rsqrt(dst, src, scale):
                step(pool.tensor_scalar(dst, src, scale, EPS, ALU.mult, ALU.add))
                return TT(dst, dst, mhalf, ALU.pow)

            pool.wait_ge(squares, NT)
            rsqrt(rs, ss[:, 0:NT], 1.0 / D).then_inc(rstd_ready, 1)

            pr = lambda i: s5p[:, i, :]
            DT, TH, MAG, SIN, COS, AR, AI, NR, T1, T2, DEN, FR, FI, T3, KR, RR, A8R, A8I = range(18)
            pool.wait_ge(par_in, 32)
            pool.wait_ge(s5_act, 1)
            step(TT(pr(T1), prm("lam_re"), pr(DT), ALU.mult))
            TT(pr(TH), prm("lam_im"), pr(DT), ALU.mult).then_inc(s5_pool, 1)
            pool.wait_ge(s5_act, 4)
            step(TT(pr(AR), pr(MAG), pr(COS), ALU.mult))
            step(TT(pr(AI), pr(MAG), pr(SIN), ALU.mult))
            step(pool.tensor_scalar(pr(NR), pr(AR), 1.0, -1.0, ALU.mult, ALU.add))
            step(TT(pr(T1), prm("lam_re"), prm("lam_re"), ALU.mult))
            step(TT(pr(T2), prm("lam_im"), prm("lam_im"), ALU.mult))
            TT(pr(DEN), pr(T1), pr(T2), ALU.add).then_inc(s5_pool, 1)
            pool.wait_ge(s5_pool, 2)
            step(TT(pr(T1), pr(NR), prm("lam_re"), ALU.mult))
            step(TT(pr(T2), pr(AI), prm("lam_im"), ALU.mult))
            step(TT(pr(FR), pr(T1), pr(T2), ALU.add))
            step(TT(pr(T1), pr(AI), prm("lam_re"), ALU.mult))
            step(TT(pr(T2), pr(NR), prm("lam_im"), ALU.mult))
            step(TT(pr(FI), pr(T1), pr(T2), ALU.subtract))
            pool.wait_ge(den_ready, 1)
            step(TT(pr(FR), pr(FR), pr(T3), ALU.mult))
            step(TT(pr(FI), pr(FI), pr(T3), ALU.mult))

            v3 = lambda ap: ap.rearrange("p (g c) -> p g c", g=GP)
            t_a, t_b = v3(bb[:, 0, :]), v3(bb[:, 1, :])

            def cmul(dr, di, ar, ai, br, bi):
                ar, ai = bc(ar, GRP), bc(ai, GRP)
                step(TT(t_a, br, ar, ALU.mult))
                step(TT(t_b, bi, ai, ALU.mult))
                step(TT(dr, t_a, t_b, ALU.subtract))
                step(TT(t_a, bi, ar, ALU.mult))
                step(TT(t_b, br, ai, ALU.mult))
                return TT(di, t_a, t_b, ALU.add)

            step(cmul(pbr[:, :, 7, :], pbi[:, :, 7, :], pr(FR), pr(FI), v3(s5in[:, 0, :]), v3(s5in[:, 1, :])))
            for m in range(1, BT):
                last = cmul(pbr[:, :, 7 - m, :], pbi[:, :, 7 - m, :], pr(AR), pr(AI),
                            pbr[:, :, 8 - m, :], pbi[:, :, 8 - m, :])
                if m < BT - 1:
                    step(last)
            last.then_inc(pb_ready, 1)
            pool.tensor_scalar(bb[:, 2, :], s5in[:, 3, :], -1.0, 0.0, ALU.mult, ALU.add).then_inc(neg_c, 1)
            step(pool.tensor_copy(pr(A8R), pr(AR)))
            step(pool.tensor_copy(pr(A8I), pr(AI)))

            def square():
                step(TT(pr(T1), pr(A8R), pr(A8R), ALU.mult))
                step(TT(pr(T2), pr(A8I), pr(A8I), ALU.mult))
                step(TT(pr(KR), pr(A8R), pr(A8I), ALU.mult))
                step(TT(pr(A8R), pr(T1), pr(T2), ALU.subtract))
                step(TT(pr(A8I), pr(KR), pr(KR), ALU.add))

            for _ in range(3):
                square()
            pool.wait_ge(*full("kb1"))
            step(cmul(gre[:, :, 0, :], gim[:, :, 0, :], pr(AR), pr(AI), v3(s5in[:, 2, :]), v3(s5in[:, 3, :])))
            for r in range(1, BT):
                step(cmul(gre[:, :, r, :], gim[:, :, r, :], pr(AR), pr(AI),
                          gre[:, :, r - 1, :], gim[:, :, r - 1, :]))
            pool.tensor_scalar(s5a[:, 2048:4096], s5a[:, 2048:4096], -1.0, 0.0, ALU.mult, ALU.add)\
                .then_inc(g_ready, 1)
            pool.wait_ge(*emptied("kb1"))
            pool.wait_ge(*full("ub3"))
            pool.memset(big[5][:, :], 0.0).then_inc(m0_zero, 1)
            pool.wait_ge(m0_zero, 1)
            for r in range(BT):
                n = GRP * (r + 1)
                pool.dma_start(m0r[0:n, r, :], k7[P - n:P, :]).then_inc(m0_in, 16)
            pool.wait_ge(m0_in, 16 * BT)
            pool.wait_ge(*full("xs3"))
            pool.tensor_copy(m0T.rearrange("p g (r c) -> p g r c", r=BT),
                             m0r.rearrange("p r (g c) -> p g r c", g=NG)).then_inc(m0_ready, 1)
            pool.wait_ge(m0_ready, 1)
            pool.wait_ge(*emptied("xs3"))
            d = 1
            while d < NB:
                w = NB - d
                ar, ai = bc(pr(A8R), w), bc(pr(A8I), w)
                s1, s2 = sc1[:, :, 0:w], sc2[:, :, 0:w]
                t1, t2 = ysb[:, 0:GP, 0:w], ysb[:, GP:2 * GP, 0:w]
                fr, fi, tr, ti = xr[:, :, 0:w], xi[:, :, 0:w], xr[:, :, d:NB], xi[:, :, d:NB]
                step(TT(s1, fr, ar, ALU.mult))
                step(TT(t1, fi, ai, ALU.mult))
                step(TT(s2, fi, ar, ALU.mult))
                step(TT(t2, fr, ai, ALU.mult))
                step(TT(s1, s1, t1, ALU.subtract))
                step(TT(s2, s2, t2, ALU.add))
                step(TT(tr, tr, s1, ALU.add))
                last = TT(ti, ti, s2, ALU.add)
                d *= 2
                if d < NB:
                    step(last)
                    square()
            last.then_inc(scan_done, 1)

            for h in range(HEADS):
                pool.wait_ge(gn_var, h + 1)
                rsqrt(mv[:, :, 2], mv[:, :, 1], 1.0).then_inc(gn_rstd, 1)

            pool.wait_ge(squares, 2 * NT)
            rsqrt(rs, ss[:, 0:NT], 1.0 / D).then_inc(rstd_ready, 1)

            pool.dma_start(slot_dram.rearrange("(e s) o -> e (s o)", e=E), fill).then_inc(fill_in, 16)
            pool.wait_ge(fill_in, 16)
            pool.wait_ge(dest_ready, 1)
            for c in range(NT * TOPK):
                pool.indirect_dma_start(slot_dram, bass.IndirectOffsetOnAxis(dest[:, c:c + 1], 0),
                                        aid[:, c:c + 1], None).then_inc(slots_put, 16)
            pool.wait_ge(slots_put, 16 * NT * TOPK)
            pool.dma_start(tabi[:, :], slot_dram.rearrange("(e s) o -> e (s o)", e=E)).then_inc(slots_in, 16)

            pool.wait_ge(tab_ready, 1)
            pool.wait_ge(h2_out, 16 * NT)
            pool.memset(big[1][:, :], 0.0).then_inc(xe_zero, 1)
            pool.wait_ge(xe_zero, 1)

            def blocks(expert, move, sems, indexed, settle=False):
                n, n_long = expert
                with pool.If(n <= N_SMALL):
                    pool.wait_ge(*indexed)
                    pool.sem_inc(index_seen, 1)
                    move(0, N_SMALL).then_inc(sems[0], 16)
                with pool.Else():
                    pool.wait_ge(*indexed)
                    pool.sem_inc(index_seen, 1)
                    for b in range(NT):
                        move(b, P).then_inc(sems[b], 16)
                    if settle:
                        for b in range(1, NT):
                            pool.wait_ge(sems[b], n_long * 16 + 16)
                        pool.nop()
                pool.nop()

            token_bound, assign_bound = pool.to_reg(SEQ - 1), pool.to_reg(NA - 1)

            def get_rows(b, rows):
                return pool.indirect_dma_start(
                    xe[0:rows, b, :], None, h2_dram, bass.IndirectOffsetOnAxis(get_e[0:rows, b:b + 1], 0),
                    bounds_check=token_bound, oob_is_err=False)

            def put_rows(b, rows):
                return pool.indirect_dma_start(
                    y_dram, bass.IndirectOffsetOnAxis(put_e[0:rows, b:b + 1], 0), ye[0:rows, b, :], None,
                    bounds_check=assign_bound, oob_is_err=False)

            def gather(x_, expert):
                pool.tensor_copy(get_e[:, :], get_i[:, :, bass.ds(x_, 1)].rearrange("p b o -> p (b o)"))\
                    .then_inc(get_e_ready, 1)
                blocks(expert, get_rows, got, (get_e_ready, x_ + 1))

            def scatter(x_, expert):
                pool.tensor_copy(put_e[:, :], put_i[:, :, bass.ds(x_, 1)].rearrange("p b o -> p (b o)"))\
                    .then_inc(put_e_ready, 1)
                blocks(expert, put_rows, put, (put_e_ready, x_ + 1), settle=True)
                pool.wait_ge(put[0], x_ * 16 + 16)
                pool.sem_inc(ye_free, 1)

            def load(x_):
                return (pool.value_load(cnt[0:1, bass.ds(x_, 1)], min_val=0, max_val=SEQ),
                        pool.value_load(n_long[0:1, bass.ds(x_, 1)], min_val=0, max_val=E))

            gather(0, load(0))
            with pool.Fori(0, E - 1) as e:
                this, after = load(e), load(e + 1)
                pool.wait_ge(t_full, e * 4 + 4)
                gather(e + 1, after)
                pool.wait_ge(y_empty, e * W2C + 2 * W2C)
                scatter(e, this)
            pool.wait_ge(y_empty, (E + 1) * W2C)
            scatter(E - 1, load(E - 1))
            for i in range(NT):
                pool.wait_ge(fsq, i + 1)
                step(pool.tensor_scalar(rs[:, i:i + 1], ss[:, i:i + 1], 1.0 / D, EPS, ALU.mult, ALU.add))
                TT(rs[:, i:i + 1], rs[:, i:i + 1], mhalf[:, 0:1], ALU.pow).then_inc(frstd, 1)

        @block.scalar
        def _(act):
            n_chain = [0]

            def step(ins):
                n_chain[0] += 1
                ins.then_inc(act_chain, 1)
                act.wait_ge(act_chain, n_chain[0])

            xt = x.rearrange("(i p) d -> i p d", i=NT)
            for i in range(NT):
                act.dma_start(xn[:, i, :], xt[i]).then_inc(x_in[i], 16)
            act.dma_start(par_s[:, :], par).then_inc(par_in, 16)
            act.dma_start(ring[:, 4, 512:1536], s5bc).then_inc(par_in, 16)
            act.dma_start(pos_i, pos.partition_broadcast(P)).then_inc(pos_in, 16)
            act.dma_start(b1_s[:, :, :], b1).then_inc(moe_in, 16)
            act.dma_start(rw_s[:, :, :], rw).then_inc(moe_in, 16)

            for i in range(NT):
                act.wait_ge(x_in[i], 16)
                act.activation(hT[:, 2 * i:2 * i + 2, :].rearrange("p a b -> p (a b)"), xn[:, i, :], ACT.Square,
                               accum_out=ss[:, i:i + 1]).then_inc(squares, 1)
            pr = lambda i: s5p[:, i, :]
            act.wait_ge(par_in, 32)
            act.activation(pr(0), prm("log_dt"), ACT.Exp).then_inc(s5_act, 1)
            act.wait_ge(s5_pool, 1)
            act.activation(pr(2), pr(8), ACT.Exp).then_inc(s5_act, 1)
            act.wait_ge(angles, 1)
            act.activation(pr(3), pr(15), ACT.Sin).then_inc(s5_act, 1)
            act.activation(pr(4), pr(14), ACT.Sin).then_inc(s5_act, 1)
            act.wait_ge(angles, 2)
            act.activation(sinT, sinT, ACT.Sin).then_inc(rope_act, 1)
            act.activation(cosT, cosT, ACT.Sin).then_inc(rope_act, 1)

            act.wait_ge(xn_ready, NT)
            act.wait_ge(squares, NT)
            for k in range(KD):
                act.wait_ge(*full(f"xT{k}"))
                act.activation(hT[:, k, :], bk(f"xT{k}")[:, :], ACT.Copy,
                               scale=prm("norm_mix", k)).then_inc(act_emptied, 1)
            for c in range(4):
                act.wait_ge(*full(f"u{c}"))
                act.activation(uT[:, c, :], bk(f"u{c}")[:, :], ACT.Copy).then_inc(act_emptied, 1)
            for r in range(BT):
                act.wait_ge(*full(f"ua{r}"))
                act.activation(ujr[0:NB, :, r, :], bk(f"ua{r}")[0:NB, :].rearrange("p (g c) -> p g c", g=NG),
                               ACT.Copy).then_inc(act_emptied, 1)
            for i in range(8):
                dst = (hTr, hTi)[i // 4]
                act.wait_ge(*full(f"hT{i}"))
                act.activation(dst[:, 4 * (i % 4):4 * (i % 4) + 4, :].rearrange("p g n -> p (g n)"),
                               bk(f"hT{i}")[:, :], ACT.Copy).then_inc(act_emptied, 1)
            for c in range(4):
                for i in range(2):
                    act.wait_ge(*full(f"v{2 * c + i}"))
                    act.activation(vt[:, 2 * i:2 * i + 2, c * CW:(c + 1) * CW],
                                   bk(f"v{2 * c + i}")[:, :].rearrange("p (a n) -> p a n", a=2),
                                   ACT.Copy).then_inc(act_emptied, 1)
            for k in range(KD):
                act.wait_ge(*full(f"g{k}"))
                act.activation(gs[:, k, :], bk(f"g{k}")[:, :], ACT.Silu).then_inc(act_emptied, 1)
            for r in range(BT):
                act.wait_ge(*full(f"yc{r}"))
                act.activation(yjr[0:NB, :, 64 * r:64 * r + 64],
                               bk(f"yc{r}")[0:NB, :].rearrange("p (g r c) -> p r g c", g=4, r=BT),
                               ACT.Copy).then_inc(act_emptied, 1)
            for k in range(KD):
                act.wait_ge(*full(f"ga{k}"))
                act.activation(siga[:, k, :], bk(f"ga{k}")[:, :], ACT.Sigmoid).then_inc(act_emptied, 1)
            for k in range(KD):
                act.wait_ge(*full(f"gb{k}"))
                act.activation(sigb[:, k, :], bk(f"gb{k}")[:, :], ACT.Sigmoid).then_inc(act_emptied, 1)
            act.wait_ge(*emptied("yd3"))
            act.dma_start(b2_s, b2).then_inc(moe_in, 16)
            act.dma_start(gvec, g_ffn.partition_broadcast(P)).then_inc(gf_in, 16)
            act.activation(big[5][:, 0:2048], big[5][:, 0:2048], ACT.Gelu_apprx_tanh).then_inc(z_ready, 1)
            for c in range(4):
                act.wait_ge(*full(f"z{c}"))
                act.activation(zg[:, c, :], bk(f"z{c}")[:, :], ACT.Sigmoid,
                               bias=prm("b_glu", c)).then_inc(act_emptied, 1)
            act.wait_ge(*full("gb7"))
            for i in range(NT):
                act.dma_start(x2[:, i, :], xt[i]).then_inc(x_in2[i], 16)
            for i in range(NT):
                act.wait_ge(*emptied(f"wo{6 + i // 2}"))
                act.activation(h2[:, i, :], x2[:, i, :], ACT.Square,
                               accum_out=ss[:, i:i + 1]).then_inc(squares, 1)
            for k in range(KD):
                act.wait_ge(*full(f"h2T{k}"))
                act.activation(h2T[:, k, :], bk(f"h2T{k}")[:, :], ACT.Copy).then_inc(act_emptied, 1)
            act.wait_ge(top_ready, 1)
            for i in range(NT):
                act.activation(gate[:, i, :], top_v[:, i, 0:TOPK], ACT.Exp, bias=negm[:, i:i + 1],
                               accum_out=gsum[:, i:i + 1]).then_inc(gate_exp, 1)
            act.wait_ge(h2_ready, NT)
            act.dma_start(gvec, g_fin.partition_broadcast(P)).then_inc(gfin_in, 16)
            for i in range(NT):
                act.dma_start(h2_dram[i * P:(i + 1) * P, :], h2[:, i, :]).then_inc(h2_out, 16)

            def rows(t, width):
                for r in range(4):
                    act.wait_ge(t_full, t + r + 1)
                    for k in (2 * r, 2 * r + 1):
                        last = act.activation(xeT[:, k, 0:width], bank[4 + 2 * (r % 2) + k % 2][:, 0:width], ACT.Copy)
                    last.then_inc(t_empty, 1)

            def sigmoids(e, width):
                for j in range(FT):
                    act.wait_ge(glu_ready, e * FT + j + 1)
                    act.activation(sg_t[:, j % 2, 0:width], g_t[:, j % 2, 0:width], ACT.Sigmoid,
                                   scale=SIG_ALPHA).then_inc(sg_ready, 1)

            def results(e, blocks, width):
                for c in range(W2C):
                    act.wait_ge(y_full, e * W2C + c + 1)
                    for b in range(blocks):
                        last = act.activation(
                            ye[0:width, b, c * CW:(c + 1) * CW],
                            bank[4 + 2 * (c % 2) + b // 2][0:width, (b % 2) * CW:(b % 2 + 1) * CW], ACT.Copy)
                    last.then_inc(y_empty, 1)

            act.sem_inc(y_empty, W2C)
            act.wait_ge(tab_ready, 1)
            n = act.value_load(cnt[0:1, 0:1], min_val=0, max_val=SEQ)
            with act.If(n <= N_SMALL):
                rows(0, N_SMALL)
            with act.Else():
                rows(0, SEQ)
            act.nop()
            with act.Fori(0, E - 1) as e:
                n = act.value_load(cnt[0:1, bass.ds(e, 1)], min_val=0, max_val=SEQ)
                n1 = act.value_load(cnt[0:1, bass.ds(e + 1, 1)], min_val=0, max_val=SEQ)
                with act.If(n <= N_SMALL):
                    sigmoids(e, N_SMALL)
                with act.Else():
                    sigmoids(e, SEQ)
                with act.If(n1 <= N_SMALL):
                    rows(e * 4 + 4, N_SMALL)
                with act.Else():
                    rows(e * 4 + 4, SEQ)
                with act.If(n <= N_SMALL):
                    results(e, 1, N_SMALL)
                with act.Else():
                    results(e, NT, P)
                act.nop()
            n = act.value_load(cnt[0:1, E - 1:E], min_val=0, max_val=SEQ)
            with act.If(n <= N_SMALL):
                sigmoids(E - 1, N_SMALL)
                act.wait_ge(ye_free, E - 1)
                results(E - 1, 1, N_SMALL)
            with act.Else():
                sigmoids(E - 1, SEQ)
                act.wait_ge(ye_free, E - 1)
                results(E - 1, NT, P)
            for i in range(NT):
                act.wait_ge(summed, i + 1)
                act.activation(big[3][:, i * D:(i + 1) * D], x2[:, i, :], ACT.Square,
                               accum_out=ss[:, i:i + 1]).then_inc(fsq, 1)

        @block.vector
        def _(dve):
            n_chain = [0]

            def step(ins):
                n_chain[0] += 1
                ins.then_inc(dve_chain, 1)
                dve.wait_ge(dve_chain, n_chain[0])

            TT, TS, STT = dve.tensor_tensor, dve.tensor_scalar, dve.scalar_tensor_tensor
            rs = ss[:, NT:2 * NT]
            dve.wait_ge(rstd_ready, 1)
            for i in range(NT):
                TS(xn[:, i, :], xn[:, i, :], rs[:, i:i + 1], None, ALU.mult).then_inc(xn_ready, 1)

            def reduce_angle(r, c, tk):
                step(TS(tk, r, 1.0 / TWO_PI, ROUND, ALU.mult, ALU.add))
                step(TS(tk, tk, ROUND, None, ALU.subtract))
                for part in (PI_1, PI_2, PI_3):
                    step(STT(r, tk, -part, r, ALU.mult, ALU.add))
                step(TS(r, r, PI_IN, -PI_IN, ALU.min, ALU.max))
                step(TS(tk, r, -1.0, None, ALU.mult))
                step(TT(tk, tk, r, ALU.max))
                return TS(c, tk, -1.0, float(np.float32(np.pi / 2)), ALU.mult, ALU.add)

            pr = lambda i: s5p[:, i, :]
            dve.wait_ge(s5_pool, 1)
            step(dve.tensor_copy(pr(15), pr(1)))
            reduce_angle(pr(15), pr(14), pr(18)).then_inc(angles, 1)
            dve.wait_ge(s5_pool, 2)
            dve.reciprocal(pr(13), pr(10)).then_inc(den_ready, 1)
            dve.wait_ge(pos_in, 16)
            dve.wait_ge(cst_in, 16)
            step(dve.tensor_copy(rope_k, pos_i))
            step(TS(sinT, rope_k, con("inv_freq"), None, ALU.mult))
            reduce_angle(sinT, cosT, rope_k).then_inc(angles, 1)
            for i in range(4):
                dve.wait_ge(*full(f"ub{i}"))
                dve.tensor_copy(ub[:, 8 * i:8 * i + 8, :].rearrange("p g j -> p (g j)"),
                                bk(f"ub{i}")[:, :]).then_inc(dve_emptied, 1)
            dve.wait_ge(rope_act, 2)
            step(TS(sinT, sinT, con("sin_sign"), None, ALU.mult))
            H = DK // 2
            for name, dst, scale in (("q", qT, 1.0), ("k", kT, DK ** -0.5)):
                for h in range(HEADS):
                    dve.wait_ge(*full(f"{name}{h}"))
                    b = bk(f"{name}{h}")
                    if (name, h) != ("q", 0):
                        dve.wait_ge(*emptied(f"{name}{h - 1}" if h else "q3"))
                    STT(rot_a, b[:, :], scale, cosT, ALU.mult, ALU.mult)
                    STT(rot_b[0:H, :], b[H:P, :], scale, sinT[0:H, :], ALU.mult, ALU.mult)
                    step(STT(rot_b[H:P, :], b[0:H, :], scale, sinT[H:P, :], ALU.mult, ALU.mult))
                    TT(dst[:, h, :], rot_a, rot_b, ALU.add).then_inc(dve_emptied, 1)
            for odd in range(2):
                dve.wait_ge(*full(f"kb{odd}"))
                dve.tensor_copy(k7.rearrange("p (g o c) -> p g o c", o=2, c=GRP)[:, :, odd, :],
                                bk(f"kb{odd}")[:, 0:GP * GRP].rearrange("p (g c) -> p g c", g=GP))\
                    .then_inc(dve_emptied, 1)
            for i in range(4):
                dst = (xr, xi)[i // 2]
                dve.wait_ge(*full(f"xs{i}"))
                dve.tensor_copy(dst[:, 8 * (i % 2):8 * (i % 2) + 8, :].rearrange("p g j -> p (g j)"),
                                bk(f"xs{i}")[:, :]).then_inc(dve_emptied, 1)
            dve.wait_ge(dec_in, 16)
            for h in range(HEADS):
                for j in range(NT):
                    w = SEQ - j * P
                    dve.wait_ge(*full(f"sc{4 * h + j}"))
                    TT(sT[:, j, 0:w], bk(f"sc{4 * h + j}")[:, 0:w], decay[:, h, 0:w],
                       ALU.mult).then_inc(dve_emptied, 1)
                for m in range(2):
                    b = bk(f"in{2 * h + m}")
                    dve.wait_ge(*full(f"in{2 * h + m}"))
                    for a in range(2):
                        last = dve.bn_stats(stat[:, 2 * m + a, 0:6], b[:, a * DV:(a + 1) * DV])
                step(last)
                if h:
                    dve.wait_ge(*emptied(f"in{2 * h - 1}"))
                for i in range(NT):
                    last = dve.bn_aggr(mv[:, i, 0:2], stat[:, i, 0:6])
                last.then_inc(gn_var, 1)
                dve.wait_ge(gn_rstd, h + 1)
                for i in range(NT):
                    b = bk(f"in{2 * h + i // 2}")
                    last = TS(ret[:, i, h * DV:(h + 1) * DV], b[:, (i % 2) * DV:(i % 2 + 1) * DV],
                              mv[:, i, 0:1], mv[:, i, 2:3], ALU.subtract, ALU.mult)
                    if i % 2:
                        last.then_inc(dve_emptied, 1)
            for k in range(KD):
                dve.wait_ge(*full(f"rT{k}"))
                dve.wait_ge(*emptied(f"g{k}"))
                STT(gs[:, k, :], bk(f"rT{k}")[:, :], prm("ret_gn", k), gs[:, k, :],
                    ALU.mult, ALU.mult).then_inc(dve_emptied, 1)
            for i in range(4):
                dve.wait_ge(*full(f"ys{i}"))
                dve.tensor_copy(ysb.rearrange("p (g o) j -> p g o j", o=2)[:, 8 * (i // 2):8 * (i // 2) + 8, i % 2, :],
                                bk(f"ys{i}")[:, :].rearrange("p (g j) -> p g j", g=8)).then_inc(dve_emptied, 1)
            for c in range(4):
                dve.wait_ge(*full(f"yd{c}"))
                by_r = lambda ap: ap.rearrange("p (j r) -> p r j", r=BT)
                STT(by_r(zT[:, c, :]), by_r(uT[:, c, :]), prm("d_skip", c),
                    bk(f"yd{c}")[:, :].rearrange("p (r j) -> p r j", r=BT),
                    ALU.mult, ALU.add).then_inc(dve_emptied, 1)
            for c in range(4):
                dve.wait_ge(*emptied(f"z{c}"))
                TT(zg[:, c, :], zg[:, c, :], zT[:, c, :], ALU.mult).then_inc(zg_ready, 1)
            for k in range(KD):
                dve.wait_ge(*full(f"ya{k}"))
                TT(mg[:, k, :], bk(f"ya{k}")[:, :], siga[:, k, :], ALU.mult).then_inc(dve_emptied, 1)
            for k in range(KD):
                dve.wait_ge(*full(f"yb{k}"))
                step(TT(sigb[:, k, :], bk(f"yb{k}")[:, :], sigb[:, k, :], ALU.mult))
                TT(mg[:, k, :], mg[:, k, :], sigb[:, k, :], ALU.add).then_inc(dve_emptied, 1)
            for i in range(NT):
                dve.wait_ge(x_in2[i], 16)
            for n in range(8):
                c, m = n // 2, n % 2
                dve.wait_ge(*full(f"wo{n}"))
                dst = x2[:, 2 * m:2 * m + 2, c * CW:(c + 1) * CW]
                TT(dst, bk(f"wo{n}")[:, :].rearrange("p (a n) -> p a n", a=2), dst,
                   ALU.add).then_inc(dve_emptied, 1)
            dve.wait_ge(rstd_ready, 2)
            dve.wait_ge(gf_in, 16)
            for i in range(NT):
                STT(h2[:, i, :], x2[:, i, :], rs[:, i:i + 1], gvec[:, :], ALU.mult, ALU.mult)\
                    .then_inc(h2_ready, 1)

            dve.wait_ge(*full("lg0"))
            TT(lg[:, :, :], bk("lg0")[:, 0:NT * E].rearrange("p (i e) -> p i e", i=NT),
               prm("router_b").unsqueeze(1).to_broadcast([P, NT, E]), ALU.add).then_inc(dve_emptied, 1)
            dve.wait_ge(*emptied("lg0"))
            for i in range(NT):
                step(dve.max(top_v[:, i, :], lg[:, i, :]))
            for i in range(NT):
                last = dve.max_index(top_i[:, i, :], top_v[:, i, :], lg[:, i, :])
            step(last)
            TS(negm[:, :], top_v[:, :, 0], -1.0, None, ALU.mult).then_inc(top_ready, 1)
            step(dve.tensor_copy(top_f[:, :, :], top_i[:, :, :]))
            topb = top_f[:, :, 0:TOPK].unsqueeze(3).to_broadcast([P, NT, TOPK, E])
            eid = con("expert_id").unsqueeze(1).unsqueeze(1).to_broadcast([P, NT, TOPK, E])
            step(TT(oneh[:, :, :, :], topb, eid, ALU.is_equal))
            over_k = lambda ap: ap.rearrange("p i k e -> p i e k")
            dve.tensor_reduce(hot[:, :, :], over_k(oneh[:, :, :, :]), AX.X, ALU.add).then_inc(hot_ready, 1)
            dve.tensor_copy(aid[:, :], con("assign_id"))
            dve.wait_ge(*full("rk0"))
            dve.tensor_copy(cnt[:, :], bk("rk0")[0:1, NT * E:(NT + 1) * E])
            dve.tensor_copy(cum[:, :, :], bk("rk0")[:, 0:NT * E].rearrange("p (i e) -> p i e", i=NT))\
                .then_inc(dve_emptied, 1)
            dve.wait_ge(*emptied("rk0"))
            step(TT(wrk[:, :, :, :], oneh[:, :, :, :],
                    cum[:, :, :].unsqueeze(2).to_broadcast([P, NT, TOPK, E]), ALU.mult))
            step(dve.tensor_reduce(rank[:, :], wrk[:, :, :, :].rearrange("p i k e -> p (i k) e"), AX.X, ALU.add))
            STT(dest[:, :].rearrange("p (i k) -> p i k", i=NT), top_f[:, :, 0:TOPK], float(SEQ),
                rank[:, :].rearrange("p (i k) -> p i k", i=NT), ALU.mult, ALU.add).then_inc(dest_ready, 1)
            step(TS(is_long, cnt[:, :], float(N_SMALL), None, ALU.is_gt))
            eid0 = con("expert_id")[0:1, :]
            step(TT(pairs, eid0.unsqueeze(1).to_broadcast([1, E, E]), eid0.unsqueeze(2).to_broadcast([1, E, E]),
                    ALU.is_lt))
            step(TT(pairs, pairs, is_long.unsqueeze(1).to_broadcast([1, E, E]), ALU.mult))
            step(dve.tensor_reduce(is_long, pairs, AX.X, ALU.add))
            dve.tensor_copy(n_long[:, :], is_long)
            dve.wait_ge(gate_exp, NT)
            step(dve.reciprocal(gsum[:, NT:2 * NT], gsum[:, 0:NT]))
            step(TT(gate[:, :, :], gate[:, :, :], bc(gsum[:, NT:2 * NT], TOPK), ALU.mult))
            step(TT(wrk[:, :, :, :], oneh[:, :, :, :],
                    gate[:, :, :].unsqueeze(3).to_broadcast([P, NT, TOPK, E]), ALU.mult))
            dve.tensor_reduce(gte[:, :, :], over_k(wrk[:, :, :, :]), AX.X, ALU.add).then_inc(gte_ready, 1)
            dve.wait_ge(*full("gT0"))
            dve.tensor_copy(gTs[:, :], bk("gT0")[0:E, :]).then_inc(dve_emptied, 1)
            dve.wait_ge(moe_in, 48)
            ones_of = b1_s[:, :, :].rearrange("p e (j s) -> p (e j) s", s=2)[:, :, 1]
            TS(ones_of, ones_of, 1.0, None, ALU.add).then_inc(b1_ready, 1)
            for n in range(8):
                i, m = n // 2, n % 2
                dve.wait_ge(*full(f"b2{n}"))
                dst = x2[:, i, m * 512:(m + 1) * 512]
                TT(dst, bk(f"b2{n}")[:, :], dst, ALU.add).then_inc(dve_emptied, 1)
            dve.wait_ge(slots_in, 16)
            dve.tensor_copy(tabf[:, :], tabi[:, :]).then_inc(tabf_ready, 1)
            dve.wait_ge(*full("tb0"))
            step(dve.tensor_copy(put_i[:, :, :].rearrange("p b e -> p (b e)"), bk("tb0")[:, 0:NT * E]))
            TS(get_i[:, :, :], put_i[:, :, :], 2, None, ALU.arith_shift_right).then_inc(dve_emptied, 1)
            dve.wait_ge(*emptied("tb0"))
            dve.sem_inc(tab_ready, 1)
            dve.sem_inc(gu_empty, 2)
            dve.wait_ge(b1_ready, 1)

            def ffn(e, width):
                for j in range(FT + 1):
                    if j < FT:
                        b = j % 2
                        dve.wait_ge(gu_full, e * FT + j + 1)
                        if j >= 2:
                            dve.wait_ge(act_ready, e * FT + (j - 1))
                        TS(g_t[:, b, 0:width], bank[2 * b][:, 0:width], b1e[:, 2 * j:2 * j + 1], LIMIT,
                           ALU.add, ALU.min).then_inc(glu_ready, 1)
                        TS(l_t[:, b, 0:width], bank[2 * b + 1][:, 0:width], b1e[:, 2 * j + 1:2 * j + 2],
                           LIMIT + 1.0, ALU.add, ALU.min).then_inc(gu_empty, 1)
                    if j > 0:
                        b = (j - 1) % 2
                        dve.wait_ge(sg_ready, e * FT + j)
                        TT(gs_t[:, b, 0:width], g_t[:, b, 0:width], sg_t[:, b, 0:width],
                           ALU.mult).then_inc(gs_ready, 1)
                        dve.wait_ge(gs_ready, e * FT + j)
                        STT(aT[:, j - 1, 0:width], l_t[:, b, 0:width], 1.0 - LIMIT, gs_t[:, b, 0:width],
                            ALU.max, ALU.mult).then_inc(act_ready, 1)

            def bias(x_):
                dve.tensor_copy(b1e[:, :], b1_s[:, bass.ds(x_, 1), :].rearrange("p o f -> p (o f)"))\
                    .then_inc(b1e_ready, 1)

            bias(0)
            with dve.Fori(0, E - 1) as e:
                n = dve.value_load(cnt[0:1, bass.ds(e, 1)], min_val=0, max_val=SEQ)
                with dve.If(n <= N_SMALL):
                    dve.wait_ge(b1e_ready, e + 1)
                    ffn(e, N_SMALL)
                with dve.Else():
                    dve.wait_ge(b1e_ready, e + 1)
                    ffn(e, SEQ)
                dve.wait_ge(act_ready, e * FT + FT)
                bias(e + 1)
            n = dve.value_load(cnt[0:1, E - 1:E], min_val=0, max_val=SEQ)
            with dve.If(n <= N_SMALL):
                dve.wait_ge(b1e_ready, E)
                ffn(E - 1, N_SMALL)
            with dve.Else():
                dve.wait_ge(b1e_ready, E)
                ffn(E - 1, SEQ)
            dve.nop()

            for i in range(NT):
                dve.wait_ge(yk_in[i % 2], 16 * (i // 2 + 1))
                for k in range(TOPK):
                    last = STT(x2[:, i, :], yk[i % 2][:, k, :], gate[:, i, k:k + 1], x2[:, i, :],
                               ALU.mult, ALU.add)
                    if k < TOPK - 1:
                        step(last)
                last.then_inc(summed, 1)
            dve.wait_ge(gfin_in, 16)
            for i in range(NT):
                dve.wait_ge(frstd, i + 1)
                STT(x2[:, i, :], x2[:, i, :], rs[:, i:i + 1], gvec[:, :], ALU.mult, ALU.mult)\
                    .then_inc(fin_ready, 1)

        @block.tensor
        def _(pe):
            MM, TR = pe.matmul, pe.transpose

            def start(name):
                n = JOB[name]
                if n >= 8:
                    e, v = EMPTIED[n - 8]
                    pe.wait_ge(EMPT[e], v)
                return bank[n % 8]

            def chunk(n, k=KD):
                pe.wait_ge(landed[n % RING_T], 16 * (n // RING_T + 1))
                return ring[:, n % RING_T, :].rearrange("p (k n) -> p k n", k=k)

            def channel_major(name, c0, rhs, k_tiles, first):
                per = CH // k_tiles // P
                n = sum(1 for j, _ in JOBS if j.startswith(name) and j[len(name):].isdigit())
                for m in range(n):
                    if m % per == 0:
                        w = chunk(c0 + m // per, k_tiles)
                    b = start(f"{name}{m}")
                    for k in range(k_tiles):
                        if m == 0 and first:
                            pe.wait_ge(*first(k))
                        last = MM(b[:, :], w[:, k, (m % per) * P:(m % per + 1) * P], rhs[:, k, :],
                                  start=(k == 0), stop=(k == k_tiles - 1))
                    last.then_inc(bank_full, 1)

            pe.wait_ge(cst_in, 16)
            pe.wait_ge(xn_ready, NT)
            for k in range(KD):
                b = start(f"xT{k}")
                for i in range(NT):
                    last = TR(b[:, i * P:(i + 1) * P], xn[:, i, k * P:(k + 1) * P], ident)
                last.then_inc(bank_full, 1)
            channel_major("u", C_U, hT, KD, lambda k: emptied(f"xT{k}"))
            pe.wait_ge(*emptied("u3"))
            for r in range(BT):
                b = start(f"ua{r}")
                for c in range(4):
                    last = TR(b[0:NB, c * P:(c + 1) * P], uT[:, c, r:SEQ:BT], ident)
                last.then_inc(bank_full, 1)
            pe.wait_ge(*emptied("ua7"))
            for i in range(4):
                b = start(f"ub{i}")
                for g in range(8):
                    last = TR(b[:, g * NB:(g + 1) * NB],
                              ujr[0:NB, 8 * i + g, :, :].rearrange("p r c -> p (r c)"), ident[0:NB, 0:NB])
                last.then_inc(bank_full, 1)
            channel_major("q", C_Q, hT, KD, None)
            channel_major("k", C_K, hT, KD, None)
            pe.wait_ge(pb_ready, 1)
            for i in range(8):
                b = start(f"hT{i}")
                src = (pbr, pbi)[i // 4]
                for g in range(4):
                    last = TR(b[:, g * P:(g + 1) * P],
                              src[:, 4 * (i % 4) + g, :, :].rearrange("p m c -> p (m c)"), ident)
                last.then_inc(bank_full, 1)
            pe.wait_ge(neg_c, 1)
            for odd in range(2):
                b = start(f"kb{odd}")
                p0 = NS * odd
                for gp in range(GP):
                    for s, (w, c) in enumerate(((pbr, s5in[:, 2, :]), (pbi, bb[:, 2, :]))):
                        last = MM(b[:, gp * GRP:(gp + 1) * GRP],
                                  w[p0:p0 + NS, gp, :, :].rearrange("p m c -> p (m c)"),
                                  c[p0:p0 + NS, gp * GRP:(gp + 1) * GRP], start=(s == 0), stop=(s == 1))
                last.then_inc(bank_full, 1)
            pe.wait_ge(*emptied("hT7"))
            pe.wait_ge(*emptied("ub3"))
            for i in range(4):
                b = start(f"xs{i}")
                w = (hTr, hTi)[i // 2]
                for g in range(16):
                    gg = 16 * (i % 2) + g
                    p0 = NS * (gg % 2)
                    last = MM(b[p0:p0 + NS, (g // 2) * NB:(g // 2 + 1) * NB], w[:, gg // 2, p0:p0 + NS],
                              ub[:, gg, :], start=True, stop=True)
                last.then_inc(bank_full, 1)
            for c in range(4):
                w = chunk(C_V + c)
                for m in range(2):
                    b = start(f"v{2 * c + m}")
                    for a in range(2):
                        i = 2 * m + a
                        for k in range(KD):
                            last = MM(b[:, a * CW:(a + 1) * CW], hT[:, k, i * P:(i + 1) * P], w[:, k, :],
                                      start=(k == 0), stop=(k == KD - 1))
                    last.then_inc(bank_full, 1)
            pe.wait_ge(*emptied("k3"))
            pe.wait_ge(*emptied("v7"))
            for h in range(HEADS):
                for j in range(NT):
                    b = start(f"sc{4 * h + j}")
                    MM(b[:, 0:SEQ - j * P], kT[:, h, j * P:(j + 1) * P], qT[:, h, j * P:SEQ],
                       start=True, stop=True).then_inc(bank_full, 1)
                for m in range(2):
                    b = start(f"in{2 * h + m}")
                    for a in range(2):
                        i = 2 * m + a
                        for j in range(i + 1):
                            pe.wait_ge(*emptied(f"sc{4 * h + j}"))
                            last = MM(b[:, a * DV:(a + 1) * DV], sT[:, j, (i - j) * P:(i - j + 1) * P],
                                      vt[:, j, h * DV:(h + 1) * DV], start=(j == 0), stop=(j == i))
                    last.then_inc(bank_full, 1)
            channel_major("g", C_G, hT, KD, None)
            pe.wait_ge(*emptied("in7"))
            for k in range(KD):
                b = start(f"rT{k}")
                for i in range(NT):
                    last = TR(b[:, i * P:(i + 1) * P], ret[:, i, k * P:(k + 1) * P], ident)
                last.then_inc(bank_full, 1)
            pe.wait_ge(m0_ready, 1)
            pe.wait_ge(g_ready, 1)
            pe.wait_ge(scan_done, 1)
            for i in range(4):
                b = start(f"ys{i}")
                for g in range(8):
                    gg = 2 * (8 * (i // 2) + g) + i % 2
                    p0, gp, col = NS * (gg % 2), gg // 2, g * NB
                    MM(b[:, col:col + NB], m0T[:, gg, :], ub[:, gg, :],
                       start=True, stop=False)
                    MM(b[:, col + 1:col + NB], gre[p0:p0 + NS, gp, :, :].rearrange("p m c -> p (m c)"),
                       xr[p0:p0 + NS, gp, 0:NB - 1], start=False, stop=False)
                    last = MM(b[:, col + 1:col + NB], gim[p0:p0 + NS, gp, :, :].rearrange("p m c -> p (m c)"),
                              xi[p0:p0 + NS, gp, 0:NB - 1], start=False, stop=True)
                last.then_inc(bank_full, 1)
            for i in range(8):
                if i % 4 == 0:
                    pe.wait_ge(*emptied(f"ys{i // 2 + 1}"))
                b = start(f"yc{i}")
                for g in range(4):
                    last = TR(b[0:NB, g * P:(g + 1) * P], ysb[:, 4 * i + g, :], ident)
                last.then_inc(bank_full, 1)
            for c in range(4):
                pe.wait_ge(*emptied(f"yc{2 * c + 1}"))
                b = start(f"yd{c}")
                for r in range(BT):
                    last = TR(b[:, r * NB:(r + 1) * NB], yjr[0:NB, r, c * P:(c + 1) * P], ident[0:NB, 0:NB])
                last.then_inc(bank_full, 1)
            channel_major("ga", C_GA, hT, KD, None)
            channel_major("gb", C_GB, hT, KD, None)
            pe.wait_ge(z_ready, 1)
            channel_major("z", C_GLU, zT, 4, None)
            channel_major("ya", C_BS5, zg, 4, lambda k: (zg_ready, k + 1))
            channel_major("yb", C_BRET, gs, KD, None)
            for c in range(4):
                w = chunk(C_OUT + c)
                for m in range(2):
                    b = start(f"wo{2 * c + m}")
                    for a in range(2):
                        i = 2 * m + a
                        for k in range(KD):
                            if c == 0 and i == 0:
                                pe.wait_ge(*emptied(f"yb{k}"))
                            last = MM(b[:, a * CW:(a + 1) * CW], mg[:, k, i * P:(i + 1) * P], w[:, k, :],
                                      start=(k == 0), stop=(k == KD - 1))
                    last.then_inc(bank_full, 1)
            pe.wait_ge(h2_ready, NT)
            for k in range(KD):
                b = start(f"h2T{k}")
                for i in range(NT):
                    last = TR(b[:, i * P:(i + 1) * P], h2[:, i, k * P:(k + 1) * P], ident)
                last.then_inc(bank_full, 1)
            pe.wait_ge(moe_in, 48)
            pe.wait_ge(*emptied("h2T7"))
            b = start("lg0")
            for i in range(NT):
                for k in range(KD):
                    last = MM(b[:, i * E:(i + 1) * E], h2T[:, k, i * P:(i + 1) * P], rw_s[:, k, :],
                              start=(k == 0), stop=(k == KD - 1))
            last.then_inc(bank_full, 1)
            pe.wait_ge(hot_ready, 1)
            b = start("rk0")
            for i in range(NT + 1):
                for j in range(min(i, NT)):
                    last = MM(b[:, i * E:(i + 1) * E], ones, hot[:, j, :], start=(j == 0),
                              stop=(j == NT - 1))
                if i < NT:
                    last = MM(b[:, i * E:(i + 1) * E], con("before"), hot[:, i, :], start=(i == 0), stop=True)
            last.then_inc(bank_full, 1)
            pe.wait_ge(gte_ready, 1)
            b = start("gT0")
            for i in range(NT):
                last = TR(b[0:E, i * P:(i + 1) * P], gte[:, i, :], ident)
            last.then_inc(bank_full, 1)
            pe.wait_ge(*emptied("gT0"))
            for n in range(8):
                b = start(f"b2{n}")
                MM(b[:, :], gTs[:, (n // 2) * P:(n // 2 + 1) * P], b2_s[:, (n % 2) * 512:(n % 2 + 1) * 512],
                   start=True, stop=True).then_inc(bank_full, 1)
            pe.wait_ge(tabf_ready, 1)
            b = start("tb0")
            for i in range(NT):
                last = TR(b[:, i * E:(i + 1) * E], tabf[:, i * P:(i + 1) * P], ident[0:E, 0:E])
            last.then_inc(bank_full, 1)

            pe.wait_ge(tab_ready, 1)

            def rows(x_, blocks, width, n_before=None, first=False):
                pe.wait_ge(got[0], x_ * 16 + 16)
                for b in range(1, blocks):
                    pe.wait_ge(got[b], n_before * 16 + 16)
                for r in range(4):
                    if r >= 2:
                        pe.wait_ge(t_empty, x_ * 4 + (r - 1))
                    elif not first:
                        pe.wait_ge(y_empty, x_ * 4 + (r - 1))
                        pe.wait_ge(t_empty, x_ * 4 + (r - 1))
                    for k in (2 * r, 2 * r + 1):
                        for b in range(blocks):
                            last = TR(bank[4 + 2 * (r % 2) + k % 2][:, b * P:b * P + width],
                                      xe[0:width, b, k * P:(k + 1) * P], ident[0:width, 0:width])
                    last.then_inc(t_full, 1)

            def expert_chunk(e, c):
                slot = (RING_T + c) % RING
                before = sum(1 for n in range(N_TRUNK) if n % RING_T == slot) if slot < RING_T else 0
                pe.wait_ge(landed[slot], e * 16 + 16 * (before + 1))
                return ring[:, slot, :]

            def up(e, width):
                pe.wait_ge(t_empty, e * 4 + 4)
                for j in range(FT):
                    w = expert_chunk(e, j).rearrange("p (k s n) -> p k s n", k=KD, s=2)
                    pe.wait_ge(gu_empty, e * FT + (j + 1))
                    for s in range(2):
                        for k in range(KD):
                            last = MM(bank[2 * (j % 2) + s][:, 0:width], w[:, k, s, :], xeT[:, k, 0:width],
                                      start=(k == 0), stop=(k == KD - 1))
                    last.then_inc(gu_full, 1)

            def down(e, blocks, width, final=False):
                pe.wait_ge(act_ready, e * FT + FT)
                for c in range(W2C):
                    w = expert_chunk(e, FT + c).rearrange("p (k n) -> p k n", k=FT)
                    if c >= 2:
                        pe.wait_ge(y_empty, e * 4 + (c + 3))
                    elif final:
                        pe.wait_ge(y_empty, e * 4 + (c + 3))
                    else:
                        pe.wait_ge(t_empty, e * 4 + (c + 7))
                    for b in range(blocks):
                        for k in range(FT):
                            last = MM(bank[4 + 2 * (c % 2) + b // 2][0:width, (b % 2) * CW:(b % 2 + 1) * CW],
                                      aT[:, k, b * P:b * P + width], w[:, k, :],
                                      start=(k == 0), stop=(k == FT - 1))
                    last.then_inc(y_full, 1)

            n = pe.value_load(cnt[0:1, 0:1], min_val=0, max_val=SEQ)
            with pe.If(n <= N_SMALL):
                rows(0, 1, N_SMALL, first=True)
            with pe.Else():
                rows(0, NT, P, 0, first=True)
            pe.nop()
            with pe.Fori(0, E - 1) as e:
                n = pe.value_load(cnt[0:1, bass.ds(e, 1)], min_val=0, max_val=SEQ)
                n1 = pe.value_load(cnt[0:1, bass.ds(e + 1, 1)], min_val=0, max_val=SEQ)
                long1 = pe.value_load(n_long[0:1, bass.ds(e + 1, 1)], min_val=0, max_val=E)
                with pe.If(n <= N_SMALL):
                    up(e, N_SMALL)
                with pe.Else():
                    up(e, SEQ)
                with pe.If(n1 <= N_SMALL):
                    rows(e + 1, 1, N_SMALL)
                with pe.Else():
                    rows(e + 1, NT, P, long1)
                with pe.If(n <= N_SMALL):
                    down(e, 1, N_SMALL)
                with pe.Else():
                    down(e, NT, P)
                pe.nop()
            n = pe.value_load(cnt[0:1, E - 1:E], min_val=0, max_val=SEQ)
            with pe.If(n <= N_SMALL):
                up(E - 1, N_SMALL)
                down(E - 1, 1, N_SMALL, final=True)
            with pe.Else():
                up(E - 1, SEQ)
                down(E - 1, NT, P, final=True)
            pe.nop()


_INPUTS = ("x", "pos", "wt", "we", "par", "s5bc", "b1", "b2", "rw", "g_ffn", "g_fin", "cst", "dmask", "fill")


def _constants():
    i = np.arange(P)
    c = {
        "ident": np.eye(P), "before": (i[:, None] < i[None, :]), "ones": np.ones((P, P)),
        "expert_id": np.broadcast_to(np.arange(E), (P, E)),
        "assign_id": np.concatenate([TOPK * (t * P + i)[:, None] + np.arange(TOPK) for t in range(NT)], 1),
        "inv_freq": (np.float32(10000.0) ** (-(i % (DK // 2)).astype(np.float32) / np.float32(DK // 2)))[:, None],
        "sin_sign": np.where(i < DK // 2, -1.0, 1.0)[:, None],
    }
    cst = np.concatenate([np.asarray(c[n], np.float32) for n in CST], 1)
    lag = np.arange(SEQ)[None, :] - i[:, None]
    dm = [np.where(lag >= 0, (1.0 - 2.0 ** (-5.0 - h)) ** np.maximum(lag, 0), 0.0) for h in range(HEADS)]
    fill = np.full((E, SEQ), NO_SLOT, np.int32)
    return np.ascontiguousarray(cst), np.stack(dm, 1).astype(np.float32), fill


def kernel(x, positions, norm_mix_g, w_in, s5_lambda_re, s5_lambda_im, s5_log_dt, s5_b_re, s5_b_im,
           s5_c_re, s5_c_im, s5_d, s5_w_glu, s5_b_glu, ret_gn_g, w_branch_s5, w_branch_ret, w_out,
           norm_ffn_g, router_w, router_b, expert_w1, expert_b1, expert_w2, expert_b2, norm_final_g):
    import concourse.bacc as bacc
    from concourse.bass_utils import run_bass_kernel_spmd

    f = np.asarray

    def chunks(w):
        w = f(w)
        k = w.shape[0] // P
        return w.reshape(k, P, -1, CH // k).transpose(2, 1, 0, 3).reshape(-1, P, CH)

    def cols(v):
        return f(v).reshape(-1, P).T

    def states(v):
        v = f(v).reshape(GP, 2 * NS, -1)
        return v.transpose(1, 0, 2).reshape(P, -1)

    cst, dmask, fill = _constants()
    w1 = f(expert_w1)[0].reshape(E, KD, P, FT, P, 2).transpose(0, 3, 2, 1, 5, 4).reshape(E, FT, P, CH)
    w2 = f(expert_w2)[0].reshape(E, FT, P, W2C, CW).transpose(0, 3, 2, 1, 4).reshape(E, W2C, P, CH)
    par = {
        "norm_mix": cols(norm_mix_g[0]), "ret_gn": cols(ret_gn_g[0]), "d_skip": cols(s5_d[0]),
        "b_glu": cols(s5_b_glu[0]), "lam_re": states(s5_lambda_re[0]), "lam_im": states(s5_lambda_im[0]),
        "log_dt": states(np.broadcast_to(f(s5_log_dt)[0][:, None], (NG, NS))),
        "router_b": np.broadcast_to(f(router_b)[0][None, :], (P, E)),
    }
    arrays = {
        "x": f(x)[0], "pos": f(positions), "we": np.concatenate([w1, w2], 1),
        "wt": np.concatenate([chunks(w[0]) for w in (w_in, s5_w_glu, w_branch_s5, w_branch_ret, w_out)]),
        "s5bc": np.concatenate([states(f(v)) for v in (s5_b_re[0], s5_b_im[0], f(s5_c_re)[0].transpose(0, 2, 1),
                                                        f(s5_c_im)[0].transpose(0, 2, 1))], 1),
        "par": np.concatenate([par[n] for n in PAR], 1),
        "b1": f(expert_b1)[0].reshape(E, FT, P, 2).transpose(2, 0, 1, 3).reshape(P, E, 2 * FT),
        "b2": f(expert_b2)[0], "rw": f(router_w)[0].reshape(KD, P, E).transpose(1, 0, 2),
        "g_ffn": f(norm_ffn_g), "g_fin": f(norm_final_g)[None, :], "cst": cst, "dmask": dmask, "fill": fill,
    }
    nc = bacc.Bacc("TRN2", target_bir_lowering=False, num_devices=1)
    ins, aps = {}, []
    for n in _INPUTS:
        a = np.ascontiguousarray(arrays[n])
        ins[n] = a
        aps.append(nc.dram_tensor(n, a.shape, mybir.dt.from_np(a.dtype), kind="ExternalInput").ap())
    out = nc.dram_tensor("out", (SEQ, D), F32, kind="ExternalOutput").ap()
    build(nc, *aps, out)
    r = run_bass_kernel_spmd(nc, [ins], core_ids=[0])
    return f(r.results[0]["out"]).reshape(1, SEQ, D)
```

```python
from contextlib import ExitStack

import numpy as np

import concourse.bass as bass
from concourse import mybir

F32 = mybir.dt.float32
F32R = mybir.dt.float32r
I32 = mybir.dt.int32
U32 = mybir.dt.uint32
ALU = mybir.AluOpType
ACT = mybir.ActivationFunctionType
AX = mybir.AxisListType

P = 128
D = 1024
SEQ = 512
NT = SEQ // P
KD = D // P
S5W = 512
GRP = 16
NG = S5W // GRP
NS = 64
GP = NG // 2
BT = P // GRP
NB = SEQ // BT
HEADS, DK, DV = 4, 128, 256
E, TOPK, DFF = 32, 4, 1024
FT = DFF // P
NA = SEQ * TOPK
EPS = 1e-5
LIMIT, SIG_ALPHA = 7.0, 1.702

CH = 2048
CW = CH // KD
C_U, C_Q, C_K, C_V, C_G, C_GA, C_GB = 0, 2, 4, 6, 10, 14, 18
C_GLU, C_BRET, C_BS5, C_OUT = 22, 23, 27, 29
N_TRUNK = 33
RING = 12
T_SLOTS = (0, 1, 5)
T_HI = (2, 3)
EXPERT_0 = 4
W2C = 4
EC = FT + W2C
N_ITEMS = E + NA // P
AHEAD = 3
N_HI = 4
POOL_SPLITS = (3, 6, 9)
NO_SLOT = 1 << 13

PAR = {}
_at = 0
for _n, _w in (("norm_mix", KD), ("ret_gn", KD), ("d_skip", S5W // P), ("b_glu", S5W // P),
               ("lam_re", GP), ("lam_im", GP), ("log_dt", GP), ("router_b", E)):
    PAR[_n] = (_at, _w)
    _at += _w
N_PAR = _at
CST = {}
_at = 0
for _n, _w in (("ident", P), ("before", P), ("ones", P), ("expert_id", E), ("item_id", N_ITEMS + 1), ("pick", E),
               ("assign_id", NT * TOPK),
               ("inv_freq", 1), ("sin_sign", 1)):
    CST[_n] = (_at, _w)
    _at += _w
N_CST = _at

TWO_PI = 2 * np.pi
PI_1 = 6.28125
PI_2 = float(np.float32(int((TWO_PI - PI_1) * 2 ** 21) / 2 ** 21))
PI_3 = float(np.float32(TWO_PI - PI_1 - PI_2))
PI_IN = 3.1415925
ROUND = 1.5 * 2 ** 23

JOBS = []


def _jobs(name, n, engine):
    JOBS.extend((f"{name}{i}", engine) for i in range(n))


_jobs("xT", KD, "V")
_jobs("u", 4, "A")
_jobs("ua", BT, "A")
_jobs("ub", 4, "V")
_jobs("q", HEADS, "V")
_jobs("k", HEADS, "V")
_jobs("hT", 8, "A")
_jobs("kb", 2, "V")
_jobs("xs", 4, "V")
_jobs("v", 8, "A")
for _h in range(HEADS):
    JOBS.extend([(f"sc{_h * 4 + j}", "V") for j in range(4)] + [(f"in{_h * 2 + j}", "V") for j in range(2)])
_jobs("g", KD, "A")
_jobs("rT", KD, "V")
_jobs("ga", KD, "A")
_jobs("ys", 4, "V")
_jobs("yc", BT, "A")
_jobs("yd", 4, "V")
_jobs("gb", KD, "A")
_jobs("z", 4, "A")
_jobs("yb", KD, "V")
_jobs("ya", KD, "V")
_jobs("wo", 8, "V")
_jobs("h2T", KD, "A")
_jobs("lg", 1, "V")
_jobs("rk", 1, "V")
_jobs("gT", 1, "V")
_jobs("b2", 8, "V")
_jobs("tb", 1, "V")
LAST_USE = [f"{name}{i}" for name, ids in (
    ("u", (1, 3)), ("q", (1, 3)), ("k", (1, 3)), ("v", (1, 3, 5, 7)), ("g", (1, 3, 5, 7)), ("ga", (1, 3, 5, 7)),
    ("gb", (1, 3, 5, 7)), ("z", (3,)), ("yb", (1, 3, 5, 7)), ("ya", (3, 7)), ("wo", (1, 3, 5, 7))) for i in ids]
JOB = {name: n for n, (name, _) in enumerate(JOBS)}
FIRST_LOADS = ((0, "z3"), (6, "z3"), (2, "yb7"), (3, "yb7"), (7, "ya7"), (8, "wo3"), (9, "wo5"), (11, "wo5"),
               (1, "wo7"), (4, "wo7"), (5, "wo7"), (10, "wo7"))
EMPTIED = []
_c = {"A": 0, "V": 0}
for _name, _e in JOBS:
    _c[_e] += 1
    EMPTIED.append((_e, _c[_e]))


def build(nc, x, pos, wt, we, par, s5bc, b1, b2, rw, g_ffn, g_fin, cst, dmask, fill, out):
    h2_dram = nc.dram_tensor("h2_rows", (SEQ, D), F32).ap()
    y_dram = nc.dram_tensor("y_rows", (NA, D), F32).ap()
    slot_dram = nc.dram_tensor("slots", ((N_ITEMS + 1) * P, 1), I32).ap()

    with ExitStack() as ctx:
        place = {}

        def sb(name, shape, dt=F32):
            return ctx.enter_context(nc.sbuf_tensor(name, shape, dt))

        def large(name, floats):
            t = sb(name, [P, floats])
            place[name] = nc.sbuf_base - 4 * floats
            return t

        def rounded(name, where, start, *shape):
            return nc.alloc_sbuf_tensor_at(name, [P, *shape], F32R, offset=place[where] + 4 * start)

        def sem(name):
            return ctx.enter_context(nc.semaphore(name))

        bank = [ctx.enter_context(nc.psum_tensor(f"bank{i}", [P, 512], F32)) for i in range(8)]

        ring = large("ring", RING * CH)[:, :].rearrange("p (s n) -> p s n", s=RING)
        big = [large(f"big{i}", 4096) for i in range(6)]
        uT = sb("uT", [P, 4, SEQ])
        par_s = sb("par_s", [P, N_PAR])
        cst_s = sb("cst_s", [P, N_CST])

        def prm(name, i=None, n=1):
            a, w = PAR[name]
            return par_s[:, a:a + w] if i is None else par_s[:, a + i:a + i + n]

        def con(name):
            a, w = CST[name]
            return cst_s[:, a:a + w]

        ident, ones = con("ident"), con("ones")

        h_hi, h_lo = (rounded(f"h_{n}", f"big{b}", 0, KD, SEQ) for n, b in (("hi", 0), ("lo", 4)))
        t_hi = [rounded(f"t_hi{i}", "ring", i * CH, CH)[:, :] for i in T_HI]
        w_lo = [rounded(f"w_lo{i}", "ring", i * CH, CH)[:, :] for i in range(RING)]
        xn = big[1][:, :].rearrange("p (i d) -> p i d", i=NT)
        rot_a, rot_b = big[1][:, 0:512], big[1][:, 512:1024]
        vt = xn
        ret = vt
        siga = big[1][:, :].rearrange("p (k t) -> p k t", k=KD)
        pos_i = big[2][:, 0:512].bitcast(I32)
        qT = big[2][:, 0:2048].rearrange("p (h t) -> p h t", h=HEADS)
        kT = big[2][:, 2048:4096].rearrange("p (h t) -> p h t", h=HEADS)
        gs = big[2][:, :].rearrange("p (k t) -> p k t", k=KD)
        gs_hi, gs_lo = rounded("gs_hi", "ring", 6 * CH, KD, SEQ), rounded("gs_lo", "big2", 0, KD, SEQ)
        cosT, sinT = big[3][:, 0:SEQ], big[3][:, SEQ:2 * SEQ]
        rope_k = big[3][:, 1024:1536]
        rope_t = big[3][:, 1536:2048]
        sT = big[3][:, 0:2048].rearrange("p (j t) -> p j t", j=NT)
        decay = big[3][:, 2048:4096].rearrange("p (h t) -> p h t", h=HEADS)
        sigb = big[3][:, :].rearrange("p (k t) -> p k t", k=KD)
        mg = big[4][:, :].rearrange("p (k t) -> p k t", k=KD)
        mg_hi, mg_lo = rounded("mg_hi", "ring", 8 * CH, KD, SEQ), rounded("mg_lo", "big4", 0, KD, SEQ)
        x2 = big[0][:, :].rearrange("p (i d) -> p i d", i=NT)
        h2 = big[1][:, :].rearrange("p (i d) -> p i d", i=NT)
        h2T = big[2][:, :].rearrange("p (k t) -> p k t", k=KD)

        s5a = ring[:, 6:8, :].rearrange("p a b -> p (a b)")
        s5b = ring[:, 8:10, :].rearrange("p a b -> p (a b)")
        pbr = s5a[:, 0:2048].rearrange("p (g m c) -> p g m c", g=GP, m=BT)
        pbi = s5a[:, 2048:4096].rearrange("p (g m c) -> p g m c", g=GP, m=BT)
        gre, gim = pbr, pbi
        yjr = s5a.rearrange("p (r c) -> p r c", r=BT)
        hTr = s5b[:, 0:2048].rearrange("p (g n) -> p g n", g=GP)
        hTi = s5b[:, 2048:4096].rearrange("p (g n) -> p g n", g=GP)
        m0T = s5b.rearrange("p (g n) -> p g n", g=NG)
        m0r = big[5][:, :].rearrange("p (r n) -> p r n", r=BT)
        ub = ring[:, 10, :].rearrange("p (g j) -> p g j", g=NG)
        xr = ring[:, 11, 0:1024].rearrange("p (g j) -> p g j", g=GP)
        xi = ring[:, 11, 1024:2048].rearrange("p (g j) -> p g j", g=GP)
        ujr = big[5][:, :].rearrange("p (g r c) -> p g r c", g=NG, r=BT)
        sc1 = big[5][:, 0:1024].rearrange("p (g j) -> p g j", g=GP)
        sc2 = big[5][:, 1024:2048].rearrange("p (g j) -> p g j", g=GP)
        ysb = big[5][:, 2048:4096].rearrange("p (g j) -> p g j", g=NG)
        zT = big[5][:, 0:2048].rearrange("p (k t) -> p k t", k=4)
        zg = big[5][:, 2048:4096].rearrange("p (k t) -> p k t", k=4)
        z_hi, z_lo = (rounded(f"z_{n}", "ring", i * CH, 4, SEQ) for n, i in (("hi", 4), ("lo", 10)))
        zg_hi, zg_lo = rounded("zg_hi", "ring", 11 * CH, 4, SEQ), rounded("zg_lo", "big5", 2048, 4, SEQ)
        k7 = ring[:, 4, 0:512]
        s5in = ring[:, 4, 512:1536].rearrange("p (a n) -> p a n", a=4)
        s5p = ring[:, 4, 1536:1536 + 24 * GP].rearrange("p (a n) -> p a n", a=24)
        bb = sb("bb", [P, 2, GP * GRP])

        xe, ye = big[1][:, 0:D], big[1][:, D:2 * D]
        b1_hl = rounded("b1_hl", "big1", 2048, 2 * DFF)[:, :]
        x_hi, x_lo = (rounded(f"x_{n}", "big2", i * D, KD, P) for i, n in enumerate(("hi", "lo")))
        b1_raw = big[2][:, 2048:4096]
        w_hi = [rounded(f"w_hi{i}", f"big{3 + i // 2}", (i % 2) * CH, CH)[:, :] for i in range(N_HI)]
        g_t, l_t, sg_t, gs_t, a_t = (big[5][:, 2 * i * P:2 * (i + 1) * P].rearrange("p (b t) -> p b t", b=2)
                                     for i in range(5))
        a_hi, a_lo = (rounded(f"a_{n}", "big5", (10 + i * FT) * P, FT, P) for i, n in enumerate(("hi", "lo")))
        pick = rounded("pick", "big5", (10 + 2 * FT) * P, P)[:, :]
        yk = [big[i][:, :].rearrange("p (k d) -> p k d", k=TOPK) for i in (1, 2)]
        flat_u = uT[:, :, :].rearrange("p c t -> p (c t)")
        gvec = flat_u[:, 0:D]
        b2_s = flat_u[0:E, D:2 * D]

        ss = sb("ss", [P, 4 * NT])
        stat = sb("stat", [P, NT, 8])
        mv = sb("mv", [P, NT, 4])
        rw_s = sb("rw_s", [P, KD, E])
        at = [0]

        def tmp_tile(rows, *shape):
            n = int(np.prod(shape))
            ap = big[5][0:rows, at[0]:at[0] + n]
            at[0] += n
            names = "abc"[:len(shape)]
            if len(shape) == 1:
                return ap
            return ap.rearrange(f"p ({' '.join(names)}) -> p {' '.join(names)}", **dict(zip(names, shape)))

        lg, cum, hot, gte = (tmp_tile(P, NT, E) for _ in range(4))
        oneh, wrk = (tmp_tile(P, NT, TOPK, E) for _ in range(2))
        n_of, n_blocks, end_a, end_b, first = (tmp_tile(P, E) for _ in range(5))
        ended = tmp_tile(1, N_ITEMS + 1, E)
        gTs, tabf = tmp_tile(E, SEQ), tmp_tile(N_ITEMS + 1, P)
        tabi = tmp_tile(N_ITEMS + 1, P).bitcast(I32)
        top_v = sb("top_v", [P, NT, 8])
        top_i = sb("top_i", [P, NT, 8], U32)
        top_f = sb("top_f", [P, NT, 8])
        gate = sb("gate", [P, NT, TOPK])
        negm = sb("negm", [P, NT])
        gsum = sb("gsum", [P, 2 * NT])
        rank = sb("rank", [P, NT * TOPK])
        dest = sb("dest", [P, NT * TOPK], U32)
        aid = sb("aid", [P, NT * TOPK], I32)
        item_f = sb("item_f", [1, N_ITEMS + 2])
        item_e = sb("item_e", [1, N_ITEMS + 2], I32)
        put_i = sb("put_i", [P, N_ITEMS + 1], I32)
        get_i = sb("get_i", [P, N_ITEMS + 1], I32)
        get_1, put_1 = sb("get_1", [P, 1], I32), sb("put_1", [P, 1], I32)

        landed = [sem(f"landed{i}") for i in range(RING)]
        bank_full = sem("bank_full")
        act_emptied, dve_emptied = sem("act_emptied"), sem("dve_emptied")
        act_chain, dve_chain, pool_chain = sem("act_chain"), sem("dve_chain"), sem("pool_chain")
        x_in, x_in2 = [sem(f"x_in{i}") for i in range(NT)], [sem(f"x_again{i}") for i in range(NT)]
        par_in, cst_in, pos_in, dec_in = sem("par_in"), sem("cst_in"), sem("pos_in"), sem("dec_in")
        moe_in, gf_in, gfin_in = sem("moe_in"), sem("gf_in"), sem("gfin_in")
        squares, rstd_ready, xn_ready = sem("squares"), sem("rstd_ready"), sem("xn_ready")
        h_rounded = sem("h_rounded")
        t_rounded, t_split = sem("t_rounded"), sem("t_split")
        z_rounded, z_split, zg_split = sem("z_rounded"), sem("z_split"), sem("zg_split")
        gated_rounded, gated_split = sem("gated_rounded"), sem("gated_split")
        mg_rounded, mg_split = sem("mg_rounded"), sem("mg_split")
        rope_act = sem("rope_act")
        s5_act, s5_pool = sem("s5_act"), sem("s5_pool")
        pb_ready, g_ready, scan_done = sem("pb_ready"), sem("g_ready"), sem("scan_done")
        m0_zero, m0_in, m0_ready = sem("m0_zero"), sem("m0_in"), sem("m0_ready")
        gn_var, gn_std = sem("gn_var"), sem("gn_std")
        h2_ready, h2_out = sem("h2_ready"), sem("h2_out")
        top_ready, gate_exp = sem("top_ready"), sem("gate_exp")
        hot_ready, gte_ready = sem("hot_ready"), sem("gte_ready")
        fill_in, dest_ready, slots_put, slots_in = sem("fill_in"), sem("dest_ready"), sem("slots_put"), sem("slots_in")
        tabf_ready = sem("tabf_ready")
        moved = sem("moved")
        get_ready, put_ready = sem("get_ready"), sem("put_ready")
        index_seen = sem("index_seen")
        ye_free = sem("ye_free")
        xe_zero = sem("xe_zero")
        b1_zero, b1_in, b1_ready = sem("b1_zero"), sem("b1_in"), sem("b1_ready")
        pick_ready = sem("pick_ready")
        w_rounded, w_split, w_split_p = sem("w_rounded"), sem("w_split"), sem("w_split_p")
        x_full, x_rounded, x_split = sem("x_full"), sem("x_rounded"), sem("x_split")
        gu_full, gu_empty = sem("gu_full"), sem("gu_empty")
        glu_ready, sg_ready, gs_ready, act_ready = sem("glu_ready"), sem("sig_ready"), sem("gs_ready"), sem("act_ready")
        a_full, a_rounded, a_split = sem("a_full"), sem("a_rounded"), sem("a_split")
        y_full, y_empty = sem("y_full"), sem("y_empty")
        angles, den_ready, neg_c, tab_ready = sem("angles"), sem("den_ready"), sem("neg_c"), sem("tab_ready")
        yk_in = [sem("yk_in0"), sem("yk_in1")]
        summed, fsq, frstd, fin_ready, out_done = sem("summed"), sem("fsq"), sem("frstd"), sem("fin_ready"), sem("out_done")
        dumped = sem("dumped")

        EMPT = {"A": act_emptied, "V": dve_emptied}

        def full(name):
            return bank_full, JOB[name] + 1

        def emptied(name):
            e, n = EMPTIED[JOB[name]]
            return EMPT[e], n

        def t_slot(n):
            return T_SLOTS[n % len(T_SLOTS)]

        def used(i, c):
            return (gu_full, i * FT + (c + 1)) if c < FT else (y_full, i * W2C + (c - FT + 1 + W2C))

        def item_chunk(i, c):
            slot = (EXPERT_0 + c) % RING
            before = sum(1 for n in range(N_TRUNK) if t_slot(n) == slot)
            return slot, (landed[slot], i * 16 + 16 * (before + 1))

        def split(i, c):
            if c in POOL_SPLITS:
                return w_split_p, i * len(POOL_SPLITS) + (POOL_SPLITS.index(c) + 1)
            return w_split, i * (EC - len(POOL_SPLITS)) + (1 + sum(1 for n in range(c) if n not in POOL_SPLITS))

        def bk(name):
            return bank[JOB[name] % 8]

        def bc(ap, n):
            return ap.unsqueeze(2).to_broadcast([ap.shape[0], ap.shape[1], n])

        block = ctx.enter_context(nc.Block())

        @block.sync
        def _(sp):
            sp.dma_start(cst_s[:, :], cst).then_inc(cst_in, 16)
            sp.wait_ge(x_in[NT - 1], 16)
            for n in range(N_TRUNK):
                if n >= len(T_SLOTS):
                    sp.wait_ge(*full(LAST_USE[n - len(T_SLOTS)]))
                sp.dma_start(ring[:, t_slot(n), :], wt[n]).then_inc(landed[t_slot(n)], 16)
                if n == 1:
                    sp.dma_start(decay, dmask).then_inc(dec_in, 16)
            for c, last in FIRST_LOADS:
                sp.wait_ge(*full(last))
                slot = item_chunk(0, c)[0]
                sp.dma_start(ring[:, slot, :], we[0, c]).then_inc(landed[slot], 16)
            sp.wait_ge(tab_ready, 1)

            def load(i, chunks):
                e = sp.value_load(item_e[0:1, bass.ds(i, 1)], min_val=0, max_val=E - 1)
                for c in chunks:
                    slot = item_chunk(i, c)[0]
                    sp.wait_ge(*used(i - 1, c))
                    sp.dma_start(ring[:, slot, :], we[bass.ds(e, 1), c].rearrange("o p n -> (o p) n"))\
                        .then_inc(landed[slot], 16)

            def item(i):
                load(i, range(AHEAD, EC))
                load(i + 1, range(AHEAD))

            load(1, range(AHEAD))
            with sp.Fori(1, E) as i:
                item(i)
            n = sp.value_load(item_e[0:1, N_ITEMS + 1:N_ITEMS + 2], min_val=E, max_val=N_ITEMS)
            with sp.If(n > E):
                with sp.Fori(E, N_ITEMS) as i:
                    with sp.If(i < n):
                        item(i)
                    sp.nop()
            sp.nop()
            sp.wait_ge(y_full, n * W2C + W2C)
            sp.wait_ge(moved, n * 32 + 16)
            for i in range(NT):
                if i >= 2:
                    sp.wait_ge(summed, i - 1)
                sp.dma_start(yk[i % 2], y_dram.rearrange("(i p k) d -> i p k d", i=NT, p=P)[i])\
                    .then_inc(yk_in[i % 2], 16)
            for i in range(NT):
                sp.wait_ge(fin_ready, i + 1)
                sp.dma_start(out[i * P:(i + 1) * P, :], x2[:, i, :]).then_inc(out_done, 16)
            sp.wait_ge(out_done, 16 * NT)

        @block.gpsimd
        def _(pool):
            n_chain = [0]

            def step(ins):
                n_chain[0] += 1
                ins.then_inc(pool_chain, 1)
                pool.wait_ge(pool_chain, n_chain[0])

            TT = pool.tensor_tensor
            rs = ss[:, NT:2 * NT]
            mhalf = ss[:, 3 * NT:4 * NT]
            step(pool.memset(mhalf, -0.5))

            def row_rstd(i):
                step(pool.tensor_scalar(rs[:, i:i + 1], ss[:, i:i + 1], 1.0 / D, EPS, ALU.mult, ALU.add))
                return TT(rs[:, i:i + 1], rs[:, i:i + 1], mhalf[:, 0:1], ALU.pow)

            for i in range(NT):
                pool.wait_ge(squares, i + 1)
                row_rstd(i).then_inc(rstd_ready, 1)

            pr = lambda i: s5p[:, i, :]
            DT, TH, MAG, SIN, COS, AR, AI, NR, T1, T2, DEN, FR, FI, T3, KR, RR, A8R, A8I = range(18)
            pool.wait_ge(par_in, 32)
            pool.wait_ge(s5_act, 1)
            step(TT(pr(T1), prm("lam_re"), pr(DT), ALU.mult))
            TT(pr(TH), prm("lam_im"), pr(DT), ALU.mult).then_inc(s5_pool, 1)
            pool.wait_ge(s5_act, 4)
            step(TT(pr(AR), pr(MAG), pr(COS), ALU.mult))
            step(TT(pr(AI), pr(MAG), pr(SIN), ALU.mult))
            step(pool.tensor_scalar(pr(NR), pr(AR), 1.0, -1.0, ALU.mult, ALU.add))
            step(TT(pr(T1), prm("lam_re"), prm("lam_re"), ALU.mult))
            step(TT(pr(T2), prm("lam_im"), prm("lam_im"), ALU.mult))
            TT(pr(DEN), pr(T1), pr(T2), ALU.add).then_inc(s5_pool, 1)
            pool.wait_ge(s5_pool, 2)
            step(TT(pr(T1), pr(NR), prm("lam_re"), ALU.mult))
            step(TT(pr(T2), pr(AI), prm("lam_im"), ALU.mult))
            step(TT(pr(FR), pr(T1), pr(T2), ALU.add))
            step(TT(pr(T1), pr(AI), prm("lam_re"), ALU.mult))
            step(TT(pr(T2), pr(NR), prm("lam_im"), ALU.mult))
            step(TT(pr(FI), pr(T1), pr(T2), ALU.subtract))
            pool.wait_ge(den_ready, 1)
            step(TT(pr(FR), pr(FR), pr(T3), ALU.mult))
            step(TT(pr(FI), pr(FI), pr(T3), ALU.mult))

            v3 = lambda ap: ap.rearrange("p (g c) -> p g c", g=GP)
            t_a, t_b = v3(bb[:, 0, :]), v3(bb[:, 1, :])

            def cmul(dr, di, ar, ai, br, bi):
                ar, ai = bc(ar, GRP), bc(ai, GRP)
                step(TT(t_a, br, ar, ALU.mult))
                step(TT(t_b, bi, ai, ALU.mult))
                step(TT(dr, t_a, t_b, ALU.subtract))
                step(TT(t_a, bi, ar, ALU.mult))
                step(TT(t_b, br, ai, ALU.mult))
                return TT(di, t_a, t_b, ALU.add)

            step(cmul(pbr[:, :, 7, :], pbi[:, :, 7, :], pr(FR), pr(FI), v3(s5in[:, 0, :]), v3(s5in[:, 1, :])))
            for m in range(1, BT):
                last = cmul(pbr[:, :, 7 - m, :], pbi[:, :, 7 - m, :], pr(AR), pr(AI),
                            pbr[:, :, 8 - m, :], pbi[:, :, 8 - m, :])
                if m < BT - 1:
                    step(last)
            last.then_inc(pb_ready, 1)
            pool.tensor_scalar(s5in[:, 1, :], s5in[:, 3, :], -1.0, 0.0, ALU.mult, ALU.add).then_inc(neg_c, 1)
            step(pool.tensor_copy(pr(A8R), pr(AR)))
            step(pool.tensor_copy(pr(A8I), pr(AI)))

            def square():
                step(TT(pr(T1), pr(A8R), pr(A8R), ALU.mult))
                step(TT(pr(T2), pr(A8I), pr(A8I), ALU.mult))
                step(TT(pr(KR), pr(A8R), pr(A8I), ALU.mult))
                step(TT(pr(A8R), pr(T1), pr(T2), ALU.subtract))
                step(TT(pr(A8I), pr(KR), pr(KR), ALU.add))

            for _ in range(3):
                square()
            pool.wait_ge(*full("kb1"))
            step(cmul(gre[:, :, 0, :], gim[:, :, 0, :], pr(AR), pr(AI), v3(s5in[:, 2, :]), v3(s5in[:, 3, :])))
            for r in range(1, BT):
                step(cmul(gre[:, :, r, :], gim[:, :, r, :], pr(AR), pr(AI),
                          gre[:, :, r - 1, :], gim[:, :, r - 1, :]))
            pool.tensor_scalar(s5a[:, 2048:4096], s5a[:, 2048:4096], -1.0, 0.0, ALU.mult, ALU.add)\
                .then_inc(g_ready, 1)
            pool.wait_ge(*emptied("kb1"))
            pool.wait_ge(*full("ub3"))
            pool.memset(big[5][:, :], 0.0).then_inc(m0_zero, 1)
            pool.wait_ge(m0_zero, 1)
            for r in range(BT):
                n = GRP * (r + 1)
                pool.dma_start(m0r[0:n, r, :], k7[P - n:P, :]).then_inc(m0_in, 16)
            pool.wait_ge(m0_in, 16 * BT)
            pool.wait_ge(*full("xs3"))
            pool.tensor_copy(m0T.rearrange("p g (r c) -> p g r c", r=BT),
                             m0r.rearrange("p r (g c) -> p g r c", g=NG)).then_inc(m0_ready, 1)
            pool.wait_ge(m0_ready, 1)
            pool.wait_ge(*emptied("xs3"))
            d = 1
            while d < NB:
                w = NB - d
                ar, ai = bc(pr(A8R), w), bc(pr(A8I), w)
                s1, s2 = sc1[:, :, 0:w], sc2[:, :, 0:w]
                t1, t2 = ysb[:, 0:GP, 0:w], ysb[:, GP:2 * GP, 0:w]
                fr, fi, tr, ti = xr[:, :, 0:w], xi[:, :, 0:w], xr[:, :, d:NB], xi[:, :, d:NB]
                step(TT(s1, fr, ar, ALU.mult))
                step(TT(t1, fi, ai, ALU.mult))
                step(TT(s2, fi, ar, ALU.mult))
                step(TT(t2, fr, ai, ALU.mult))
                step(TT(s1, s1, t1, ALU.subtract))
                step(TT(s2, s2, t2, ALU.add))
                step(TT(tr, tr, s1, ALU.add))
                last = TT(ti, ti, s2, ALU.add)
                d *= 2
                if d < NB:
                    step(last)
                    square()
            last.then_inc(scan_done, 1)

            for i in range(NT):
                pool.wait_ge(squares, NT + i + 1)
                row_rstd(i).then_inc(rstd_ready, 1)

            pool.dma_start(slot_dram.rearrange("(e s) o -> e (s o)", e=N_ITEMS + 1), fill).then_inc(fill_in, 16)
            pool.wait_ge(fill_in, 16)
            pool.wait_ge(dest_ready, 1)
            for c in range(NT * TOPK):
                pool.indirect_dma_start(slot_dram, bass.IndirectOffsetOnAxis(dest[:, c:c + 1], 0),
                                        aid[:, c:c + 1], None).then_inc(slots_put, 16)
            pool.wait_ge(slots_put, 16 * NT * TOPK)
            pool.dma_start(tabi[:, :], slot_dram.rearrange("(e s) o -> e (s o)", e=N_ITEMS + 1)).then_inc(slots_in, 16)

            pool.wait_ge(*full("lg0"))
            pool.memset(b1_raw, 0.0).then_inc(b1_zero, 1)
            pool.wait_ge(h2_out, 16 * NT)
            pool.memset(xe, 0.0).then_inc(xe_zero, 1)
            pool.wait_ge(xe_zero, 1)
            pool.wait_ge(tab_ready, 1)
            token_bound, assign_bound = pool.to_reg(SEQ - 1), pool.to_reg(NA - 1)

            def gather(i):
                pool.tensor_copy(get_1[:, :], get_i[:, bass.ds(i, 1)]).then_inc(get_ready, 1)
                pool.wait_ge(get_ready, i + 1)
                pool.sem_inc(index_seen, 1)
                pool.indirect_dma_start(xe, None, h2_dram, bass.IndirectOffsetOnAxis(get_1[:, 0:1], 0),
                                        bounds_check=token_bound, oob_is_err=False).then_inc(moved, 16)

            def scatter(i):
                pool.tensor_copy(put_1[:, :], put_i[:, bass.ds(i, 1)]).then_inc(put_ready, 1)
                pool.wait_ge(put_ready, i + 1)
                pool.wait_ge(y_empty, i * W2C + (W2C + 2))
                pool.sem_inc(index_seen, 1)
                pool.indirect_dma_start(y_dram, bass.IndirectOffsetOnAxis(put_1[:, 0:1], 0), ye, None,
                                        bounds_check=assign_bound, oob_is_err=False).then_inc(moved, 16)

            def split_chunk(i, c):
                pool.wait_ge(w_rounded, i * EC + (c + 1))
                slot = item_chunk(i, c)[0]
                TT(w_lo[slot], ring[:, slot, :], w_hi[c % N_HI].bitcast(F32), ALU.subtract).then_inc(w_split_p, 1)

            def item(i):
                split_chunk(i, POOL_SPLITS[0])
                pool.wait_ge(moved, i * 32 + 16)
                pool.sem_inc(ye_free, 1)
                pool.wait_ge(x_full, i * 2 + 2)
                gather(i + 1)
                for c in POOL_SPLITS[1:]:
                    split_chunk(i, c)
                scatter(i)

            gather(0)
            n = pool.value_load(item_e[0:1, N_ITEMS + 1:N_ITEMS + 2], min_val=E, max_val=N_ITEMS)
            with pool.Fori(0, E) as i:
                item(i)
            with pool.If(n > E):
                with pool.Fori(E, N_ITEMS) as i:
                    with pool.If(i < n):
                        item(i)
                    pool.nop()
            pool.nop()
            for i in range(NT):
                pool.wait_ge(fsq, i + 1)
                row_rstd(i).then_inc(frstd, 1)

        @block.scalar
        def _(act):
            n_chain = [0]

            def step(ins):
                n_chain[0] += 1
                ins.then_inc(act_chain, 1)
                act.wait_ge(act_chain, n_chain[0])

            xt = x.rearrange("(i p) d -> i p d", i=NT)
            for i in range(NT):
                act.dma_start(xn[:, i, :], xt[i]).then_inc(x_in[i], 16)
            act.dma_start(par_s[:, :], par).then_inc(par_in, 16)
            act.dma_start(ring[:, 4, 512:1536], s5bc).then_inc(par_in, 16)
            act.dma_start(pos_i, pos.partition_broadcast(P)).then_inc(pos_in, 16)
            act.dma_start(rw_s[:, :, :], rw).then_inc(moe_in, 16)

            for i in range(NT):
                act.wait_ge(x_in[i], 16)
                act.activation(big[0][:, i * D:(i + 1) * D], xn[:, i, :], ACT.Square,
                               accum_out=ss[:, i:i + 1]).then_inc(squares, 1)

            def round_chunk_t(n):
                act.wait_ge(landed[t_slot(n)], 16 * (n // len(T_SLOTS) + 1))
                if n >= len(T_HI):
                    act.wait_ge(*full(LAST_USE[n - len(T_HI)]))
                act.activation(t_hi[n % 2], ring[:, t_slot(n), :], ACT.Copy).then_inc(t_rounded, 1)

            round_chunk_t(0)
            act.wait_ge(par_in, 32)
            act.wait_ge(squares, NT)
            for k in range(KD):
                act.wait_ge(*full(f"xT{k}"))
                act.activation(h_hi[:, k, :], bk(f"xT{k}")[:, :], ACT.Copy,
                               scale=prm("norm_mix", k)).then_inc(h_rounded, 1)
            round_chunk_t(1)
            pr = lambda i: s5p[:, i, :]
            act.activation(pr(0), prm("log_dt"), ACT.Exp).then_inc(s5_act, 1)
            act.wait_ge(s5_pool, 1)
            act.activation(pr(2), pr(8), ACT.Exp).then_inc(s5_act, 1)
            act.wait_ge(angles, 1)
            act.activation(pr(3), pr(15), ACT.Sin).then_inc(s5_act, 1)
            act.activation(pr(4), pr(14), ACT.Sin).then_inc(s5_act, 1)
            act.wait_ge(angles, 2)
            act.activation(sinT, sinT, ACT.Sin).then_inc(rope_act, 1)
            act.activation(cosT, cosT, ACT.Sin).then_inc(rope_act, 1)
            for c in range(4):
                act.wait_ge(*full(f"u{c}"))
                act.activation(uT[:, c, :], bk(f"u{c}")[:, :], ACT.Copy).then_inc(act_emptied, 1)
                if c % 2:
                    round_chunk_t(C_U + c // 2 + 2)
            for r in range(BT):
                act.wait_ge(*full(f"ua{r}"))
                act.activation(ujr[0:NB, :, r, :], bk(f"ua{r}")[0:NB, :].rearrange("p (g c) -> p g c", g=NG),
                               ACT.Copy).then_inc(act_emptied, 1)
            for n in range(C_Q + 2, C_V + 2):
                round_chunk_t(n)
            for i in range(8):
                dst = (hTr, hTi)[i // 4]
                act.wait_ge(*full(f"hT{i}"))
                act.activation(dst[:, 4 * (i % 4):4 * (i % 4) + 4, :].rearrange("p g n -> p (g n)"),
                               bk(f"hT{i}")[:, :], ACT.Copy).then_inc(act_emptied, 1)
            act.wait_ge(*emptied("k3"))
            for c in range(4):
                for i in range(2):
                    act.wait_ge(*full(f"v{2 * c + i}"))
                    act.activation(vt[:, 2 * i:2 * i + 2, c * CW:(c + 1) * CW],
                                   bk(f"v{2 * c + i}")[:, :].rearrange("p (a n) -> p a n", a=2),
                                   ACT.Copy).then_inc(act_emptied, 1)
                round_chunk_t(C_V + c + 2)
            for h in range(HEADS):
                act.wait_ge(gn_var, h + 1)
                act.activation(mv[:, :, 2], mv[:, :, 1], ACT.Sqrt).then_inc(gn_std, 1)
            for k in range(KD):
                act.wait_ge(*full(f"g{k}"))
                act.activation(gs[:, k, :], bk(f"g{k}")[:, :], ACT.Silu).then_inc(act_emptied, 1)
                if k % 2:
                    round_chunk_t(C_G + k // 2 + 2)
            for k in range(KD):
                act.wait_ge(*full(f"ga{k}"))
                act.activation(siga[:, k, :], bk(f"ga{k}")[:, :], ACT.Sigmoid).then_inc(act_emptied, 1)
                if k % 2:
                    round_chunk_t(C_GA + k // 2 + 2)
            for r in range(BT):
                act.wait_ge(*full(f"yc{r}"))
                act.activation(yjr[0:NB, :, 64 * r:64 * r + 64],
                               bk(f"yc{r}")[0:NB, :].rearrange("p (g r c) -> p r g c", g=4, r=BT),
                               ACT.Copy).then_inc(act_emptied, 1)
            act.wait_ge(*emptied("yd3"))
            act.dma_start(b2_s, b2).then_inc(moe_in, 16)
            act.dma_start(gvec, g_ffn.partition_broadcast(P)).then_inc(gf_in, 16)
            step(act.activation(zT[:, :, :], zT[:, :, :], ACT.Gelu_apprx_tanh))
            act.activation(z_hi[:, :, :], zT[:, :, :], ACT.Copy).then_inc(z_rounded, 1)
            act.wait_ge(*emptied("rT7"))
            for h in range(2):
                act.activation(gs_hi[:, 4 * h:4 * h + 4, :], gs[:, 4 * h:4 * h + 4, :], ACT.Copy)\
                    .then_inc(gated_rounded, 1)
            for k in range(KD):
                act.wait_ge(*full(f"gb{k}"))
                act.activation(sigb[:, k, :], bk(f"gb{k}")[:, :], ACT.Sigmoid).then_inc(act_emptied, 1)
                if k % 2:
                    round_chunk_t(C_GB + k // 2 + 2)
            for c in range(4):
                act.wait_ge(*full(f"z{c}"))
                act.activation(zg[:, c, :], bk(f"z{c}")[:, :], ACT.Sigmoid,
                               bias=prm("b_glu", c)).then_inc(act_emptied, 1)
            round_chunk_t(C_GLU + 2)
            act.wait_ge(*full("gb7"))
            for i in range(NT):
                act.dma_start(x2[:, i, :], xt[i]).then_inc(x_in2[i], 16)
            for c in range(4):
                round_chunk_t(C_BRET + c + 2)
            for k in range(KD):
                act.wait_ge(*emptied(f"ya{k}"))
                act.activation(mg_hi[:, k, :], mg[:, k, :], ACT.Copy).then_inc(mg_rounded, 1)
                if k % 4 == 3:
                    round_chunk_t(C_BS5 + k // 4 + 2)
            for c in range(2):
                round_chunk_t(C_OUT + c + 2)
            for i in range(NT):
                act.wait_ge(*emptied(f"wo{6 + i // 2}"))
                act.activation(h2[:, i, :], x2[:, i, :], ACT.Square,
                               accum_out=ss[:, i:i + 1]).then_inc(squares, 1)
            for k in range(KD):
                act.wait_ge(*full(f"h2T{k}"))
                act.activation(h2T[:, k, :], bk(f"h2T{k}")[:, :], ACT.Copy).then_inc(act_emptied, 1)
            act.wait_ge(top_ready, 1)
            for i in range(NT):
                act.activation(gate[:, i, :], top_v[:, i, 0:TOPK], ACT.Exp, bias=negm[:, i:i + 1],
                               accum_out=gsum[:, i:i + 1]).then_inc(gate_exp, 1)
            act.wait_ge(h2_ready, NT)
            act.dma_start(gvec, g_fin.partition_broadcast(P)).then_inc(gfin_in, 16)
            for i in range(NT):
                act.dma_start(h2_dram[i * P:(i + 1) * P, :], h2[:, i, :]).then_inc(h2_out, 16)

            act.wait_ge(b1_zero, 1)
            for half in range(2):
                act.dma_start(b1_raw[half * E:(half + 1) * E, :], b1).then_inc(b1_in, 16)

            def round_chunk(i, c):
                slot, arrived = item_chunk(i, c)
                act.wait_ge(*arrived)
                act.activation(w_hi[c % N_HI], ring[:, slot, :], ACT.Copy).then_inc(w_rounded, 1)

            def round_rows(i):
                for h in range(2):
                    act.wait_ge(x_full, i * 2 + (h + 1))
                    act.activation(x_hi[:, 4 * h:4 * h + 4, :].rearrange("p k t -> p (k t)"), bank[4 + h][:, :],
                                   ACT.Copy).then_inc(x_rounded, 1)

            def round_tile(i, j):
                act.wait_ge(a_full, i * FT + (j + 1))
                act.activation(a_hi[:, j, :], bank[2 + j % 2][:, 0:P], ACT.Copy).then_inc(a_rounded, 1)

            def item(i):
                for s in range(EC):
                    if 1 <= s <= FT:
                        j = s - 1
                        act.wait_ge(glu_ready, i * FT + (j + 1))
                        act.activation(sg_t[:, j % 2, :], g_t[:, j % 2, :], ACT.Sigmoid,
                                       scale=SIG_ALPHA).then_inc(sg_ready, 1)
                        if j > 0:
                            round_tile(i, j - 1)
                    if s == FT:
                        round_rows(i + 1)
                        round_tile(i, FT - 1)
                    if s > FT:
                        results(i, s - FT - 1)
                    c = s + AHEAD
                    if c < EC:
                        act.wait_ge(*(used(i, c - N_HI) if c >= N_HI else used(i - 1, c - N_HI + EC)))
                        round_chunk(i, c)
                    else:
                        act.wait_ge(*used(i, c - N_HI))
                        round_chunk(i + 1, c - EC)
                results(i, W2C - 1)

            def results(i, c):
                if c == 0:
                    act.wait_ge(ye_free, i + 1)
                act.wait_ge(y_full, i * W2C + (c + 1 + W2C))
                act.activation(ye[:, c * CW:(c + 1) * CW], bank[6 + c % 2][:, 0:CW], ACT.Copy).then_inc(y_empty, 1)

            act.sem_inc(y_empty, 2)
            act.wait_ge(*full("wo7"))
            for c in range(AHEAD):
                round_chunk(0, c)
            act.wait_ge(tab_ready, 1)
            round_rows(0)
            n = act.value_load(item_e[0:1, N_ITEMS + 1:N_ITEMS + 2], min_val=E, max_val=N_ITEMS)
            with act.Fori(0, E) as i:
                item(i)
            with act.If(n > E):
                with act.Fori(E, N_ITEMS) as i:
                    with act.If(i < n):
                        item(i)
                    act.nop()
            act.nop()
            for i in range(NT):
                act.wait_ge(summed, i + 1)
                act.activation(big[3][:, i * D:(i + 1) * D], x2[:, i, :], ACT.Square,
                               accum_out=ss[:, i:i + 1]).then_inc(fsq, 1)

        @block.vector
        def _(dve):
            n_chain = [0]

            def step(ins):
                n_chain[0] += 1
                ins.then_inc(dve_chain, 1)
                dve.wait_ge(dve_chain, n_chain[0])

            TT, TS, STT = dve.tensor_tensor, dve.tensor_scalar, dve.scalar_tensor_tensor
            rs = ss[:, NT:2 * NT]

            def split_chunk_t(n):
                dve.wait_ge(t_rounded, n + 1)
                TT(w_lo[t_slot(n)], ring[:, t_slot(n), :], t_hi[n % 2].bitcast(F32), ALU.subtract)\
                    .then_inc(t_split, 1)

            for i in range(NT):
                dve.wait_ge(rstd_ready, i + 1)
                TS(xn[:, i, :], xn[:, i, :], rs[:, i:i + 1], None, ALU.mult).then_inc(xn_ready, 1)

            def reduce_angle(r, c, tk):
                step(TS(tk, r, 1.0 / TWO_PI, ROUND, ALU.mult, ALU.add))
                step(TS(tk, tk, ROUND, None, ALU.subtract))
                for part in (PI_1, PI_2, PI_3):
                    step(STT(r, tk, -part, r, ALU.mult, ALU.add))
                step(TS(r, r, PI_IN, -PI_IN, ALU.min, ALU.max))
                step(TS(tk, r, -1.0, None, ALU.mult))
                step(TT(tk, tk, r, ALU.max))
                return TS(c, tk, -1.0, float(np.float32(np.pi / 2)), ALU.mult, ALU.add)

            split_chunk_t(0)
            for k in range(KD):
                dve.wait_ge(h_rounded, k + 1)
                STT(h_lo[:, k, :], bk(f"xT{k}")[:, :], prm("norm_mix", k), h_hi[:, k, :].bitcast(F32),
                    ALU.mult, ALU.subtract).then_inc(dve_emptied, 1)
            split_chunk_t(1)
            pr = lambda i: s5p[:, i, :]
            dve.wait_ge(s5_pool, 1)
            step(dve.tensor_copy(pr(15), pr(1)))
            reduce_angle(pr(15), pr(14), pr(18)).then_inc(angles, 1)
            dve.wait_ge(s5_pool, 2)
            dve.reciprocal(pr(13), pr(10)).then_inc(den_ready, 1)
            dve.wait_ge(pos_in, 16)
            dve.wait_ge(cst_in, 16)
            step(dve.tensor_copy(rope_k, pos_i))
            step(TS(sinT, rope_k, con("inv_freq"), None, ALU.mult))
            reduce_angle(sinT, cosT, rope_k).then_inc(angles, 1)
            for n in range(C_U + 2, C_Q + 2):
                split_chunk_t(n)
            for i in range(4):
                dve.wait_ge(*full(f"ub{i}"))
                dve.tensor_copy(ub[:, 8 * i:8 * i + 8, :].rearrange("p g j -> p (g j)"),
                                bk(f"ub{i}")[:, :]).then_inc(dve_emptied, 1)
            dve.wait_ge(rope_act, 2)
            step(TS(sinT, sinT, con("sin_sign"), None, ALU.mult))
            H = DK // 2
            for name, dst, scale, c0 in (("q", qT, 1.0, C_Q), ("k", kT, DK ** -0.5, C_K)):
                for h in range(HEADS):
                    dve.wait_ge(*full(f"{name}{h}"))
                    b = bk(f"{name}{h}")
                    if (name, h) != ("q", 0):
                        dve.wait_ge(*emptied(f"{name}{h - 1}" if h else "q3"))
                    STT(rot_a, b[:, :], scale, cosT, ALU.mult, ALU.mult)
                    STT(rot_b[0:H, :], b[H:P, :], scale, sinT[0:H, :], ALU.mult, ALU.mult)
                    step(STT(rot_b[H:P, :], b[0:H, :], scale, sinT[H:P, :], ALU.mult, ALU.mult))
                    TT(dst[:, h, :], rot_a, rot_b, ALU.add).then_inc(dve_emptied, 1)
                    if h % 2:
                        split_chunk_t(c0 + h // 2 + 2)
            for odd in range(2):
                dve.wait_ge(*full(f"kb{odd}"))
                dve.tensor_copy(k7.rearrange("p (g o c) -> p g o c", o=2, c=GRP)[:, :, odd, :],
                                bk(f"kb{odd}")[:, 0:GP * GRP].rearrange("p (g c) -> p g c", g=GP))\
                    .then_inc(dve_emptied, 1)
            for i in range(4):
                dst = (xr, xi)[i // 2]
                dve.wait_ge(*full(f"xs{i}"))
                dve.tensor_copy(dst[:, 8 * (i % 2):8 * (i % 2) + 8, :].rearrange("p g j -> p (g j)"),
                                bk(f"xs{i}")[:, :]).then_inc(dve_emptied, 1)
            for n in range(C_V + 2, C_G + 2):
                split_chunk_t(n)
            dve.wait_ge(dec_in, 16)
            for h in range(HEADS):
                for j in range(NT):
                    w = SEQ - j * P
                    dve.wait_ge(*full(f"sc{4 * h + j}"))
                    TT(sT[:, j, 0:w], bk(f"sc{4 * h + j}")[:, 0:w], decay[:, h, 0:w],
                       ALU.mult).then_inc(dve_emptied, 1)
                for m in range(2):
                    b = bk(f"in{2 * h + m}")
                    dve.wait_ge(*full(f"in{2 * h + m}"))
                    for a in range(2):
                        last = dve.bn_stats(stat[:, 2 * m + a, 0:6], b[:, a * DV:(a + 1) * DV])
                step(last)
                if h:
                    dve.wait_ge(*emptied(f"in{2 * h - 1}"))
                for i in range(NT):
                    last = dve.bn_aggr(mv[:, i, 0:2], stat[:, i, 0:6])
                step(last)
                TS(mv[:, :, 1], mv[:, :, 1], EPS, None, ALU.add).then_inc(gn_var, 1)
                dve.wait_ge(gn_std, h + 1)
                step(dve.reciprocal(mv[:, :, 2], mv[:, :, 2]))
                for i in range(NT):
                    b = bk(f"in{2 * h + i // 2}")
                    last = TS(ret[:, i, h * DV:(h + 1) * DV], b[:, (i % 2) * DV:(i % 2 + 1) * DV],
                              mv[:, i, 0:1], mv[:, i, 2:3], ALU.subtract, ALU.mult)
                    if i % 2:
                        last.then_inc(dve_emptied, 1)
            for n in range(C_G + 2, C_GA + 2):
                split_chunk_t(n)
            for k in range(KD):
                dve.wait_ge(*full(f"rT{k}"))
                dve.wait_ge(*emptied(f"g{k}"))
                STT(gs[:, k, :], bk(f"rT{k}")[:, :], prm("ret_gn", k), gs[:, k, :],
                    ALU.mult, ALU.mult).then_inc(dve_emptied, 1)
            for n in range(C_GA + 2, C_GB + 2):
                split_chunk_t(n)
            for i in range(4):
                dve.wait_ge(*full(f"ys{i}"))
                dve.tensor_copy(ysb.rearrange("p (g o) j -> p g o j", o=2)[:, 8 * (i // 2):8 * (i // 2) + 8, i % 2, :],
                                bk(f"ys{i}")[:, :].rearrange("p (g j) -> p g j", g=8)).then_inc(dve_emptied, 1)
            for c in range(4):
                dve.wait_ge(*full(f"yd{c}"))
                by_r = lambda ap: ap.rearrange("p (j r) -> p r j", r=BT)
                STT(by_r(zT[:, c, :]), by_r(uT[:, c, :]), prm("d_skip", c),
                    bk(f"yd{c}")[:, :].rearrange("p (r j) -> p r j", r=BT),
                    ALU.mult, ALU.add).then_inc(dve_emptied, 1)
            dve.wait_ge(z_rounded, 1)
            TT(z_lo[:, :, :], zT[:, :, :], z_hi[:, :, :].bitcast(F32), ALU.subtract).then_inc(z_split, 1)
            for h in range(2):
                dve.wait_ge(gated_rounded, h + 1)
                v = slice(4 * h, 4 * h + 4)
                TT(gs_lo[:, v, :], gs[:, v, :], gs_hi[:, v, :].bitcast(F32), ALU.subtract).then_inc(gated_split, 1)
            for n in range(C_GB + 2, C_GLU + 2):
                split_chunk_t(n)
            for c in range(4):
                dve.wait_ge(*emptied(f"z{c}"))
                step(TT(zg[:, c, :], zg[:, c, :], zT[:, c, :], ALU.mult))
                step(dve.tensor_copy(zg_hi[:, c, :], zg[:, c, :]))
                TT(zg_lo[:, c, :], zg[:, c, :], zg_hi[:, c, :].bitcast(F32), ALU.subtract).then_inc(zg_split, 1)
            split_chunk_t(C_GLU + 2)
            for k in range(KD):
                dve.wait_ge(*full(f"yb{k}"))
                TT(mg[:, k, :], bk(f"yb{k}")[:, :], sigb[:, k, :], ALU.mult).then_inc(dve_emptied, 1)
                if k % 2:
                    split_chunk_t(C_BRET + k // 2 + 2)

            def split_merged(k):
                dve.wait_ge(mg_rounded, k + 1)
                TT(mg_lo[:, k, :], mg[:, k, :], mg_hi[:, k, :].bitcast(F32), ALU.subtract).then_inc(mg_split, 1)

            for k in range(KD):
                dve.wait_ge(*full(f"ya{k}"))
                step(TT(siga[:, k, :], bk(f"ya{k}")[:, :], siga[:, k, :], ALU.mult))
                TT(mg[:, k, :], mg[:, k, :], siga[:, k, :], ALU.add).then_inc(dve_emptied, 1)
                if k:
                    split_merged(k - 1)
                if k % 4 == 3:
                    split_chunk_t(C_BS5 + k // 4 + 2)
            split_merged(KD - 1)
            for i in range(NT):
                dve.wait_ge(x_in2[i], 16)
            for n in range(8):
                c, m = n // 2, n % 2
                dve.wait_ge(*full(f"wo{n}"))
                dst = x2[:, 2 * m:2 * m + 2, c * CW:(c + 1) * CW]
                TT(dst, bk(f"wo{n}")[:, :].rearrange("p (a n) -> p a n", a=2), dst,
                   ALU.add).then_inc(dve_emptied, 1)
                if n in (1, 3):
                    split_chunk_t(C_OUT + n // 2 + 2)
            dve.wait_ge(gf_in, 16)
            for i in range(NT):
                dve.wait_ge(rstd_ready, NT + i + 1)
                STT(h2[:, i, :], x2[:, i, :], rs[:, i:i + 1], gvec[:, :], ALU.mult, ALU.mult)\
                    .then_inc(h2_ready, 1)

            dve.wait_ge(*full("lg0"))
            TT(lg[:, :, :], bk("lg0")[:, 0:NT * E].rearrange("p (i e) -> p i e", i=NT),
               prm("router_b").unsqueeze(1).to_broadcast([P, NT, E]), ALU.add).then_inc(dve_emptied, 1)
            dve.wait_ge(*emptied("lg0"))
            for i in range(NT):
                step(dve.max(top_v[:, i, :], lg[:, i, :]))
            for i in range(NT):
                last = dve.max_index(top_i[:, i, :], top_v[:, i, :], lg[:, i, :])
            step(last)
            TS(negm[:, :], top_v[:, :, 0], -1.0, None, ALU.mult).then_inc(top_ready, 1)
            step(dve.tensor_copy(top_f[:, :, :], top_i[:, :, :]))
            topb = top_f[:, :, 0:TOPK].unsqueeze(3).to_broadcast([P, NT, TOPK, E])
            eid = con("expert_id").unsqueeze(1).unsqueeze(1).to_broadcast([P, NT, TOPK, E])
            step(TT(oneh[:, :, :, :], topb, eid, ALU.is_equal))
            over_k = lambda ap: ap.rearrange("p i k e -> p i e k")
            dve.tensor_reduce(hot[:, :, :], over_k(oneh[:, :, :, :]), AX.X, ALU.add).then_inc(hot_ready, 1)
            dve.tensor_copy(aid[:, :], con("assign_id"))
            dve.wait_ge(*full("rk0"))
            dve.tensor_copy(n_of, bk("rk0")[:, NT * E:(NT + 1) * E])
            dve.tensor_copy(cum[:, :, :], bk("rk0")[:, 0:NT * E].rearrange("p (i e) -> p i e", i=NT))\
                .then_inc(dve_emptied, 1)
            dve.wait_ge(*emptied("rk0"))
            step(TS(n_blocks, n_of, float(P), 1.0, ALU.is_gt, ALU.add))
            for k in range(2, NT):
                step(STT(n_blocks, n_of, float(k * P), n_blocks, ALU.is_gt, ALU.add))
            src, dst, d = n_blocks, end_a, 1
            while d < E:
                dve.tensor_copy(dst[:, 0:d], src[:, 0:d])
                step(TT(dst[:, d:E], src[:, d:E], src[:, 0:E - d], ALU.add))
                src, dst, d = dst, (end_b if dst is end_a else end_a), 2 * d
            ends = src
            step(TT(first, ends, n_blocks, ALU.subtract))
            step(STT(cum[:, :, :], first.unsqueeze(1).to_broadcast([P, NT, E]), float(P), cum[:, :, :],
                     ALU.mult, ALU.add))
            step(TT(wrk[:, :, :, :], oneh[:, :, :, :],
                    cum[:, :, :].unsqueeze(2).to_broadcast([P, NT, TOPK, E]), ALU.mult))
            step(dve.tensor_reduce(rank[:, :], wrk[:, :, :, :].rearrange("p i k e -> p (i k) e"), AX.X, ALU.add))
            dve.tensor_copy(dest[:, :], rank[:, :]).then_inc(dest_ready, 1)
            step(TT(ended, ends[0:1, :].unsqueeze(1).to_broadcast([1, N_ITEMS + 1, E]),
                    con("item_id")[0:1, :].unsqueeze(2).to_broadcast([1, N_ITEMS + 1, E]), ALU.is_le))
            dve.tensor_copy(item_f[:, N_ITEMS + 1:N_ITEMS + 2], ends[0:1, E - 1:E])
            step(dve.tensor_reduce(item_f[:, 0:N_ITEMS + 1], ended, AX.X, ALU.add))
            step(TS(item_f[:, 0:N_ITEMS + 1], item_f[:, 0:N_ITEMS + 1], float(E - 1), None, ALU.min))
            dve.tensor_copy(item_e[:, :], item_f[:, :])
            dve.wait_ge(gate_exp, NT)
            step(dve.reciprocal(gsum[:, NT:2 * NT], gsum[:, 0:NT]))
            step(TT(gate[:, :, :], gate[:, :, :], bc(gsum[:, NT:2 * NT], TOPK), ALU.mult))
            step(TT(wrk[:, :, :, :], oneh[:, :, :, :],
                    gate[:, :, :].unsqueeze(3).to_broadcast([P, NT, TOPK, E]), ALU.mult))
            dve.tensor_reduce(gte[:, :, :], over_k(wrk[:, :, :, :]), AX.X, ALU.add).then_inc(gte_ready, 1)
            dve.wait_ge(*full("gT0"))
            dve.tensor_copy(gTs[:, :], bk("gT0")[0:E, :]).then_inc(dve_emptied, 1)
            for n in range(8):
                i, m = n // 2, n % 2
                dve.wait_ge(*full(f"b2{n}"))
                dst = x2[:, i, m * 512:(m + 1) * 512]
                TT(dst, bk(f"b2{n}")[:, :], dst, ALU.add).then_inc(dve_emptied, 1)
            dve.wait_ge(b1_in, 32)
            dve.wait_ge(h2_out, 16 * NT)
            step(dve.tensor_copy(b1_hl, b1_raw))
            TT(b1_hl[E:2 * E, :], b1_raw[E:2 * E, :], b1_hl[E:2 * E, :].bitcast(F32), ALU.subtract)\
                .then_inc(b1_ready, 1)

            def split_chunk(i, c):
                dve.wait_ge(w_rounded, i * EC + (c + 1))
                slot = item_chunk(i, c)[0]
                TT(w_lo[slot], ring[:, slot, :], w_hi[c % N_HI].bitcast(F32), ALU.subtract).then_inc(w_split, 1)

            for c in range(AHEAD - 1):
                split_chunk(0, c)
            dve.wait_ge(slots_in, 16)
            dve.tensor_copy(tabf[:, :], tabi[:, :]).then_inc(tabf_ready, 1)
            dve.wait_ge(*full("tb0"))
            step(dve.tensor_copy(put_i[:, :], bk("tb0")[:, 0:N_ITEMS + 1]))
            TS(get_i[:, :], put_i[:, :], 2, None, ALU.arith_shift_right).then_inc(dve_emptied, 1)
            dve.wait_ge(*emptied("tb0"))
            dve.sem_inc(tab_ready, 1)
            dve.sem_inc(gu_empty, 2)

            def split_rows(i):
                for h in range(2):
                    dve.wait_ge(x_rounded, i * 2 + (h + 1))
                    hi, lo = (v[:, 4 * h:4 * h + 4, :].rearrange("p k t -> p (k t)") for v in (x_hi, x_lo))
                    TT(lo, bank[4 + h][:, :], hi.bitcast(F32), ALU.subtract).then_inc(x_split, 1)

            def split_tile(i, j):
                dve.wait_ge(a_rounded, i * FT + (j + 1))
                TT(a_lo[:, j, :], bank[2 + j % 2][:, 0:P], a_hi[:, j, :].bitcast(F32),
                   ALU.subtract).then_inc(a_split, 1)

            def pick_bias(i):
                e = dve.value_load(item_e[0:1, bass.ds(i, 1)], min_val=0, max_val=E - 1)
                dve.tensor_copy(pick, con("pick")[:, bass.ds(e, 1)].to_broadcast([P, P])).then_inc(pick_ready, 1)

            def item(i):
                for s in range(EC):
                    if 1 <= s <= FT:
                        j = s - 1
                        b = j % 2
                        dve.wait_ge(gu_full, i * FT + (j + 1))
                        if j >= 2:
                            dve.wait_ge(act_ready, i * FT + (j - 1))
                        TS(g_t[:, b, :], bank[b][:, 0:P], LIMIT, None, ALU.min).then_inc(glu_ready, 1)
                        TS(l_t[:, b, :], bank[b][:, P:2 * P], LIMIT, -LIMIT, ALU.min, ALU.max)\
                            .then_inc(gu_empty, 1)
                        if j > 0:
                            split_tile(i, j - 1)
                        dve.wait_ge(sg_ready, i * FT + (j + 1))
                        TT(gs_t[:, b, :], g_t[:, b, :], sg_t[:, b, :], ALU.mult).then_inc(gs_ready, 1)
                        dve.wait_ge(gs_ready, i * FT + (j + 1))
                        STT(a_t[:, b, :], l_t[:, b, :], 1.0, gs_t[:, b, :], ALU.add, ALU.mult)\
                            .then_inc(act_ready, 1)
                    if s == FT:
                        pick_bias(i + 1)
                        split_rows(i + 1)
                        split_tile(i, FT - 1)
                    c = s + AHEAD - 1
                    if c % EC not in POOL_SPLITS:
                        split_chunk(*((i, c) if c < EC else (i + 1, c - EC)))

            pick_bias(0)
            split_rows(0)
            n = dve.value_load(item_e[0:1, N_ITEMS + 1:N_ITEMS + 2], min_val=E, max_val=N_ITEMS)
            with dve.Fori(0, E) as i:
                item(i)
            with dve.If(n > E):
                with dve.Fori(E, N_ITEMS) as i:
                    with dve.If(i < n):
                        item(i)
                    dve.nop()
            dve.nop()

            for i in range(NT):
                dve.wait_ge(yk_in[i % 2], 16 * (i // 2 + 1))
                for k in range(TOPK):
                    last = STT(x2[:, i, :], yk[i % 2][:, k, :], gate[:, i, k:k + 1], x2[:, i, :],
                               ALU.mult, ALU.add)
                    if k < TOPK - 1:
                        step(last)
                last.then_inc(summed, 1)
            dve.wait_ge(gfin_in, 16)
            for i in range(NT):
                dve.wait_ge(frstd, i + 1)
                STT(x2[:, i, :], x2[:, i, :], rs[:, i:i + 1], gvec[:, :], ALU.mult, ALU.mult)\
                    .then_inc(fin_ready, 1)

        @block.tensor
        def _(pe):
            MM, TR = pe.matmul, pe.transpose

            def start(name):
                n = JOB[name]
                if n >= 8:
                    e, v = EMPTIED[n - 8]
                    pe.wait_ge(EMPT[e], v)
                return bank[n % 8]

            def chunk(n, k=KD):
                pe.wait_ge(t_split, n + 1)
                return [w.rearrange("p (k n) -> p k n", k=k) for w in (t_hi[n % 2], w_lo[t_slot(n)])]

            def channel_major(name, c0, rhs, k_tiles, first):
                r_hi, r_lo = rhs
                per = CH // k_tiles // P
                for m in range(sum(1 for j, _ in JOBS if j.rstrip("0123456789") == name)):
                    if m % per == 0:
                        w_h, w_l = chunk(c0 + m // per, k_tiles)
                    b = start(f"{name}{m}")
                    cols = slice((m % per) * P, (m % per + 1) * P)
                    for k in range(k_tiles):
                        if m == 0 and first:
                            pe.wait_ge(*first(k))
                        for n, (w, r) in enumerate(((w_h, r_hi), (w_h, r_lo), (w_l, r_hi))):
                            last = MM(b[:, :], w[:, k, cols], r[:, k, :], start=(k == 0 and n == 0),
                                      stop=(k == k_tiles - 1 and n == 2))
                    last.then_inc(bank_full, 1)

            def token_major(name, c0, lhs, first):
                l_hi, l_lo = lhs
                for c in range(4):
                    w_h, w_l = chunk(c0 + c)
                    for m in range(2):
                        b = start(f"{name}{2 * c + m}")
                        for a in range(2):
                            i = 2 * m + a
                            for k in range(KD):
                                if first and c == 0 and i == 0:
                                    pe.wait_ge(*first(k))
                                for n, (h, w) in enumerate(((l_hi, w_h), (l_hi, w_l), (l_lo, w_h))):
                                    last = MM(b[:, a * CW:(a + 1) * CW], h[:, k, i * P:(i + 1) * P], w[:, k, :],
                                              start=(k == 0 and n == 0), stop=(k == KD - 1 and n == 2))
                        last.then_inc(bank_full, 1)

            hT = (h_hi, h_lo)
            pe.wait_ge(cst_in, 16)
            b = [start(f"xT{k}") for k in range(KD)]
            for i in range(NT):
                pe.wait_ge(xn_ready, i + 1)
                for k in range(KD):
                    last = TR(b[k][:, i * P:(i + 1) * P], xn[:, i, k * P:(k + 1) * P], ident)
                    if i == NT - 1:
                        last.then_inc(bank_full, 1)
            channel_major("u", C_U, hT, KD, lambda k: emptied(f"xT{k}"))
            pe.wait_ge(*emptied("u3"))
            for r in range(BT):
                b = start(f"ua{r}")
                for c in range(4):
                    last = TR(b[0:NB, c * P:(c + 1) * P], uT[:, c, r:SEQ:BT], ident)
                last.then_inc(bank_full, 1)
            pe.wait_ge(*emptied("ua7"))
            for i in range(4):
                b = start(f"ub{i}")
                for g in range(8):
                    last = TR(b[:, g * NB:(g + 1) * NB],
                              ujr[0:NB, 8 * i + g, :, :].rearrange("p r c -> p (r c)"), ident[0:NB, 0:NB])
                last.then_inc(bank_full, 1)
            channel_major("q", C_Q, hT, KD, None)
            channel_major("k", C_K, hT, KD, None)
            pe.wait_ge(pb_ready, 1)
            for i in range(8):
                b = start(f"hT{i}")
                src = (pbr, pbi)[i // 4]
                for g in range(4):
                    last = TR(b[:, g * P:(g + 1) * P],
                              src[:, 4 * (i % 4) + g, :, :].rearrange("p m c -> p (m c)"), ident)
                last.then_inc(bank_full, 1)
            pe.wait_ge(neg_c, 1)
            for odd in range(2):
                b = start(f"kb{odd}")
                p0 = NS * odd
                for gp in range(GP):
                    for s, (w, c) in enumerate(((pbr, s5in[:, 2, :]), (pbi, s5in[:, 1, :]))):
                        last = MM(b[:, gp * GRP:(gp + 1) * GRP],
                                  w[p0:p0 + NS, gp, :, :].rearrange("p m c -> p (m c)"),
                                  c[p0:p0 + NS, gp * GRP:(gp + 1) * GRP], start=(s == 0), stop=(s == 1))
                last.then_inc(bank_full, 1)
            pe.wait_ge(*emptied("hT7"))
            pe.wait_ge(*emptied("ub3"))
            for i in range(4):
                b = start(f"xs{i}")
                w = (hTr, hTi)[i // 2]
                for g in range(16):
                    gg = 16 * (i % 2) + g
                    p0 = NS * (gg % 2)
                    last = MM(b[p0:p0 + NS, (g // 2) * NB:(g // 2 + 1) * NB], w[:, gg // 2, p0:p0 + NS],
                              ub[:, gg, :], start=True, stop=True)
                last.then_inc(bank_full, 1)
            token_major("v", C_V, hT, None)
            pe.wait_ge(*emptied("k3"))
            pe.wait_ge(*emptied("v7"))
            for h in range(HEADS):
                for j in range(NT):
                    b = start(f"sc{4 * h + j}")
                    MM(b[:, 0:SEQ - j * P], kT[:, h, j * P:(j + 1) * P], qT[:, h, j * P:SEQ],
                       start=True, stop=True).then_inc(bank_full, 1)
                for m in range(2):
                    b = start(f"in{2 * h + m}")
                    for a in range(2):
                        i = 2 * m + a
                        for j in range(i + 1):
                            pe.wait_ge(*emptied(f"sc{4 * h + j}"))
                            last = MM(b[:, a * DV:(a + 1) * DV], sT[:, j, (i - j) * P:(i - j + 1) * P],
                                      vt[:, j, h * DV:(h + 1) * DV], start=(j == 0), stop=(j == i))
                    last.then_inc(bank_full, 1)
            channel_major("g", C_G, hT, KD, None)
            pe.wait_ge(*emptied("in7"))
            for k in range(KD):
                b = start(f"rT{k}")
                for i in range(NT):
                    last = TR(b[:, i * P:(i + 1) * P], ret[:, i, k * P:(k + 1) * P], ident)
                last.then_inc(bank_full, 1)
            channel_major("ga", C_GA, hT, KD, None)
            pe.wait_ge(m0_ready, 1)
            pe.wait_ge(g_ready, 1)
            pe.wait_ge(scan_done, 1)
            for i in range(4):
                b = start(f"ys{i}")
                for g in range(8):
                    gg = 2 * (8 * (i // 2) + g) + i % 2
                    p0, gp, col = NS * (gg % 2), gg // 2, g * NB
                    MM(b[:, col:col + NB], m0T[:, gg, :], ub[:, gg, :],
                       start=True, stop=False)
                    MM(b[:, col + 1:col + NB], gre[p0:p0 + NS, gp, :, :].rearrange("p m c -> p (m c)"),
                       xr[p0:p0 + NS, gp, 0:NB - 1], start=False, stop=False)
                    last = MM(b[:, col + 1:col + NB], gim[p0:p0 + NS, gp, :, :].rearrange("p m c -> p (m c)"),
                              xi[p0:p0 + NS, gp, 0:NB - 1], start=False, stop=True)
                last.then_inc(bank_full, 1)
            for i in range(8):
                if i % 4 == 0:
                    pe.wait_ge(*emptied(f"ys{i // 2 + 1}"))
                b = start(f"yc{i}")
                for g in range(4):
                    last = TR(b[0:NB, g * P:(g + 1) * P], ysb[:, 4 * i + g, :], ident)
                last.then_inc(bank_full, 1)
            for c in range(4):
                pe.wait_ge(*emptied(f"yc{2 * c + 1}"))
                b = start(f"yd{c}")
                for r in range(BT):
                    last = TR(b[:, r * NB:(r + 1) * NB], yjr[0:NB, r, c * P:(c + 1) * P], ident[0:NB, 0:NB])
                last.then_inc(bank_full, 1)
            channel_major("gb", C_GB, hT, KD, None)
            pe.wait_ge(z_split, 1)
            channel_major("z", C_GLU, (z_hi, z_lo), 4, None)
            pe.wait_ge(gated_split, 2)
            channel_major("yb", C_BRET, (gs_hi, gs_lo), KD, None)
            channel_major("ya", C_BS5, (zg_hi, zg_lo), 4, lambda k: (zg_split, k + 1))
            token_major("wo", C_OUT, (mg_hi, mg_lo), lambda k: (mg_split, k + 1))
            b = [start(f"h2T{k}") for k in range(KD)]
            for i in range(NT):
                pe.wait_ge(h2_ready, i + 1)
                for k in range(KD):
                    last = TR(b[k][:, i * P:(i + 1) * P], h2[:, i, k * P:(k + 1) * P], ident)
                    if i == NT - 1:
                        last.then_inc(bank_full, 1)
            pe.wait_ge(moe_in, 32)
            pe.wait_ge(*emptied("h2T7"))
            b = start("lg0")
            for i in range(NT):
                for k in range(KD):
                    last = MM(b[:, i * E:(i + 1) * E], h2T[:, k, i * P:(i + 1) * P], rw_s[:, k, :],
                              start=(k == 0), stop=(k == KD - 1))
            last.then_inc(bank_full, 1)
            pe.wait_ge(hot_ready, 1)
            b = start("rk0")
            for i in range(NT + 1):
                for j in range(min(i, NT)):
                    last = MM(b[:, i * E:(i + 1) * E], ones, hot[:, j, :], start=(j == 0),
                              stop=(j == NT - 1))
                if i < NT:
                    last = MM(b[:, i * E:(i + 1) * E], con("before"), hot[:, i, :], start=(i == 0), stop=True)
            last.then_inc(bank_full, 1)
            pe.wait_ge(gte_ready, 1)
            b = start("gT0")
            for i in range(NT):
                last = TR(b[0:E, i * P:(i + 1) * P], gte[:, i, :], ident)
            last.then_inc(bank_full, 1)
            pe.wait_ge(*emptied("gT0"))
            for n in range(8):
                b = start(f"b2{n}")
                MM(b[:, :], gTs[:, (n // 2) * P:(n // 2 + 1) * P], b2_s[:, (n % 2) * 512:(n % 2 + 1) * 512],
                   start=True, stop=True).then_inc(bank_full, 1)
            pe.wait_ge(tabf_ready, 1)
            b = start("tb0")
            TR(b[:, 0:N_ITEMS + 1], tabf[:, :], ident[0:N_ITEMS + 1, 0:N_ITEMS + 1]).then_inc(bank_full, 1)

            pe.wait_ge(tab_ready, 1)
            pe.wait_ge(b1_ready, 1)
            pe.sem_inc(y_full, W2C)

            def rows(moves):
                pe.wait_ge(moved, moves)
                for h in range(2):
                    for k in range(4):
                        last = TR(bank[4 + h][:, k * P:(k + 1) * P], xe[:, (4 * h + k) * P:(4 * h + k + 1) * P], ident)
                    last.then_inc(x_full, 1)

            def products(dst, hi, lo, slot, c, k_tiles, ready=None, started=False):
                w_l = w_lo[slot].rearrange("p (k n) -> p k n", k=k_tiles)
                w_h = w_hi[c % N_HI].rearrange("p (k n) -> p k n", k=k_tiles)
                for k in range(k_tiles):
                    if ready and ready(k):
                        pe.wait_ge(*ready(k))
                    for n, (a, w) in enumerate(((hi, w_h), (hi, w_l), (lo, w_h))):
                        last = MM(dst, a[:, k, :], w[:, k, :], start=(k == 0 and n == 0 and not started),
                                  stop=(k == k_tiles - 1 and n == 2))
                return last

            def transpose_tile(i, j):
                pe.wait_ge(act_ready, i * FT + (j + 1))
                if j >= 2:
                    pe.wait_ge(a_split, i * FT + (j - 1))
                TR(bank[2 + j % 2][:, 0:P], a_t[:, j % 2, :], ident).then_inc(a_full, 1)

            def item(i):
                for j in range(FT):
                    if j == 0:
                        pe.wait_ge(pick_ready, i + 1)
                    pe.wait_ge(gu_empty, i * FT + (j + 1))
                    dst = bank[j % 2][:, 0:CW]
                    MM(dst, pick, b1_hl[:, j * CW:(j + 1) * CW], start=True, stop=False)
                    if j == 0:
                        pe.wait_ge(x_split, i * 2 + 2)
                    pe.wait_ge(*split(i, j))
                    products(dst, x_hi, x_lo, item_chunk(i, j)[0], j, KD, started=True).then_inc(gu_full, 1)
                    if j > 0:
                        transpose_tile(i, j - 1)
                rows(i * 32 + 32)
                transpose_tile(i, FT - 1)
                for c in range(W2C):
                    pe.wait_ge(*split(i, FT + c))
                    pe.wait_ge(y_empty, i * W2C + (c + 1))
                    ready = lambda k: (a_split, i * FT + (k + 1)) if c == 0 and k in (0, FT - 2, FT - 1) else None
                    products(bank[6 + c % 2][:, 0:CW], a_hi, a_lo, item_chunk(i, FT + c)[0], FT + c, FT,
                             ready).then_inc(y_full, 1)

            rows(16)
            n = pe.value_load(item_e[0:1, N_ITEMS + 1:N_ITEMS + 2], min_val=E, max_val=N_ITEMS)
            with pe.Fori(0, E) as i:
                item(i)
            with pe.If(n > E):
                with pe.Fori(E, N_ITEMS) as i:
                    with pe.If(i < n):
                        item(i)
                    pe.nop()
            pe.nop()


_INPUTS = ("x", "pos", "wt", "we", "par", "s5bc", "b1", "b2", "rw", "g_ffn", "g_fin", "cst", "dmask", "fill")


def _constants():
    i = np.arange(P)
    c = {
        "ident": np.eye(P), "before": (i[:, None] < i[None, :]), "ones": np.ones((P, P)),
        "expert_id": np.broadcast_to(np.arange(E), (P, E)),
        "item_id": np.broadcast_to(np.arange(N_ITEMS + 1), (P, N_ITEMS + 1)),
        "pick": (i[:, None] % E == np.arange(E)) & (i[:, None] < 2 * E),
        "assign_id": np.concatenate([TOPK * (t * P + i)[:, None] + np.arange(TOPK) for t in range(NT)], 1),
        "inv_freq": (np.float32(10000.0) ** (-(i % (DK // 2)).astype(np.float32) / np.float32(DK // 2)))[:, None],
        "sin_sign": np.where(i < DK // 2, -1.0, 1.0)[:, None],
    }
    cst = np.concatenate([np.asarray(c[n], np.float32) for n in CST], 1)
    lag = np.arange(SEQ)[None, :] - i[:, None]
    dm = [np.where(lag >= 0, (1.0 - 2.0 ** (-5.0 - h)) ** np.maximum(lag, 0), 0.0) for h in range(HEADS)]
    fill = np.full((N_ITEMS + 1, P), NO_SLOT, np.int32)
    return np.ascontiguousarray(cst), np.stack(dm, 1).astype(np.float32), fill


def kernel(x, positions, norm_mix_g, w_in, s5_lambda_re, s5_lambda_im, s5_log_dt, s5_b_re, s5_b_im,
           s5_c_re, s5_c_im, s5_d, s5_w_glu, s5_b_glu, ret_gn_g, w_branch_s5, w_branch_ret, w_out,
           norm_ffn_g, router_w, router_b, expert_w1, expert_b1, expert_w2, expert_b2, norm_final_g):
    import concourse.bacc as bacc
    from concourse.bass_utils import run_bass_kernel_spmd

    f = np.asarray

    def chunks(w):
        w = f(w)
        k = w.shape[0] // P
        return w.reshape(k, P, -1, CH // k).transpose(2, 1, 0, 3).reshape(-1, P, CH)

    def cols(v):
        return f(v).reshape(-1, P).T

    def states(v):
        v = f(v).reshape(GP, 2 * NS, -1)
        return v.transpose(1, 0, 2).reshape(P, -1)

    cst, dmask, fill = _constants()
    w1 = f(expert_w1)[0].reshape(E, KD, P, FT, P, 2).transpose(0, 3, 2, 1, 5, 4).reshape(E, FT, P, CH)
    w2 = f(expert_w2)[0].reshape(E, FT, P, W2C, CW).transpose(0, 3, 2, 1, 4).reshape(E, W2C, P, CH)
    par = {
        "norm_mix": cols(norm_mix_g[0]), "ret_gn": cols(ret_gn_g[0]), "d_skip": cols(s5_d[0]),
        "b_glu": cols(s5_b_glu[0]), "lam_re": states(s5_lambda_re[0]), "lam_im": states(s5_lambda_im[0]),
        "log_dt": states(np.broadcast_to(f(s5_log_dt)[0][:, None], (NG, NS))),
        "router_b": np.broadcast_to(f(router_b)[0][None, :], (P, E)),
    }
    arrays = {
        "x": f(x)[0], "pos": f(positions), "we": np.concatenate([w1, w2], 1),
        "wt": np.concatenate([chunks(w[0]) for w in (w_in, s5_w_glu, w_branch_ret, w_branch_s5, w_out)]),
        "s5bc": np.concatenate([states(f(v)) for v in (s5_b_re[0], s5_b_im[0], f(s5_c_re)[0].transpose(0, 2, 1),
                                                        f(s5_c_im)[0].transpose(0, 2, 1))], 1),
        "par": np.concatenate([par[n] for n in PAR], 1),
        "b1": f(expert_b1)[0].reshape(E, FT, P, 2).transpose(0, 1, 3, 2).reshape(E, 2 * DFF),
        "b2": f(expert_b2)[0], "rw": f(router_w)[0].reshape(KD, P, E).transpose(1, 0, 2),
        "g_ffn": f(norm_ffn_g), "g_fin": f(norm_final_g)[None, :], "cst": cst, "dmask": dmask, "fill": fill,
    }
    nc = bacc.Bacc("TRN2", target_bir_lowering=False, num_devices=1)
    ins, aps = {}, []
    for n in _INPUTS:
        a = np.ascontiguousarray(arrays[n])
        ins[n] = a
        aps.append(nc.dram_tensor(n, a.shape, mybir.dt.from_np(a.dtype), kind="ExternalInput").ap())
    out = nc.dram_tensor("out", (SEQ, D), F32, kind="ExternalOutput").ap()
    build(nc, *aps, out)
    r = run_bass_kernel_spmd(nc, [ins], core_ids=[0])
    return f(r.results[0]["out"]).reshape(1, SEQ, D)
```

```python
from contextlib import ExitStack

import numpy as np

import concourse.bass as bass
from concourse import mybir

F32 = mybir.dt.float32
BF16 = mybir.dt.bfloat16
F32R = mybir.dt.float32r
I32 = mybir.dt.int32
U32 = mybir.dt.uint32
ALU = mybir.AluOpType
ACT = mybir.ActivationFunctionType
AX = mybir.AxisListType

P = 128
D = 1024
SEQ = 512
NT = SEQ // P
KD = D // P
S5W = 512
GRP = 16
NG = S5W // GRP
NS = 64
GP = NG // 2
BT = P // GRP
NB = SEQ // BT
HEADS, DK, DV = 4, 128, 256
E, TOPK, DFF = 32, 4, 1024
FT = DFF // P
NA = SEQ * TOPK
EPS = 1e-5
LIMIT, SIG_ALPHA = 7.0, 1.702

CH = 2048
CW = CH // KD
C_U, C_Q, C_K, C_V, C_G, C_GA, C_GB = 0, 2, 4, 6, 10, 14, 18
C_GLU, C_BRET, C_BS5, C_OUT = 22, 23, 27, 29
N_TRUNK = 33
RING = 12
T_SLOTS = (0, 1, 5)
T_HI = (2, 3)
EXPERT_0 = 4
W2C = 4
EC = FT + W2C
N_ITEMS = E + NA // P
AHEAD = 3
N_HI = 4
POOL_SPLITS = (3, 6, 9)
ID_LO = 16
NO_SLOT = 1 << 13

PAR = {}
_at = 0
for _n, _w in (("norm_mix", KD), ("ret_gn", KD), ("d_skip", S5W // P), ("b_glu", S5W // P),
               ("lam_re", GP), ("lam_im", GP), ("log_dt", GP), ("router_b", E)):
    PAR[_n] = (_at, _w)
    _at += _w
N_PAR = _at
CST = {}
_at = 0
for _n, _w in (("ident", P), ("before", P), ("ones", P), ("expert_id", E), ("item_id", N_ITEMS + 1), ("pick", E),
               ("row", 1), ("slot_id", P), ("id_hi", NT * TOPK), ("id_lo", NT * TOPK),
               ("inv_freq", 1), ("sin_sign", 1)):
    CST[_n] = (_at, _w)
    _at += _w
N_CST = _at

TWO_PI = 2 * np.pi
PI_1 = 6.28125
PI_2 = float(np.float32(int((TWO_PI - PI_1) * 2 ** 21) / 2 ** 21))
PI_3 = float(np.float32(TWO_PI - PI_1 - PI_2))
PI_IN = 3.1415925
ROUND = 1.5 * 2 ** 23

JOBS = []


def _jobs(name, n, engine):
    JOBS.extend((f"{name}{i}", engine) for i in range(n))


_jobs("xT", KD, "V")
_jobs("u", 4, "A")
_jobs("ua", BT, "A")
_jobs("ub", 4, "V")
_jobs("q", HEADS, "V")
_jobs("k", HEADS, "V")
_jobs("hT", 8, "A")
_jobs("kb", 2, "V")
_jobs("xs", 4, "V")
for _h in range(HEADS):
    JOBS.extend([(f"v{2 * _h}", "A"), (f"v{2 * _h + 1}", "A")])
    if _h:
        JOBS.extend((f"in{2 * _h - 2 + j}", "V") for j in range(2))
    JOBS.extend((f"sc{4 * _h + j}", "V") for j in range(4))
JOBS.extend([("g0", "A"), ("g1", "A"), ("in6", "V"), ("in7", "V")])
JOBS.extend((f"g{_i}", "A") for _i in range(2, KD))
_jobs("rT", KD, "V")
_jobs("ga", KD, "A")
_jobs("ys", 4, "V")
_jobs("yc", BT, "A")
_jobs("yd", 4, "V")
_jobs("gb", KD, "A")
_jobs("z", 4, "A")
_jobs("yb", KD, "V")
_jobs("ya", KD, "V")
_jobs("wo", 8, "V")
_jobs("h2T", KD, "A")
_jobs("lc", 1, "A")
_jobs("lg", 1, "V")
_jobs("rk", 1, "V")
_jobs("tb", 1, "V")
_jobs("gT", 1, "V")
_jobs("b2", 8, "V")
LAST_USE = [f"{name}{i}" for name, ids in (
    ("u", (1, 3)), ("q", (1, 3)), ("k", (1, 3)), ("v", (1, 3, 5, 7)), ("g", (1, 3, 5, 7)), ("ga", (1, 3, 5, 7)),
    ("gb", (1, 3, 5, 7)), ("z", (3,)), ("yb", (1, 3, 5, 7)), ("ya", (3, 7)), ("wo", (1, 3, 5, 7))) for i in ids]
JOB = {name: n for n, (name, _) in enumerate(JOBS)}
FIRST_LOADS = ((0, "z3"), (6, "z3"), (2, "yb7"), (3, "yb7"), (7, "ya7"), (8, "wo3"), (9, "wo5"), (11, "wo5"),
               (1, "wo7"), (4, "wo7"), (5, "wo7"), (10, "wo7"))
EMPTIED = []
_c = {"A": 0, "V": 0}
for _name, _e in JOBS:
    _c[_e] += 1
    EMPTIED.append((_e, _c[_e]))


def build(nc, x, pos, wt, we, par, s5bc, b1, b2, rw, g_ffn, g_fin, cst, dmask, out):
    h2_dram = nc.dram_tensor("h2_rows", (SEQ, D), F32).ap()
    y_dram = nc.dram_tensor("y_rows", (NA, D), F32).ap()

    with ExitStack() as ctx:
        place = {}

        def sb(name, shape, dt=F32):
            return ctx.enter_context(nc.sbuf_tensor(name, shape, dt))

        def large(name, floats):
            t = sb(name, [P, floats])
            place[name] = nc.sbuf_base - 4 * floats
            return t

        def rounded(name, where, start, *shape):
            return nc.alloc_sbuf_tensor_at(name, [P, *shape], F32R, offset=place[where] + 4 * start)

        def sem(name):
            return ctx.enter_context(nc.semaphore(name))

        bank = [ctx.enter_context(nc.psum_tensor(f"bank{i}", [P, 512], F32)) for i in range(8)]

        ring = large("ring", RING * CH)[:, :].rearrange("p (s n) -> p s n", s=RING)
        big = [large(f"big{i}", 4096) for i in range(6)]
        uT = sb("uT", [P, 4, SEQ])
        par_s = sb("par_s", [P, N_PAR])
        cst_s = sb("cst_s", [P, N_CST])

        def prm(name, i=None, n=1):
            a, w = PAR[name]
            return par_s[:, a:a + w] if i is None else par_s[:, a + i:a + i + n]

        def con(name):
            a, w = CST[name]
            return cst_s[:, a:a + w]

        ident, ones = con("ident"), con("ones")

        h_hi, h_lo = (rounded(f"h_{n}", f"big{b}", 0, KD, SEQ) for n, b in (("hi", 0), ("lo", 4)))
        t_hi = [rounded(f"t_hi{i}", "ring", i * CH, CH)[:, :] for i in T_HI]
        w_lo = [rounded(f"w_lo{i}", "ring", i * CH, CH)[:, :] for i in range(RING)]
        xn = big[1][:, :].rearrange("p (i d) -> p i d", i=NT)
        rot_a, rot_b = big[1][:, 0:512], big[1][:, 512:1024]
        vt = xn
        ret = vt
        siga = big[1][:, :].rearrange("p (k t) -> p k t", k=KD)
        pos_i = big[2][:, 0:512].bitcast(I32)
        qT = big[2][:, 0:2048].rearrange("p (h t) -> p h t", h=HEADS)
        kT = big[2][:, 2048:4096].rearrange("p (h t) -> p h t", h=HEADS)
        gs = big[2][:, :].rearrange("p (k t) -> p k t", k=KD)
        gs_hi, gs_lo = rounded("gs_hi", "ring", 6 * CH, KD, SEQ), rounded("gs_lo", "big2", 0, KD, SEQ)
        cosT, sinT = big[3][:, 0:SEQ], big[3][:, SEQ:2 * SEQ]
        rope_k = big[3][:, 1024:1536]
        sT = big[3][:, 0:2048].rearrange("p (j t) -> p j t", j=NT)
        decay = big[3][:, 2048:4096].rearrange("p (h t) -> p h t", h=HEADS)
        sigb = big[3][:, :].rearrange("p (k t) -> p k t", k=KD)
        mg = big[4][:, :].rearrange("p (k t) -> p k t", k=KD)
        mg_hi, mg_lo = rounded("mg_hi", "ring", 8 * CH, KD, SEQ), rounded("mg_lo", "big4", 0, KD, SEQ)
        x2 = big[0][:, :].rearrange("p (i d) -> p i d", i=NT)
        h2 = big[1][:, :].rearrange("p (i d) -> p i d", i=NT)
        h2T = big[2][:, :].rearrange("p (k t) -> p k t", k=KD)

        s5a = ring[:, 6:8, :].rearrange("p a b -> p (a b)")
        s5b = ring[:, 8:10, :].rearrange("p a b -> p (a b)")
        pbr = s5a[:, 0:2048].rearrange("p (g m c) -> p g m c", g=GP, m=BT)
        pbi = s5a[:, 2048:4096].rearrange("p (g m c) -> p g m c", g=GP, m=BT)
        gre, gim = pbr, pbi
        yjr = s5a.rearrange("p (r c) -> p r c", r=BT)
        hTr = s5b[:, 0:2048].rearrange("p (g n) -> p g n", g=GP)
        hTi = s5b[:, 2048:4096].rearrange("p (g n) -> p g n", g=GP)
        m0T = s5b.rearrange("p (g n) -> p g n", g=NG)
        m0r = big[5][:, :].rearrange("p (r n) -> p r n", r=BT)
        ub = ring[:, 10, :].rearrange("p (g j) -> p g j", g=NG)
        xr = ring[:, 11, 0:1024].rearrange("p (g j) -> p g j", g=GP)
        xi = ring[:, 11, 1024:2048].rearrange("p (g j) -> p g j", g=GP)
        ujr = big[5][:, :].rearrange("p (g r c) -> p g r c", g=NG, r=BT)
        sc1 = big[5][:, 0:1024].rearrange("p (g j) -> p g j", g=GP)
        sc2 = big[5][:, 1024:2048].rearrange("p (g j) -> p g j", g=GP)
        ysb = big[5][:, 2048:4096].rearrange("p (g j) -> p g j", g=NG)
        zT = big[5][:, 0:2048].rearrange("p (k t) -> p k t", k=4)
        zg = big[5][:, 2048:4096].rearrange("p (k t) -> p k t", k=4)
        z_hi, z_lo = (rounded(f"z_{n}", "ring", i * CH, 4, SEQ) for n, i in (("hi", 4), ("lo", 10)))
        zg_hi, zg_lo = rounded("zg_hi", "ring", 11 * CH, 4, SEQ), rounded("zg_lo", "big5", 2048, 4, SEQ)
        k7 = ring[:, 4, 0:512]
        s5in = ring[:, 4, 512:1536].rearrange("p (a n) -> p a n", a=4)
        s5p = ring[:, 4, 1536:1536 + 24 * GP].rearrange("p (a n) -> p a n", a=24)
        bb = sb("bb", [P, 2, GP * GRP])
        DT, TH, MAG, SIN, COS, AR, AI, NR, T1, T2, DEN, FR, FI, DEN_INV, COS_ANGLE, SIN_ANGLE, A8R, A8I, T3 = range(19)

        def pr(i):
            return s5p[:, i, :]


        xe, ye = big[1][:, 0:D], big[1][:, D:2 * D]
        b1_hl = rounded("b1_hl", "big1", 2048, 2 * DFF)[:, :]
        x_hi, x_lo = (rounded(f"x_{n}", "big2", i * D, KD, P) for i, n in enumerate(("hi", "lo")))
        b1_raw = big[2][:, 2048:4096]
        w_hi = [rounded(f"w_hi{i}", f"big{3 + i // 2}", (i % 2) * CH, CH)[:, :] for i in range(N_HI)]
        g_t, l_t, sg_t, gs_t = (big[5][:, 2 * i * P:2 * (i + 1) * P].rearrange("p (b t) -> p b t", b=2)
                                for i in range(4))
        a_t = big[5][:, 8 * P:11 * P].rearrange("p (b t) -> p b t", b=3)
        a_hi, a_lo = (rounded(f"a_{n}", "big5", (11 + i * FT) * P, FT, P) for i, n in enumerate(("hi", "lo")))
        pick = rounded("pick", "big5", (11 + 2 * FT) * P, P)[:, :]
        yk = [big[i][:, :].rearrange("p (k d) -> p k d", k=TOPK) for i in (1, 2, 3, 4)]
        flat_u = uT[:, :, :].rearrange("p c t -> p (c t)")
        gvec = flat_u[:, 0:D]
        b2_s = flat_u[0:E, D:2 * D]

        ss = sb("ss", [P, 4 * NT])
        stat = sb("stat", [P, NT, 8])
        mv = sb("mv", [P, NT, 4])
        rw_s = sb("rw_s", [P, KD, E])
        at = [0]

        def tmp_tile(rows, *shape):
            n = int(np.prod(shape))
            ap = big[5][0:rows, at[0]:at[0] + n]
            at[0] += n
            names = "abc"[:len(shape)]
            if len(shape) == 1:
                return ap
            return ap.rearrange(f"p ({' '.join(names)}) -> p {' '.join(names)}", **dict(zip(names, shape)))

        lg, cum, hot, gte = (tmp_tile(P, NT, E) for _ in range(4))
        lgT = tmp_tile(E, SEQ)
        before_sum = tmp_tile(P, NT + 1, E)
        oneh, wrk = (tmp_tile(P, NT, TOPK, E) for _ in range(2))
        n_of, n_blocks, end_a, end_b, first = (tmp_tile(P, E) for _ in range(5))
        slot_hi, slot_lo = tmp_tile(P, N_ITEMS + 1), tmp_tile(P, N_ITEMS + 1)
        ended, item_c = tmp_tile(N_ITEMS + 1, E), tmp_tile(N_ITEMS + 1, 1)
        place_i, place_t = (tmp_tile(P, 2, NA // P).bitcast(I32) for _ in range(2))
        place_f = tmp_tile(P, 2, NA // P)
        in_item = wrk.rearrange("p i k e -> p (i k e)")[:, 0:NA // P * (N_ITEMS + 1) // 2].bitcast(BF16)\
            .rearrange("p (a t) -> p a t", a=NA // P)
        spare = big[4][:, CH:2 * CH].bitcast(BF16)
        in_slot = spare[:, 0:NA].rearrange("p (a s) -> p a s", s=P)
        digits = spare[:, NA:NA + 2 * (NA // P) * (N_ITEMS + 1)].rearrange("p (a v t) -> p a v t", v=2, t=N_ITEMS + 1)
        gTs = big[5][0:E, 4096 - SEQ:4096]
        top_v = sb("top_v", [P, NT, 8])
        top_i = sb("top_i", [P, NT, 8], U32)
        top_f = sb("top_f", [P, NT, 8])
        gate = sb("gate", [P, NT, TOPK])
        negm = sb("negm", [P, NT])
        gsum = sb("gsum", [P, 2 * NT])
        rank = sb("rank", [P, NT * TOPK])
        item_f = sb("item_f", [1, N_ITEMS + 2])
        item_e = sb("item_e", [1, N_ITEMS + 2], I32)
        put_i = sb("put_i", [P, N_ITEMS + 1], I32)
        get_i = sb("get_i", [P, N_ITEMS + 1], I32)
        get_1, put_1 = sb("get_1", [P, 1], I32), sb("put_1", [P, 1], I32)

        landed = [sem(f"landed{i}") for i in range(RING)]
        bank_full = sem("bank_full")
        act_emptied, dve_emptied = sem("act_emptied"), sem("dve_emptied")
        act_chain, dve_chain, pool_chain = sem("act_chain"), sem("dve_chain"), sem("pool_chain")
        x_in, x_in2 = [sem(f"x_in{i}") for i in range(NT)], [sem(f"x_again{i}") for i in range(NT)]
        par_in, cst_in, pos_in, dec_in = sem("par_in"), sem("cst_in"), sem("pos_in"), sem("dec_in")
        moe_in, gf_in, gfin_in = sem("moe_in"), sem("gf_in"), sem("gfin_in")
        squares, rstd_ready, xn_ready = sem("squares"), sem("rstd_ready"), sem("xn_ready")
        h_rounded = sem("h_rounded")
        t_rounded, t_split = sem("t_rounded"), sem("t_split")
        z_rounded, z_split, zg_split = sem("z_rounded"), sem("z_split"), sem("zg_split")
        gated_rounded, gated_split = sem("gated_rounded"), sem("gated_split")
        mg_rounded, mg_split = sem("mg_rounded"), sem("mg_split")
        rope_act = sem("rope_act")
        s5_act, s5_pool = sem("s5_act"), sem("s5_pool")
        pb_ready, g_ready, scan_done = sem("pb_ready"), sem("g_ready"), sem("scan_done")
        m0_zero, m0_in, m0_ready = sem("m0_zero"), sem("m0_in"), sem("m0_ready")
        gn_var, gn_std = sem("gn_var"), sem("gn_std")
        h2_ready, h2_out = sem("h2_ready"), sem("h2_out")
        top_ready, gate_exp = sem("top_ready"), sem("gate_exp")
        hot_ready, gte_ready = sem("hot_ready"), sem("gte_ready")
        digits_ready = sem("digits_ready")
        moved = sem("moved")
        get_ready, put_ready = sem("get_ready"), sem("put_ready")
        index_seen = sem("index_seen")
        ye_free = sem("ye_free")
        xe_zero = sem("xe_zero")
        b1_zero, b1_in, b1_ready = sem("b1_zero"), sem("b1_in"), sem("b1_ready")
        pick_ready = sem("pick_ready")
        w_rounded, w_split, w_split_p = sem("w_rounded"), sem("w_split"), sem("w_split_p")
        x_full, x_rounded, x_split = sem("x_full"), sem("x_rounded"), sem("x_split")
        gu_full, gu_empty = sem("gu_full"), sem("gu_empty")
        glu_ready, sg_ready, gs_ready, act_ready = sem("glu_ready"), sem("sig_ready"), sem("gs_ready"), sem("act_ready")
        a_full, a_rounded, a_split = sem("a_full"), sem("a_rounded"), sem("a_split")
        y_full, y_empty = sem("y_full"), sem("y_empty")
        angles, den_ready, neg_c, tab_ready = sem("angles"), sem("den_ready"), sem("neg_c"), sem("tab_ready")
        yk_in = [sem(f"yk_in{i}") for i in range(2 * NT)]
        summed, fsq, frstd, fin_ready, out_done = sem("summed"), sem("fsq"), sem("frstd"), sem("fin_ready"), sem("out_done")

        EMPT = {"A": act_emptied, "V": dve_emptied}

        def full(name):
            return bank_full, JOB[name] + 1

        def emptied(name):
            e, n = EMPTIED[JOB[name]]
            return EMPT[e], n

        def t_slot(n):
            return T_SLOTS[n % len(T_SLOTS)]

        def used(i, c):
            return (gu_full, i * FT + (c + 1)) if c < FT else (y_full, i * W2C + (c - FT + 1 + W2C))

        def item_chunk(i, c):
            slot = (EXPERT_0 + c) % RING
            before = sum(1 for n in range(N_TRUNK) if t_slot(n) == slot)
            return slot, (landed[slot], i * 16 + 16 * (before + 1))

        def split(i, c):
            if c in POOL_SPLITS:
                return w_split_p, i * len(POOL_SPLITS) + (POOL_SPLITS.index(c) + 1)
            return w_split, i * (EC - len(POOL_SPLITS)) + (1 + sum(1 for n in range(c) if n not in POOL_SPLITS))

        def bk(name):
            return bank[JOB[name] % 8]

        def bc(ap, n):
            return ap.unsqueeze(2).to_broadcast([ap.shape[0], ap.shape[1], n])

        block = ctx.enter_context(nc.Block())

        @block.sync
        def _(sp):
            sp.dma_start(cst_s[:, :], cst).then_inc(cst_in, 16)
            sp.wait_ge(x_in[NT - 1], 16)
            for n in range(N_TRUNK):
                if n >= len(T_SLOTS):
                    sp.wait_ge(*full(LAST_USE[n - len(T_SLOTS)]))
                sp.dma_start(ring[:, t_slot(n), :], wt[n]).then_inc(landed[t_slot(n)], 16)
                if n == 1:
                    sp.dma_start(decay, dmask).then_inc(dec_in, 16)
            for c, last in FIRST_LOADS:
                sp.wait_ge(*full(last))
                slot = item_chunk(0, c)[0]
                sp.dma_start(ring[:, slot, :], we[0, c]).then_inc(landed[slot], 16)
            sp.wait_ge(tab_ready, 1)

            def load(i, chunks):
                e = sp.value_load(item_e[0:1, bass.ds(i, 1)], min_val=0, max_val=E - 1)
                for c in chunks:
                    slot = item_chunk(i, c)[0]
                    sp.wait_ge(*used(i - 1, c))
                    sp.dma_start(ring[:, slot, :], we[bass.ds(e, 1), c].rearrange("o p n -> (o p) n"))\
                        .then_inc(landed[slot], 16)

            def item(i):
                load(i, range(AHEAD, EC))
                load(i + 1, range(AHEAD))

            load(1, range(AHEAD))
            with sp.Fori(1, E) as i:
                item(i)
            n = sp.value_load(item_e[0:1, N_ITEMS + 1:N_ITEMS + 2], min_val=E, max_val=N_ITEMS)
            with sp.If(n > E):
                with sp.Fori(E, N_ITEMS) as i:
                    with sp.If(i < n):
                        item(i)
                    sp.nop()
            sp.nop()
            sp.wait_ge(y_full, n * W2C + W2C)
            sp.wait_ge(moved, n * 32 + 16)
            sp.wait_ge(w_rounded, n * EC + AHEAD)
            sp.wait_ge(w_split, n * (EC - len(POOL_SPLITS)) + (AHEAD - 1))
            y_rows = y_dram.rearrange("(i p k) d -> i p k d", i=NT, p=P)
            for i in range(NT):
                for h in range(2):
                    sp.dma_start(yk[i][:, 2 * h:2 * h + 2, :], y_rows[i, :, 2 * h:2 * h + 2, :])\
                        .then_inc(yk_in[2 * i + h], 16)
            for i in range(NT):
                sp.wait_ge(fin_ready, i + 1)
                sp.dma_start(out[i * P:(i + 1) * P, :], x2[:, i, :]).then_inc(out_done, 16)
            sp.wait_ge(out_done, 16 * NT)

        @block.gpsimd
        def _(pool):
            n_chain = [0]

            def step(ins):
                n_chain[0] += 1
                ins.then_inc(pool_chain, 1)
                pool.wait_ge(pool_chain, n_chain[0])

            TT = pool.tensor_tensor
            rs = ss[:, NT:2 * NT]
            mhalf = ss[:, 3 * NT:4 * NT]
            step(pool.memset(mhalf, -0.5))

            def row_rstd(i):
                step(pool.tensor_scalar(rs[:, i:i + 1], ss[:, i:i + 1], 1.0 / D, EPS, ALU.mult, ALU.add))
                return TT(rs[:, i:i + 1], rs[:, i:i + 1], mhalf[:, 0:1], ALU.pow)

            for i in range(NT):
                pool.wait_ge(squares, i + 1)
                row_rstd(i).then_inc(rstd_ready, 1)

            pool.wait_ge(par_in, 32)
            pool.wait_ge(s5_act, 1)
            step(TT(pr(T1), prm("lam_re"), pr(DT), ALU.mult))
            TT(pr(TH), prm("lam_im"), pr(DT), ALU.mult).then_inc(s5_pool, 1)
            pool.wait_ge(s5_act, 4)
            step(TT(pr(AR), pr(MAG), pr(COS), ALU.mult))
            step(TT(pr(AI), pr(MAG), pr(SIN), ALU.mult))
            step(pool.tensor_scalar(pr(NR), pr(AR), 1.0, -1.0, ALU.mult, ALU.add))
            step(TT(pr(T1), prm("lam_re"), prm("lam_re"), ALU.mult))
            step(TT(pr(T2), prm("lam_im"), prm("lam_im"), ALU.mult))
            TT(pr(DEN), pr(T1), pr(T2), ALU.add).then_inc(s5_pool, 1)
            pool.wait_ge(s5_pool, 2)
            step(TT(pr(T1), pr(NR), prm("lam_re"), ALU.mult))
            step(TT(pr(T2), pr(AI), prm("lam_im"), ALU.mult))
            step(TT(pr(FR), pr(T1), pr(T2), ALU.add))
            step(TT(pr(T1), pr(AI), prm("lam_re"), ALU.mult))
            step(TT(pr(T2), pr(NR), prm("lam_im"), ALU.mult))
            step(TT(pr(FI), pr(T1), pr(T2), ALU.subtract))
            pool.wait_ge(den_ready, 1)
            step(TT(pr(FR), pr(FR), pr(DEN_INV), ALU.mult))
            step(TT(pr(FI), pr(FI), pr(DEN_INV), ALU.mult))

            v3 = lambda ap: ap.rearrange("p (g c) -> p g c", g=GP)
            t_a, t_b = v3(bb[:, 0, :]), v3(bb[:, 1, :])

            def cmul(dr, di, ar, ai, br, bi):
                ar, ai = bc(ar, GRP), bc(ai, GRP)
                step(TT(t_a, br, ar, ALU.mult))
                step(TT(t_b, bi, ai, ALU.mult))
                step(TT(dr, t_a, t_b, ALU.subtract))
                step(TT(t_a, bi, ar, ALU.mult))
                step(TT(t_b, br, ai, ALU.mult))
                return TT(di, t_a, t_b, ALU.add)

            step(cmul(pbr[:, :, 7, :], pbi[:, :, 7, :], pr(FR), pr(FI), v3(s5in[:, 0, :]), v3(s5in[:, 1, :])))
            for m in range(1, BT):
                last = cmul(pbr[:, :, 7 - m, :], pbi[:, :, 7 - m, :], pr(AR), pr(AI),
                            pbr[:, :, 8 - m, :], pbi[:, :, 8 - m, :])
                if m < BT - 1:
                    step(last)
            last.then_inc(pb_ready, 1)
            pool.tensor_scalar(s5in[:, 1, :], s5in[:, 3, :], -1.0, 0.0, ALU.mult, ALU.add).then_inc(neg_c, 1)
            step(pool.tensor_copy(pr(A8R), pr(AR)))
            step(pool.tensor_copy(pr(A8I), pr(AI)))

            def square():
                step(TT(pr(T1), pr(A8R), pr(A8R), ALU.mult))
                step(TT(pr(T2), pr(A8I), pr(A8I), ALU.mult))
                step(TT(pr(COS_ANGLE), pr(A8R), pr(A8I), ALU.mult))
                step(TT(pr(A8R), pr(T1), pr(T2), ALU.subtract))
                step(TT(pr(A8I), pr(COS_ANGLE), pr(COS_ANGLE), ALU.add))

            for _ in range(3):
                square()
            pool.wait_ge(*full("kb1"))
            step(cmul(gre[:, :, 0, :], gim[:, :, 0, :], pr(AR), pr(AI), v3(s5in[:, 2, :]), v3(s5in[:, 3, :])))
            for r in range(1, BT):
                step(cmul(gre[:, :, r, :], gim[:, :, r, :], pr(AR), pr(AI),
                          gre[:, :, r - 1, :], gim[:, :, r - 1, :]))
            pool.tensor_scalar(s5a[:, 2048:4096], s5a[:, 2048:4096], -1.0, 0.0, ALU.mult, ALU.add)\
                .then_inc(g_ready, 1)
            pool.wait_ge(*emptied("kb1"))
            pool.wait_ge(*full("ub3"))
            pool.memset(big[5][:, :], 0.0).then_inc(m0_zero, 1)
            pool.wait_ge(m0_zero, 1)
            for r in range(BT):
                n = GRP * (r + 1)
                pool.dma_start(m0r[0:n, r, :], k7[P - n:P, :]).then_inc(m0_in, 16)
            pool.wait_ge(m0_in, 16 * BT)
            pool.wait_ge(*full("xs3"))
            pool.tensor_copy(m0T.rearrange("p g (r c) -> p g r c", r=BT),
                             m0r.rearrange("p r (g c) -> p g r c", g=NG)).then_inc(m0_ready, 1)
            pool.wait_ge(m0_ready, 1)
            pool.wait_ge(*emptied("xs3"))
            d = 1
            while d < NB:
                w = NB - d
                ar, ai = bc(pr(A8R), w), bc(pr(A8I), w)
                s1, s2 = sc1[:, :, 0:w], sc2[:, :, 0:w]
                t1, t2 = ysb[:, 0:GP, 0:w], ysb[:, GP:2 * GP, 0:w]
                fr, fi, tr, ti = xr[:, :, 0:w], xi[:, :, 0:w], xr[:, :, d:NB], xi[:, :, d:NB]
                step(TT(s1, fr, ar, ALU.mult))
                step(TT(t1, fi, ai, ALU.mult))
                step(TT(s2, fi, ar, ALU.mult))
                step(TT(t2, fr, ai, ALU.mult))
                step(TT(s1, s1, t1, ALU.subtract))
                step(TT(s2, s2, t2, ALU.add))
                step(TT(tr, tr, s1, ALU.add))
                last = TT(ti, ti, s2, ALU.add)
                d *= 2
                if d < NB:
                    step(last)
                    square()
            last.then_inc(scan_done, 1)

            for i in range(NT):
                pool.wait_ge(squares, NT + i + 1)
                row_rstd(i).then_inc(rstd_ready, 1)

            pool.wait_ge(*full("lc0"))
            pool.memset(b1_raw, 0.0).then_inc(b1_zero, 1)
            pool.wait_ge(h2_out, 16 * NT)
            pool.memset(xe, 0.0).then_inc(xe_zero, 1)
            pool.wait_ge(xe_zero, 1)
            pool.wait_ge(b1_in, 32)
            pool.wait_ge(h2_out, 16 * NT)
            step(pool.tensor_copy(b1_hl, b1_raw))
            TT(b1_hl[E:2 * E, :], b1_raw[E:2 * E, :], b1_hl[E:2 * E, :].bitcast(F32), ALU.subtract)\
                .then_inc(b1_ready, 1)
            pool.wait_ge(b1_ready, 1)
            pool.wait_ge(tab_ready, 1)
            token_bound, assign_bound = pool.to_reg(SEQ - 1), pool.to_reg(NA - 1)

            def gather(i):
                pool.tensor_copy(get_1[:, :], get_i[:, bass.ds(i, 1)]).then_inc(get_ready, 1)
                pool.wait_ge(get_ready, i + 1)
                pool.sem_inc(index_seen, 1)
                pool.indirect_dma_start(xe, None, h2_dram, bass.IndirectOffsetOnAxis(get_1[:, 0:1], 0),
                                        bounds_check=token_bound, oob_is_err=False).then_inc(moved, 16)

            def scatter(i):
                pool.tensor_copy(put_1[:, :], put_i[:, bass.ds(i, 1)]).then_inc(put_ready, 1)
                pool.wait_ge(put_ready, i + 1)
                pool.wait_ge(y_empty, i * W2C + (W2C + 2))
                pool.sem_inc(index_seen, 1)
                pool.indirect_dma_start(y_dram, bass.IndirectOffsetOnAxis(put_1[:, 0:1], 0), ye, None,
                                        bounds_check=assign_bound, oob_is_err=False).then_inc(moved, 16)

            def split_chunk(i, c):
                pool.wait_ge(w_rounded, i * EC + (c + 1))
                slot = item_chunk(i, c)[0]
                TT(w_lo[slot], ring[:, slot, :], w_hi[c % N_HI].bitcast(F32), ALU.subtract).then_inc(w_split_p, 1)

            def item(i):
                split_chunk(i, POOL_SPLITS[0])
                pool.wait_ge(moved, i * 32 + 16)
                pool.sem_inc(ye_free, 1)
                pool.wait_ge(x_full, i * 2 + 2)
                gather(i + 1)
                for c in POOL_SPLITS[1:]:
                    split_chunk(i, c)
                scatter(i)

            gather(0)
            n = pool.value_load(item_e[0:1, N_ITEMS + 1:N_ITEMS + 2], min_val=E, max_val=N_ITEMS)
            with pool.Fori(0, E) as i:
                item(i)
            with pool.If(n > E):
                with pool.Fori(E, N_ITEMS) as i:
                    with pool.If(i < n):
                        item(i)
                    pool.nop()
            pool.nop()
            for i in range(NT):
                pool.wait_ge(fsq, i + 1)
                row_rstd(i).then_inc(frstd, 1)

        @block.scalar
        def _(act):
            n_chain = [0]

            def step(ins):
                n_chain[0] += 1
                ins.then_inc(act_chain, 1)
                act.wait_ge(act_chain, n_chain[0])

            xt = x.rearrange("(i p) d -> i p d", i=NT)
            for i in range(NT):
                act.dma_start(xn[:, i, :], xt[i]).then_inc(x_in[i], 16)
            act.dma_start(par_s[:, :], par).then_inc(par_in, 16)
            act.dma_start(ring[:, 4, 512:1536], s5bc).then_inc(par_in, 16)
            act.dma_start(pos_i, pos.partition_broadcast(P)).then_inc(pos_in, 16)
            act.dma_start(rw_s[:, :, :], rw).then_inc(moe_in, 16)

            for i in range(NT):
                act.wait_ge(x_in[i], 16)
                act.activation(big[0][:, i * D:(i + 1) * D], xn[:, i, :], ACT.Square,
                               accum_out=ss[:, i:i + 1]).then_inc(squares, 1)

            def round_chunk_t(n):
                act.wait_ge(landed[t_slot(n)], 16 * (n // len(T_SLOTS) + 1))
                if n >= len(T_HI):
                    act.wait_ge(*full(LAST_USE[n - len(T_HI)]))
                act.activation(t_hi[n % 2], ring[:, t_slot(n), :], ACT.Copy).then_inc(t_rounded, 1)

            round_chunk_t(0)
            act.wait_ge(par_in, 32)
            act.wait_ge(squares, NT)
            for k in range(KD):
                act.wait_ge(*full(f"xT{k}"))
                act.activation(h_hi[:, k, :], bk(f"xT{k}")[:, :], ACT.Copy,
                               scale=prm("norm_mix", k)).then_inc(h_rounded, 1)
            round_chunk_t(1)
            act.activation(pr(DT), prm("log_dt"), ACT.Exp).then_inc(s5_act, 1)
            act.wait_ge(s5_pool, 1)
            act.activation(pr(MAG), pr(T1), ACT.Exp).then_inc(s5_act, 1)
            act.wait_ge(angles, 1)
            act.activation(pr(SIN), pr(SIN_ANGLE), ACT.Sin).then_inc(s5_act, 1)
            act.activation(pr(COS), pr(COS_ANGLE), ACT.Sin).then_inc(s5_act, 1)
            act.wait_ge(angles, 2)
            act.activation(sinT, sinT, ACT.Sin).then_inc(rope_act, 1)
            act.activation(cosT, cosT, ACT.Sin).then_inc(rope_act, 1)
            for c in range(4):
                act.wait_ge(*full(f"u{c}"))
                act.activation(uT[:, c, :], bk(f"u{c}")[:, :], ACT.Copy).then_inc(act_emptied, 1)
                if c % 2:
                    round_chunk_t(C_U + c // 2 + 2)
            for r in range(BT):
                act.wait_ge(*full(f"ua{r}"))
                act.activation(ujr[0:NB, :, r, :], bk(f"ua{r}")[0:NB, :].rearrange("p (g c) -> p g c", g=NG),
                               ACT.Copy).then_inc(act_emptied, 1)
            for n in range(C_Q + 2, C_V + 2):
                round_chunk_t(n)
            for i in range(8):
                dst = (hTr, hTi)[i // 4]
                act.wait_ge(*full(f"hT{i}"))
                act.activation(dst[:, 4 * (i % 4):4 * (i % 4) + 4, :].rearrange("p g n -> p (g n)"),
                               bk(f"hT{i}")[:, :], ACT.Copy).then_inc(act_emptied, 1)
            def head_std(h):
                act.wait_ge(gn_var, h + 1)
                act.activation(mv[:, :, 2], mv[:, :, 1], ACT.Sqrt).then_inc(gn_std, 1)

            act.wait_ge(*emptied("k3"))
            for c in range(4):
                for i in range(2):
                    act.wait_ge(*full(f"v{2 * c + i}"))
                    act.activation(vt[:, 2 * i:2 * i + 2, c * CW:(c + 1) * CW],
                                   bk(f"v{2 * c + i}")[:, :].rearrange("p (a n) -> p a n", a=2),
                                   ACT.Copy).then_inc(act_emptied, 1)
                round_chunk_t(C_V + c + 2)
                if c:
                    head_std(c - 1)
            for k in range(KD):
                act.wait_ge(*full(f"g{k}"))
                act.activation(gs[:, k, :], bk(f"g{k}")[:, :], ACT.Silu).then_inc(act_emptied, 1)
                if k % 2:
                    round_chunk_t(C_G + k // 2 + 2)
                if k == 1:
                    head_std(HEADS - 1)
            for k in range(KD):
                act.wait_ge(*full(f"ga{k}"))
                act.activation(siga[:, k, :], bk(f"ga{k}")[:, :], ACT.Sigmoid).then_inc(act_emptied, 1)
                if k % 2:
                    round_chunk_t(C_GA + k // 2 + 2)
            for r in range(BT):
                act.wait_ge(*full(f"yc{r}"))
                act.activation(yjr[0:NB, :, 64 * r:64 * r + 64],
                               bk(f"yc{r}")[0:NB, :].rearrange("p (g r c) -> p r g c", g=4, r=BT),
                               ACT.Copy).then_inc(act_emptied, 1)
            act.wait_ge(*emptied("yd3"))
            act.dma_start(b2_s, b2).then_inc(moe_in, 16)
            act.dma_start(gvec, g_ffn.partition_broadcast(P)).then_inc(gf_in, 16)
            step(act.activation(zT[:, :, :], zT[:, :, :], ACT.Gelu_apprx_tanh))
            act.activation(z_hi[:, :, :], zT[:, :, :], ACT.Copy).then_inc(z_rounded, 1)
            act.wait_ge(*emptied("rT7"))
            for h in range(2):
                act.activation(gs_hi[:, 4 * h:4 * h + 4, :], gs[:, 4 * h:4 * h + 4, :], ACT.Copy)\
                    .then_inc(gated_rounded, 1)
            for k in range(KD):
                act.wait_ge(*full(f"gb{k}"))
                act.activation(sigb[:, k, :], bk(f"gb{k}")[:, :], ACT.Sigmoid).then_inc(act_emptied, 1)
                if k % 2:
                    round_chunk_t(C_GB + k // 2 + 2)
            for c in range(4):
                act.wait_ge(*full(f"z{c}"))
                act.activation(zg[:, c, :], bk(f"z{c}")[:, :], ACT.Sigmoid,
                               bias=prm("b_glu", c)).then_inc(act_emptied, 1)
            round_chunk_t(C_GLU + 2)
            act.wait_ge(*full("gb7"))
            for i in range(NT):
                act.dma_start(x2[:, i, :], xt[i]).then_inc(x_in2[i], 16)
            for c in range(4):
                round_chunk_t(C_BRET + c + 2)
            for k in range(KD):
                act.wait_ge(*emptied(f"ya{k}"))
                act.activation(mg_hi[:, k, :], mg[:, k, :], ACT.Copy).then_inc(mg_rounded, 1)
                if k % 4 == 3:
                    round_chunk_t(C_BS5 + k // 4 + 2)
            for c in range(2):
                round_chunk_t(C_OUT + c + 2)
            for i in range(NT):
                act.wait_ge(*emptied(f"wo{6 + i // 2}"))
                act.activation(h2[:, i, :], x2[:, i, :], ACT.Square,
                               accum_out=ss[:, i:i + 1]).then_inc(squares, 1)
            def round_chunk(i, c):
                slot, arrived = item_chunk(i, c)
                act.wait_ge(*arrived)
                act.activation(w_hi[c % N_HI], ring[:, slot, :], ACT.Copy).then_inc(w_rounded, 1)

            act.wait_ge(*full("wo7"))
            round_chunk(0, 0)
            for k in range(KD):
                act.wait_ge(*full(f"h2T{k}"))
                act.activation(h2T[:, k, :], bk(f"h2T{k}")[:, :], ACT.Copy).then_inc(act_emptied, 1)
            act.wait_ge(h2_ready, NT)
            act.dma_start(gvec, g_fin.partition_broadcast(P)).then_inc(gfin_in, 16)
            for i in range(NT):
                act.dma_start(h2_dram[i * P:(i + 1) * P, :], h2[:, i, :]).then_inc(h2_out, 16)

            act.wait_ge(*full("lc0"))
            act.activation(lgT, bk("lc0")[0:E, :], ACT.Copy).then_inc(act_emptied, 1)
            act.wait_ge(b1_zero, 1)
            for half in range(2):
                act.dma_start(b1_raw[half * E:(half + 1) * E, :], b1).then_inc(b1_in, 16)

            act.wait_ge(top_ready, 1)
            for i in range(NT):
                act.activation(gate[:, i, :], top_v[:, i, 0:TOPK], ACT.Exp, bias=negm[:, i:i + 1],
                               accum_out=gsum[:, i:i + 1]).then_inc(gate_exp, 1)
            round_chunk(0, 1)
            round_chunk(0, 2)
            def round_rows(i):
                for h in range(2):
                    act.wait_ge(x_full, i * 2 + (h + 1))
                    act.activation(x_hi[:, 4 * h:4 * h + 4, :].rearrange("p k t -> p (k t)"), bank[4 + h][:, :],
                                   ACT.Copy).then_inc(x_rounded, 1)

            def round_tile(i, j):
                act.wait_ge(a_full, i * FT + (j + 1))
                act.activation(a_hi[:, j, :], bank[2 + j % 2][:, 0:P], ACT.Copy).then_inc(a_rounded, 1)

            def item(i):
                for s in range(EC):
                    if 1 <= s <= FT:
                        j = s - 1
                        act.wait_ge(glu_ready, i * FT + (j + 1))
                        act.activation(sg_t[:, j % 2, :], g_t[:, j % 2, :], ACT.Sigmoid,
                                       scale=SIG_ALPHA).then_inc(sg_ready, 1)
                        if j > 1:
                            round_tile(i, j - 2)
                    if s == FT:
                        round_rows(i + 1)
                        round_tile(i, FT - 2)
                        round_tile(i, FT - 1)
                    if s > FT:
                        results(i, s - FT - 1)
                    c = s + AHEAD
                    if c < EC:
                        act.wait_ge(*(used(i, c - N_HI) if c >= N_HI else used(i - 1, c - N_HI + EC)))
                        round_chunk(i, c)
                    else:
                        act.wait_ge(*used(i, c - N_HI))
                        round_chunk(i + 1, c - EC)
                results(i, W2C - 1)

            def results(i, c):
                if c == 0:
                    act.wait_ge(ye_free, i + 1)
                act.wait_ge(y_full, i * W2C + (c + 1 + W2C))
                act.activation(ye[:, c * CW:(c + 1) * CW], bank[6 + c % 2][:, 0:CW], ACT.Copy).then_inc(y_empty, 1)

            act.sem_inc(y_empty, 2)
            act.wait_ge(tab_ready, 1)
            round_rows(0)
            n = act.value_load(item_e[0:1, N_ITEMS + 1:N_ITEMS + 2], min_val=E, max_val=N_ITEMS)
            with act.Fori(0, E) as i:
                item(i)
            with act.If(n > E):
                with act.Fori(E, N_ITEMS) as i:
                    with act.If(i < n):
                        item(i)
                    act.nop()
            act.nop()
            for i in range(NT):
                act.wait_ge(summed, i + 1)
                act.activation(ring[:, RING - NT + i, 0:D], x2[:, i, :], ACT.Square,
                               accum_out=ss[:, i:i + 1]).then_inc(fsq, 1)

        @block.vector
        def _(dve):
            n_chain = [0]

            def step(ins):
                n_chain[0] += 1
                ins.then_inc(dve_chain, 1)
                dve.wait_ge(dve_chain, n_chain[0])

            TT, TS, STT = dve.tensor_tensor, dve.tensor_scalar, dve.scalar_tensor_tensor
            rs = ss[:, NT:2 * NT]

            def split_chunk_t(n):
                dve.wait_ge(t_rounded, n + 1)
                TT(w_lo[t_slot(n)], ring[:, t_slot(n), :], t_hi[n % 2].bitcast(F32), ALU.subtract)\
                    .then_inc(t_split, 1)

            for i in range(NT):
                dve.wait_ge(rstd_ready, i + 1)
                TS(xn[:, i, :], xn[:, i, :], rs[:, i:i + 1], None, ALU.mult).then_inc(xn_ready, 1)

            def reduce_angle(r, c, tk):
                step(TS(tk, r, 1.0 / TWO_PI, ROUND, ALU.mult, ALU.add))
                step(TS(tk, tk, ROUND, None, ALU.subtract))
                for part in (PI_1, PI_2, PI_3):
                    step(STT(r, tk, -part, r, ALU.mult, ALU.add))
                step(TS(r, r, PI_IN, -PI_IN, ALU.min, ALU.max))
                step(TS(tk, r, -1.0, None, ALU.mult))
                step(TT(tk, tk, r, ALU.max))
                return TS(c, tk, -1.0, float(np.float32(np.pi / 2)), ALU.mult, ALU.add)

            split_chunk_t(0)
            for k in range(KD):
                dve.wait_ge(h_rounded, k + 1)
                STT(h_lo[:, k, :], bk(f"xT{k}")[:, :], prm("norm_mix", k), h_hi[:, k, :].bitcast(F32),
                    ALU.mult, ALU.subtract).then_inc(dve_emptied, 1)
            split_chunk_t(1)
            dve.wait_ge(s5_pool, 1)
            step(dve.tensor_copy(pr(SIN_ANGLE), pr(TH)))
            reduce_angle(pr(SIN_ANGLE), pr(COS_ANGLE), pr(T3)).then_inc(angles, 1)
            dve.wait_ge(s5_pool, 2)
            dve.reciprocal(pr(DEN_INV), pr(DEN)).then_inc(den_ready, 1)
            dve.wait_ge(pos_in, 16)
            dve.wait_ge(cst_in, 16)
            step(dve.tensor_copy(rope_k, pos_i))
            step(TS(sinT, rope_k, con("inv_freq"), None, ALU.mult))
            reduce_angle(sinT, cosT, rope_k).then_inc(angles, 1)
            for n in range(C_U + 2, C_Q + 2):
                split_chunk_t(n)
            for i in range(4):
                dve.wait_ge(*full(f"ub{i}"))
                dve.tensor_copy(ub[:, 8 * i:8 * i + 8, :].rearrange("p g j -> p (g j)"),
                                bk(f"ub{i}")[:, :]).then_inc(dve_emptied, 1)
            dve.wait_ge(rope_act, 2)
            step(TS(sinT, sinT, con("sin_sign"), None, ALU.mult))
            H = DK // 2
            for name, dst, scale, c0 in (("q", qT, 1.0, C_Q), ("k", kT, DK ** -0.5, C_K)):
                for h in range(HEADS):
                    dve.wait_ge(*full(f"{name}{h}"))
                    b = bk(f"{name}{h}")
                    if (name, h) != ("q", 0):
                        dve.wait_ge(*emptied(f"{name}{h - 1}" if h else "q3"))
                    STT(rot_a, b[:, :], scale, cosT, ALU.mult, ALU.mult)
                    STT(rot_b[0:H, :], b[H:P, :], scale, sinT[0:H, :], ALU.mult, ALU.mult)
                    step(STT(rot_b[H:P, :], b[0:H, :], scale, sinT[H:P, :], ALU.mult, ALU.mult))
                    TT(dst[:, h, :], rot_a, rot_b, ALU.add).then_inc(dve_emptied, 1)
                    if h % 2:
                        split_chunk_t(c0 + h // 2 + 2)
            for odd in range(2):
                dve.wait_ge(*full(f"kb{odd}"))
                dve.tensor_copy(k7.rearrange("p (g o c) -> p g o c", o=2, c=GRP)[:, :, odd, :],
                                bk(f"kb{odd}")[:, 0:GP * GRP].rearrange("p (g c) -> p g c", g=GP))\
                    .then_inc(dve_emptied, 1)
            for i in range(4):
                dst = (xr, xi)[i // 2]
                dve.wait_ge(*full(f"xs{i}"))
                dve.tensor_copy(dst[:, 8 * (i % 2):8 * (i % 2) + 8, :].rearrange("p g j -> p (g j)"),
                                bk(f"xs{i}")[:, :]).then_inc(dve_emptied, 1)
            dve.wait_ge(dec_in, 16)
            for h in range(HEADS):
                for j in range(NT):
                    w = SEQ - j * P
                    dve.wait_ge(*full(f"sc{4 * h + j}"))
                    TT(sT[:, j, 0:w], bk(f"sc{4 * h + j}")[:, 0:w], decay[:, h, 0:w],
                       ALU.mult).then_inc(dve_emptied, 1)
                split_chunk_t(C_V + h + 2)
                for m in range(2):
                    b = bk(f"in{2 * h + m}")
                    dve.wait_ge(*full(f"in{2 * h + m}"))
                    for a in range(2):
                        last = dve.bn_stats(stat[:, 2 * m + a, 0:6], b[:, a * DV:(a + 1) * DV])
                step(last)
                if h:
                    dve.wait_ge(*emptied(f"in{2 * h - 1}"))
                for i in range(NT):
                    last = dve.bn_aggr(mv[:, i, 0:2], stat[:, i, 0:6])
                step(last)
                TS(mv[:, :, 1], mv[:, :, 1], EPS, None, ALU.add).then_inc(gn_var, 1)
                dve.wait_ge(gn_std, h + 1)
                step(dve.reciprocal(mv[:, :, 2], mv[:, :, 2]))
                for i in range(NT):
                    b = bk(f"in{2 * h + i // 2}")
                    last = TS(ret[:, i, h * DV:(h + 1) * DV], b[:, (i % 2) * DV:(i % 2 + 1) * DV],
                              mv[:, i, 0:1], mv[:, i, 2:3], ALU.subtract, ALU.mult)
                    if i % 2:
                        last.then_inc(dve_emptied, 1)
            for n in range(C_G + 2, C_GA + 2):
                split_chunk_t(n)
            for k in range(KD):
                dve.wait_ge(*full(f"rT{k}"))
                dve.wait_ge(*emptied(f"g{k}"))
                STT(gs[:, k, :], bk(f"rT{k}")[:, :], prm("ret_gn", k), gs[:, k, :],
                    ALU.mult, ALU.mult).then_inc(dve_emptied, 1)
            for n in range(C_GA + 2, C_GB + 2):
                split_chunk_t(n)
            for i in range(4):
                dve.wait_ge(*full(f"ys{i}"))
                dve.tensor_copy(ysb.rearrange("p (g o) j -> p g o j", o=2)[:, 8 * (i // 2):8 * (i // 2) + 8, i % 2, :],
                                bk(f"ys{i}")[:, :].rearrange("p (g j) -> p g j", g=8)).then_inc(dve_emptied, 1)
            for c in range(4):
                dve.wait_ge(*full(f"yd{c}"))
                by_r = lambda ap: ap.rearrange("p (j r) -> p r j", r=BT)
                STT(by_r(zT[:, c, :]), by_r(uT[:, c, :]), prm("d_skip", c),
                    bk(f"yd{c}")[:, :].rearrange("p (r j) -> p r j", r=BT),
                    ALU.mult, ALU.add).then_inc(dve_emptied, 1)
            dve.wait_ge(z_rounded, 1)
            TT(z_lo[:, :, :], zT[:, :, :], z_hi[:, :, :].bitcast(F32), ALU.subtract).then_inc(z_split, 1)
            for h in range(2):
                dve.wait_ge(gated_rounded, h + 1)
                v = slice(4 * h, 4 * h + 4)
                TT(gs_lo[:, v, :], gs[:, v, :], gs_hi[:, v, :].bitcast(F32), ALU.subtract).then_inc(gated_split, 1)
            for n in range(C_GB + 2, C_GLU + 2):
                split_chunk_t(n)
            for c in range(4):
                dve.wait_ge(*emptied(f"z{c}"))
                step(TT(zg[:, c, :], zg[:, c, :], zT[:, c, :], ALU.mult))
                step(dve.tensor_copy(zg_hi[:, c, :], zg[:, c, :]))
                TT(zg_lo[:, c, :], zg[:, c, :], zg_hi[:, c, :].bitcast(F32), ALU.subtract).then_inc(zg_split, 1)
            split_chunk_t(C_GLU + 2)
            for k in range(KD):
                dve.wait_ge(*full(f"yb{k}"))
                TT(mg[:, k, :], bk(f"yb{k}")[:, :], sigb[:, k, :], ALU.mult).then_inc(dve_emptied, 1)
                if k % 2:
                    split_chunk_t(C_BRET + k // 2 + 2)

            def split_merged(k):
                dve.wait_ge(mg_rounded, k + 1)
                TT(mg_lo[:, k, :], mg[:, k, :], mg_hi[:, k, :].bitcast(F32), ALU.subtract).then_inc(mg_split, 1)

            for k in range(KD):
                dve.wait_ge(*full(f"ya{k}"))
                step(TT(siga[:, k, :], bk(f"ya{k}")[:, :], siga[:, k, :], ALU.mult))
                TT(mg[:, k, :], mg[:, k, :], siga[:, k, :], ALU.add).then_inc(dve_emptied, 1)
                if k:
                    split_merged(k - 1)
                if k == 3:
                    split_chunk_t(C_BS5 + 2)
            split_merged(KD - 1)
            split_chunk_t(C_BS5 + 3)
            for i in range(NT):
                dve.wait_ge(x_in2[i], 16)
            for n in range(8):
                c, m = n // 2, n % 2
                dve.wait_ge(*full(f"wo{n}"))
                dst = x2[:, 2 * m:2 * m + 2, c * CW:(c + 1) * CW]
                TT(dst, bk(f"wo{n}")[:, :].rearrange("p (a n) -> p a n", a=2), dst,
                   ALU.add).then_inc(dve_emptied, 1)
                if n in (1, 3):
                    split_chunk_t(C_OUT + n // 2 + 2)
            dve.wait_ge(gf_in, 16)
            for i in range(NT):
                dve.wait_ge(rstd_ready, NT + i + 1)
                STT(h2[:, i, :], x2[:, i, :], rs[:, i:i + 1], gvec[:, :], ALU.mult, ALU.mult)\
                    .then_inc(h2_ready, 1)

            def split_chunk(i, c):
                dve.wait_ge(w_rounded, i * EC + (c + 1))
                slot = item_chunk(i, c)[0]
                TT(w_lo[slot], ring[:, slot, :], w_hi[c % N_HI].bitcast(F32), ALU.subtract).then_inc(w_split, 1)

            split_chunk(0, 0)
            dve.wait_ge(*full("lg0"))
            TT(lg[:, :, :], bk("lg0")[:, 0:NT * E].rearrange("p (i e) -> p i e", i=NT),
               prm("router_b").unsqueeze(1).to_broadcast([P, NT, E]), ALU.add).then_inc(dve_emptied, 1)
            dve.wait_ge(*emptied("lg0"))
            for i in range(NT):
                step(dve.max(top_v[:, i, :], lg[:, i, :]))
            for i in range(NT):
                last = dve.max_index(top_i[:, i, :], top_v[:, i, :], lg[:, i, :])
            step(last)
            TS(negm[:, :], top_v[:, :, 0], -1.0, None, ALU.mult).then_inc(top_ready, 1)
            step(dve.tensor_copy(top_f[:, :, :], top_i[:, :, :]))
            topb = top_f[:, :, 0:TOPK].unsqueeze(3).to_broadcast([P, NT, TOPK, E])
            eid = con("expert_id").unsqueeze(1).unsqueeze(1).to_broadcast([P, NT, TOPK, E])
            step(TT(oneh[:, :, :, :], topb, eid, ALU.is_equal))
            over_k = lambda ap: ap.rearrange("p i k e -> p i e k")
            dve.memset(before_sum[:, 0, :], 0.0)
            step(dve.tensor_reduce(hot[:, :, :], over_k(oneh[:, :, :, :]), AX.X, ALU.add))
            for i in range(NT):
                last = TT(before_sum[:, i + 1, :], before_sum[:, i, :], hot[:, i, :], ALU.add)
                if i < NT - 1:
                    step(last)
            last.then_inc(hot_ready, 1)
            dve.wait_ge(*full("rk0"))
            dve.tensor_copy(n_of, bk("rk0")[:, NT * E:(NT + 1) * E])
            dve.tensor_copy(cum[:, :, :], bk("rk0")[:, 0:NT * E].rearrange("p (i e) -> p i e", i=NT))\
                .then_inc(dve_emptied, 1)
            dve.wait_ge(*emptied("rk0"))
            step(TS(n_blocks, n_of, float(P), 1.0, ALU.is_gt, ALU.add))
            for k in range(2, NT):
                step(STT(n_blocks, n_of, float(k * P), n_blocks, ALU.is_gt, ALU.add))
            src, dst, d = n_blocks, end_a, 1
            while d < E:
                dve.tensor_copy(dst[:, 0:d], src[:, 0:d])
                step(TT(dst[:, d:E], src[:, d:E], src[:, 0:E - d], ALU.add))
                src, dst, d = dst, (end_b if dst is end_a else end_a), 2 * d
            ends = src
            step(TT(first, ends, n_blocks, ALU.subtract))
            step(STT(cum[:, :, :], first.unsqueeze(1).to_broadcast([P, NT, E]), float(P), cum[:, :, :],
                     ALU.mult, ALU.add))
            step(TT(wrk[:, :, :, :], oneh[:, :, :, :],
                    cum[:, :, :].unsqueeze(2).to_broadcast([P, NT, TOPK, E]), ALU.mult))
            step(dve.tensor_reduce(rank[:, :], wrk[:, :, :, :].rearrange("p i k e -> p (i k) e"), AX.X, ALU.add))
            dest, item_slot = place_i[:, 0, :], place_t
            step(dve.tensor_copy(dest, rank[:, :]))
            TS(item_slot[:, 0, :], dest, P.bit_length() - 1, None, ALU.arith_shift_right)
            step(TS(item_slot[:, 1, :], dest, P - 1, None, ALU.bitwise_and))
            step(dve.tensor_copy(place_f[:, :, :], item_slot[:, :, :]))
            NC, NI = NA // P, N_ITEMS + 1
            wide = lambda ap, n: ap.unsqueeze(2).to_broadcast([P, NC, n])
            step(TT(in_item, con("item_id").unsqueeze(1).to_broadcast([P, NC, NI]), wide(place_f[:, 0, :], NI),
                    ALU.is_equal))
            TT(digits[:, :, 0, :], in_item, wide(con("id_hi"), NI), ALU.mult)
            TT(digits[:, :, 1, :], in_item, wide(con("id_lo"), NI), ALU.mult)
            step(TS(ended, ends[0:NI, :], con("row")[0:NI, :], None, ALU.is_le))
            step(dve.tensor_reduce(item_c, ended, AX.X, ALU.add))
            TS(item_c, item_c, float(E - 1), None, ALU.min)
            TT(in_slot, con("slot_id").unsqueeze(1).to_broadcast([P, NC, P]), wide(place_f[:, 1, :], P),
               ALU.is_equal).then_inc(digits_ready, 1)
            dve.wait_ge(*full("tb0"))
            tb = bk("tb0")
            dve.tensor_copy(item_f[:, 0:NI], tb[0:1, 2 * NI:3 * NI])
            dve.tensor_copy(item_f[:, NI:NI + 1], ends[0:1, E - 1:E])
            step(TS(slot_hi, tb[:, 0:NI], float(ID_LO), -float(ID_LO), ALU.mult, ALU.add))
            step(TT(slot_hi, slot_hi, tb[:, NI:2 * NI], ALU.add))
            step(TS(slot_lo, slot_hi, 0.0, float(2 * NO_SLOT), ALU.is_lt, ALU.mult))
            step(TT(slot_hi, slot_hi, slot_lo, ALU.add))
            step(dve.tensor_copy(put_i[:, :], slot_hi))
            TS(get_i[:, :], put_i[:, :], 2, None, ALU.arith_shift_right)
            dve.tensor_copy(item_e[:, :], item_f[:, :]).then_inc(dve_emptied, 1)
            dve.wait_ge(*emptied("tb0"))
            dve.sem_inc(tab_ready, 1)
            dve.wait_ge(gate_exp, NT)
            step(dve.reciprocal(gsum[:, NT:2 * NT], gsum[:, 0:NT]))
            step(TT(gate[:, :, :], gate[:, :, :], bc(gsum[:, NT:2 * NT], TOPK), ALU.mult))
            step(TT(wrk[:, :, :, :], oneh[:, :, :, :],
                    gate[:, :, :].unsqueeze(3).to_broadcast([P, NT, TOPK, E]), ALU.mult))
            dve.tensor_reduce(gte[:, :, :], over_k(wrk[:, :, :, :]), AX.X, ALU.add).then_inc(gte_ready, 1)
            dve.wait_ge(*full("gT0"))
            dve.tensor_copy(gTs[:, :], bk("gT0")[0:E, :]).then_inc(dve_emptied, 1)
            dve.sem_inc(gu_empty, 2)

            def split_rows(i):
                for h in range(2):
                    dve.wait_ge(x_rounded, i * 2 + (h + 1))
                    hi, lo = (v[:, 4 * h:4 * h + 4, :].rearrange("p k t -> p (k t)") for v in (x_hi, x_lo))
                    TT(lo, bank[4 + h][:, :], hi.bitcast(F32), ALU.subtract).then_inc(x_split, 1)

            def split_tile(i, j):
                dve.wait_ge(a_rounded, i * FT + (j + 1))
                TT(a_lo[:, j, :], bank[2 + j % 2][:, 0:P], a_hi[:, j, :].bitcast(F32),
                   ALU.subtract).then_inc(a_split, 1)

            def pick_bias(i):
                e = dve.value_load(item_e[0:1, bass.ds(i, 1)], min_val=0, max_val=E - 1)
                dve.tensor_copy(pick, con("pick")[:, bass.ds(e, 1)].to_broadcast([P, P])).then_inc(pick_ready, 1)

            def item(i):
                for s in range(EC):
                    if 1 <= s <= FT:
                        j = s - 1
                        b = j % 2
                        dve.wait_ge(gu_full, i * FT + (j + 1))
                        if j >= 2:
                            dve.wait_ge(act_ready, i * FT + (j - 1))
                        TS(g_t[:, b, :], bank[b][:, 0:P], LIMIT, None, ALU.min).then_inc(glu_ready, 1)
                        TS(l_t[:, b, :], bank[b][:, P:2 * P], LIMIT, -LIMIT, ALU.min, ALU.max)\
                            .then_inc(gu_empty, 1)
                        if j > 1:
                            split_tile(i, j - 2)
                        dve.wait_ge(sg_ready, i * FT + (j + 1))
                        TT(gs_t[:, b, :], g_t[:, b, :], sg_t[:, b, :], ALU.mult).then_inc(gs_ready, 1)
                        dve.wait_ge(gs_ready, i * FT + (j + 1))
                        STT(a_t[:, j % 3, :], l_t[:, b, :], 1.0, gs_t[:, b, :], ALU.add, ALU.mult)\
                            .then_inc(act_ready, 1)
                    if s == FT:
                        pick_bias(i + 1)
                        split_rows(i + 1)
                        split_tile(i, FT - 2)
                        split_tile(i, FT - 1)
                    c = s + AHEAD - 1
                    if c % EC not in POOL_SPLITS:
                        split_chunk(*((i, c) if c < EC else (i + 1, c - EC)))

            split_chunk(0, 1)
            pick_bias(0)
            split_rows(0)
            n = dve.value_load(item_e[0:1, N_ITEMS + 1:N_ITEMS + 2], min_val=E, max_val=N_ITEMS)
            with dve.Fori(0, E) as i:
                item(i)
            with dve.If(n > E):
                with dve.Fori(E, N_ITEMS) as i:
                    with dve.If(i < n):
                        item(i)
                    dve.nop()
            dve.nop()

            for n in range(8):
                i, m = n // 2, n % 2
                dve.wait_ge(*full(f"b2{n}"))
                dst = x2[:, i, m * 512:(m + 1) * 512]
                TT(dst, bk(f"b2{n}")[:, :], dst, ALU.add).then_inc(dve_emptied, 1)
            dve.wait_ge(*emptied("b27"))
            for i in range(NT):
                for k in range(TOPK):
                    if k % 2 == 0:
                        dve.wait_ge(yk_in[2 * i + k // 2], 16)
                    last = STT(x2[:, i, :], yk[i][:, k, :], gate[:, i, k:k + 1], x2[:, i, :],
                               ALU.mult, ALU.add)
                    if k < TOPK - 1:
                        step(last)
                last.then_inc(summed, 1)
            dve.wait_ge(gfin_in, 16)
            for i in range(NT):
                dve.wait_ge(frstd, i + 1)
                STT(x2[:, i, :], x2[:, i, :], rs[:, i:i + 1], gvec[:, :], ALU.mult, ALU.mult)\
                    .then_inc(fin_ready, 1)

        @block.tensor
        def _(pe):
            MM, TR = pe.matmul, pe.transpose

            def start(name):
                n = JOB[name]
                if n >= 8:
                    e, v = EMPTIED[n - 8]
                    pe.wait_ge(EMPT[e], v)
                return bank[n % 8]

            def chunk(n, k=KD):
                pe.wait_ge(t_split, n + 1)
                return [w.rearrange("p (k n) -> p k n", k=k) for w in (t_hi[n % 2], w_lo[t_slot(n)])]

            def channel_major(name, c0, rhs, k_tiles, first, jobs=None):
                r_hi, r_lo = rhs
                per = CH // k_tiles // P
                for m in jobs or range(sum(1 for j, _ in JOBS if j.rstrip("0123456789") == name)):
                    if m % per == 0:
                        w_h, w_l = chunk(c0 + m // per, k_tiles)
                    b = start(f"{name}{m}")
                    cols = slice((m % per) * P, (m % per + 1) * P)
                    for k in range(k_tiles):
                        if m == 0 and first:
                            pe.wait_ge(*first(k))
                        for n, (w, r) in enumerate(((w_h, r_hi), (w_h, r_lo), (w_l, r_hi))):
                            last = MM(b[:, :], w[:, k, cols], r[:, k, :], start=(k == 0 and n == 0),
                                      stop=(k == k_tiles - 1 and n == 2))
                    last.then_inc(bank_full, 1)

            def token_major(name, c0, lhs, chunks, first=None):
                l_hi, l_lo = lhs
                for c in chunks:
                    w_h, w_l = chunk(c0 + c)
                    for m in range(2):
                        b = start(f"{name}{2 * c + m}")
                        for a in range(2):
                            i = 2 * m + a
                            for k in range(KD):
                                if first and c == 0 and i == 0:
                                    pe.wait_ge(*first(k))
                                for n, (h, w) in enumerate(((l_hi, w_h), (l_hi, w_l), (l_lo, w_h))):
                                    last = MM(b[:, a * CW:(a + 1) * CW], h[:, k, i * P:(i + 1) * P], w[:, k, :],
                                              start=(k == 0 and n == 0), stop=(k == KD - 1 and n == 2))
                        last.then_inc(bank_full, 1)

            hT = (h_hi, h_lo)
            pe.wait_ge(cst_in, 16)
            b = [start(f"xT{k}") for k in range(KD)]
            for i in range(NT):
                pe.wait_ge(xn_ready, i + 1)
                for k in range(KD):
                    last = TR(b[k][:, i * P:(i + 1) * P], xn[:, i, k * P:(k + 1) * P], ident)
                    if i == NT - 1:
                        last.then_inc(bank_full, 1)
            channel_major("u", C_U, hT, KD, lambda k: emptied(f"xT{k}"))
            pe.wait_ge(*emptied("u3"))
            for r in range(BT):
                b = start(f"ua{r}")
                for c in range(4):
                    last = TR(b[0:NB, c * P:(c + 1) * P], uT[:, c, r:SEQ:BT], ident)
                last.then_inc(bank_full, 1)
            pe.wait_ge(*emptied("ua7"))
            for i in range(4):
                b = start(f"ub{i}")
                for g in range(8):
                    last = TR(b[:, g * NB:(g + 1) * NB],
                              ujr[0:NB, 8 * i + g, :, :].rearrange("p r c -> p (r c)"), ident[0:NB, 0:NB])
                last.then_inc(bank_full, 1)
            channel_major("q", C_Q, hT, KD, None)
            channel_major("k", C_K, hT, KD, None)
            pe.wait_ge(pb_ready, 1)
            for i in range(8):
                b = start(f"hT{i}")
                src = (pbr, pbi)[i // 4]
                for g in range(4):
                    last = TR(b[:, g * P:(g + 1) * P],
                              src[:, 4 * (i % 4) + g, :, :].rearrange("p m c -> p (m c)"), ident)
                last.then_inc(bank_full, 1)
            pe.wait_ge(neg_c, 1)
            for odd in range(2):
                b = start(f"kb{odd}")
                p0 = NS * odd
                for gp in range(GP):
                    for s, (w, c) in enumerate(((pbr, s5in[:, 2, :]), (pbi, s5in[:, 1, :]))):
                        last = MM(b[:, gp * GRP:(gp + 1) * GRP],
                                  w[p0:p0 + NS, gp, :, :].rearrange("p m c -> p (m c)"),
                                  c[p0:p0 + NS, gp * GRP:(gp + 1) * GRP], start=(s == 0), stop=(s == 1))
                last.then_inc(bank_full, 1)
            pe.wait_ge(*emptied("hT7"))
            pe.wait_ge(*emptied("ub3"))
            for i in range(4):
                b = start(f"xs{i}")
                w = (hTr, hTi)[i // 2]
                for g in range(16):
                    gg = 16 * (i % 2) + g
                    p0 = NS * (gg % 2)
                    last = MM(b[p0:p0 + NS, (g // 2) * NB:(g // 2 + 1) * NB], w[:, gg // 2, p0:p0 + NS],
                              ub[:, gg, :], start=True, stop=True)
                last.then_inc(bank_full, 1)
            def scores(h):
                for j in range(NT):
                    b = start(f"sc{4 * h + j}")
                    MM(b[:, 0:SEQ - j * P], kT[:, h, j * P:(j + 1) * P], qT[:, h, j * P:SEQ],
                       start=True, stop=True).then_inc(bank_full, 1)

            def head_rows(h):
                pe.wait_ge(*emptied(f"v{2 * h + 1}"))
                for m in range(2):
                    b = start(f"in{2 * h + m}")
                    for a in range(2):
                        i = 2 * m + a
                        for j in range(i + 1):
                            pe.wait_ge(*emptied(f"sc{4 * h + j}"))
                            last = MM(b[:, a * DV:(a + 1) * DV], sT[:, j, (i - j) * P:(i - j + 1) * P],
                                      vt[:, j, h * DV:(h + 1) * DV], start=(j == 0), stop=(j == i))
                    last.then_inc(bank_full, 1)

            pe.wait_ge(*emptied("k3"))
            for h in range(HEADS):
                token_major("v", C_V, hT, (h,))
                if h:
                    head_rows(h - 1)
                scores(h)
            channel_major("g", C_G, hT, KD, None, range(2))
            head_rows(HEADS - 1)
            channel_major("g", C_G, hT, KD, None, range(2, KD))
            pe.wait_ge(*emptied("in7"))
            for k in range(KD):
                b = start(f"rT{k}")
                for i in range(NT):
                    last = TR(b[:, i * P:(i + 1) * P], ret[:, i, k * P:(k + 1) * P], ident)
                last.then_inc(bank_full, 1)
            channel_major("ga", C_GA, hT, KD, None)
            pe.wait_ge(m0_ready, 1)
            pe.wait_ge(g_ready, 1)
            pe.wait_ge(scan_done, 1)
            for i in range(4):
                b = start(f"ys{i}")
                for g in range(8):
                    gg = 2 * (8 * (i // 2) + g) + i % 2
                    p0, gp, col = NS * (gg % 2), gg // 2, g * NB
                    MM(b[:, col:col + NB], m0T[:, gg, :], ub[:, gg, :],
                       start=True, stop=False)
                    MM(b[:, col + 1:col + NB], gre[p0:p0 + NS, gp, :, :].rearrange("p m c -> p (m c)"),
                       xr[p0:p0 + NS, gp, 0:NB - 1], start=False, stop=False)
                    last = MM(b[:, col + 1:col + NB], gim[p0:p0 + NS, gp, :, :].rearrange("p m c -> p (m c)"),
                              xi[p0:p0 + NS, gp, 0:NB - 1], start=False, stop=True)
                last.then_inc(bank_full, 1)
            for i in range(8):
                if i % 4 == 0:
                    pe.wait_ge(*emptied(f"ys{i // 2 + 1}"))
                b = start(f"yc{i}")
                for g in range(4):
                    last = TR(b[0:NB, g * P:(g + 1) * P], ysb[:, 4 * i + g, :], ident)
                last.then_inc(bank_full, 1)
            for c in range(4):
                pe.wait_ge(*emptied(f"yc{2 * c + 1}"))
                b = start(f"yd{c}")
                for r in range(BT):
                    last = TR(b[:, r * NB:(r + 1) * NB], yjr[0:NB, r, c * P:(c + 1) * P], ident[0:NB, 0:NB])
                last.then_inc(bank_full, 1)
            channel_major("gb", C_GB, hT, KD, None)
            pe.wait_ge(z_split, 1)
            channel_major("z", C_GLU, (z_hi, z_lo), 4, None)
            pe.wait_ge(gated_split, 2)
            channel_major("yb", C_BRET, (gs_hi, gs_lo), KD, None)
            channel_major("ya", C_BS5, (zg_hi, zg_lo), 4, lambda k: (zg_split, k + 1))
            token_major("wo", C_OUT, (mg_hi, mg_lo), range(4), lambda k: (mg_split, k + 1))
            b = [start(f"h2T{k}") for k in range(KD)]
            for i in range(NT):
                pe.wait_ge(h2_ready, i + 1)
                for k in range(KD):
                    last = TR(b[k][:, i * P:(i + 1) * P], h2[:, i, k * P:(k + 1) * P], ident)
                    if i == NT - 1:
                        last.then_inc(bank_full, 1)
            pe.wait_ge(moe_in, 32)
            b = start("lc0")
            for k in range(KD):
                pe.wait_ge(*emptied(f"h2T{k}"))
                last = MM(b[0:E, :], rw_s[:, k, :], h2T[:, k, :], start=(k == 0), stop=(k == KD - 1))
            last.then_inc(bank_full, 1)
            pe.wait_ge(*emptied("lc0"))
            b = start("lg0")
            for i in range(NT):
                last = TR(b[:, i * E:(i + 1) * E], lgT[:, i * P:(i + 1) * P], ident[0:E, 0:E])
            last.then_inc(bank_full, 1)
            pe.wait_ge(hot_ready, 1)
            b = start("rk0")
            MM(b[:, 0:(NT + 1) * E], ones, before_sum[:, :, :].rearrange("p i e -> p (i e)"), start=True, stop=False)
            MM(b[:, 0:NT * E], con("before"), hot[:, :, :].rearrange("p i e -> p (i e)"),
               start=False, stop=True).then_inc(bank_full, 1)
            pe.wait_ge(digits_ready, 1)
            b = start("tb0")
            NC, NI = NA // P, N_ITEMS + 1
            for c in range(NC):
                MM(b[:, 0:2 * NI], in_slot[:, c, :], digits[:, c, :, :].rearrange("p v t -> p (v t)"),
                   start=(c == 0), stop=(c == NC - 1))
            TR(b[0:1, 2 * NI:3 * NI], item_c, ident[0:NI, 0:NI]).then_inc(bank_full, 1)
            pe.wait_ge(gte_ready, 1)
            b = start("gT0")
            for i in range(NT):
                last = TR(b[0:E, i * P:(i + 1) * P], gte[:, i, :], ident)
            last.then_inc(bank_full, 1)
            pe.wait_ge(tab_ready, 1)
            pe.wait_ge(b1_ready, 1)
            pe.sem_inc(y_full, W2C)

            def rows(moves):
                pe.wait_ge(moved, moves)
                for h in range(2):
                    for k in range(4):
                        last = TR(bank[4 + h][:, k * P:(k + 1) * P], xe[:, (4 * h + k) * P:(4 * h + k + 1) * P], ident)
                    last.then_inc(x_full, 1)

            def products(dst, hi, lo, slot, c, k_tiles, ready=None, started=False):
                w_l = w_lo[slot].rearrange("p (k n) -> p k n", k=k_tiles)
                w_h = w_hi[c % N_HI].rearrange("p (k n) -> p k n", k=k_tiles)
                for k in range(k_tiles):
                    wait = ready(k) if ready else None
                    if wait:
                        pe.wait_ge(*wait)
                    for n, (a, w) in enumerate(((hi, w_h), (hi, w_l), (lo, w_h))):
                        last = MM(dst, a[:, k, :], w[:, k, :], start=(k == 0 and n == 0 and not started),
                                  stop=(k == k_tiles - 1 and n == 2))
                return last

            def transpose_tile(i, j):
                pe.wait_ge(act_ready, i * FT + (j + 1))
                if j >= 2:
                    pe.wait_ge(a_split, i * FT + (j - 1))
                TR(bank[2 + j % 2][:, 0:P], a_t[:, j % 3, :], ident).then_inc(a_full, 1)

            def item(i):
                for j in range(FT):
                    if j == 0:
                        pe.wait_ge(pick_ready, i + 1)
                    pe.wait_ge(gu_empty, i * FT + (j + 1))
                    dst = bank[j % 2][:, 0:CW]
                    MM(dst, pick, b1_hl[:, j * CW:(j + 1) * CW], start=True, stop=False)
                    if j == 0:
                        pe.wait_ge(x_split, i * 2 + 2)
                    pe.wait_ge(*split(i, j))
                    products(dst, x_hi, x_lo, item_chunk(i, j)[0], j, KD, started=True).then_inc(gu_full, 1)
                    if j > 1:
                        transpose_tile(i, j - 2)
                rows(i * 32 + 32)
                transpose_tile(i, FT - 2)

                def ready(k):
                    if k == FT - 2:
                        transpose_tile(i, FT - 1)
                    return (a_split, i * FT + (k + 1)) if k == 0 or k > FT - 4 else None

                for c in range(W2C):
                    pe.wait_ge(*split(i, FT + c))
                    pe.wait_ge(y_empty, i * W2C + (c + 1))
                    products(bank[6 + c % 2][:, 0:CW], a_hi, a_lo, item_chunk(i, FT + c)[0], FT + c, FT,
                             None if c else ready).then_inc(y_full, 1)

            rows(16)
            n = pe.value_load(item_e[0:1, N_ITEMS + 1:N_ITEMS + 2], min_val=E, max_val=N_ITEMS)
            with pe.Fori(0, E) as i:
                item(i)
            with pe.If(n > E):
                with pe.Fori(E, N_ITEMS) as i:
                    with pe.If(i < n):
                        item(i)
                    pe.nop()
            pe.nop()
            pe.wait_ge(y_empty, n * W2C + 2)
            pe.wait_ge(*emptied("gT0"))
            for n in range(8):
                b = start(f"b2{n}")
                MM(b[:, :], gTs[:, (n // 2) * P:(n // 2 + 1) * P], b2_s[:, (n % 2) * 512:(n % 2 + 1) * 512],
                   start=True, stop=True).then_inc(bank_full, 1)


_INPUTS = ("x", "pos", "wt", "we", "par", "s5bc", "b1", "b2", "rw", "g_ffn", "g_fin", "cst", "dmask")


def _constants():
    i = np.arange(P)
    assign = np.concatenate([TOPK * (t * P + i)[:, None] + np.arange(TOPK) for t in range(NT)], 1)
    c = {
        "ident": np.eye(P), "before": (i[:, None] < i[None, :]), "ones": np.ones((P, P)),
        "expert_id": np.broadcast_to(np.arange(E), (P, E)),
        "item_id": np.broadcast_to(np.arange(N_ITEMS + 1), (P, N_ITEMS + 1)),
        "pick": (i[:, None] % E == np.arange(E)) & (i[:, None] < 2 * E),
        "row": i[:, None], "slot_id": np.broadcast_to(i, (P, P)),
        "id_hi": assign // ID_LO + 1, "id_lo": assign % ID_LO,
        "inv_freq": (np.float32(10000.0) ** (-(i % (DK // 2)).astype(np.float32) / np.float32(DK // 2)))[:, None],
        "sin_sign": np.where(i < DK // 2, -1.0, 1.0)[:, None],
    }
    cst = np.concatenate([np.asarray(c[n], np.float32) for n in CST], 1)
    lag = np.arange(SEQ)[None, :] - i[:, None]
    dm = [np.where(lag >= 0, (1.0 - 2.0 ** (-5.0 - h)) ** np.maximum(lag, 0), 0.0) for h in range(HEADS)]
    return np.ascontiguousarray(cst), np.stack(dm, 1).astype(np.float32)


def kernel(x, positions, norm_mix_g, w_in, s5_lambda_re, s5_lambda_im, s5_log_dt, s5_b_re, s5_b_im,
           s5_c_re, s5_c_im, s5_d, s5_w_glu, s5_b_glu, ret_gn_g, w_branch_s5, w_branch_ret, w_out,
           norm_ffn_g, router_w, router_b, expert_w1, expert_b1, expert_w2, expert_b2, norm_final_g):
    import concourse.bacc as bacc
    from concourse.bass_utils import run_bass_kernel_spmd

    f = np.asarray

    def chunks(w):
        w = f(w)
        k = w.shape[0] // P
        return w.reshape(k, P, -1, CH // k).transpose(2, 1, 0, 3).reshape(-1, P, CH)

    def cols(v):
        return f(v).reshape(-1, P).T

    def states(v):
        v = f(v).reshape(GP, 2 * NS, -1)
        return v.transpose(1, 0, 2).reshape(P, -1)

    cst, dmask = _constants()
    w1 = f(expert_w1)[0].reshape(E, KD, P, FT, P, 2).transpose(0, 3, 2, 1, 5, 4).reshape(E, FT, P, CH)
    w2 = f(expert_w2)[0].reshape(E, FT, P, W2C, CW).transpose(0, 3, 2, 1, 4).reshape(E, W2C, P, CH)
    par = {
        "norm_mix": cols(norm_mix_g[0]), "ret_gn": cols(ret_gn_g[0]), "d_skip": cols(s5_d[0]),
        "b_glu": cols(s5_b_glu[0]), "lam_re": states(s5_lambda_re[0]), "lam_im": states(s5_lambda_im[0]),
        "log_dt": states(np.broadcast_to(f(s5_log_dt)[0][:, None], (NG, NS))),
        "router_b": np.broadcast_to(f(router_b)[0][None, :], (P, E)),
    }
    arrays = {
        "x": f(x)[0], "pos": f(positions), "we": np.concatenate([w1, w2], 1),
        "wt": np.concatenate([chunks(w[0]) for w in (w_in, s5_w_glu, w_branch_ret, w_branch_s5, w_out)]),
        "s5bc": np.concatenate([states(f(v)) for v in (s5_b_re[0], s5_b_im[0], f(s5_c_re)[0].transpose(0, 2, 1),
                                                        f(s5_c_im)[0].transpose(0, 2, 1))], 1),
        "par": np.concatenate([par[n] for n in PAR], 1),
        "b1": f(expert_b1)[0].reshape(E, FT, P, 2).transpose(0, 1, 3, 2).reshape(E, 2 * DFF),
        "b2": f(expert_b2)[0], "rw": f(router_w)[0].reshape(KD, P, E).transpose(1, 0, 2),
        "g_ffn": f(norm_ffn_g), "g_fin": f(norm_final_g)[None, :], "cst": cst, "dmask": dmask,
    }
    nc = bacc.Bacc("TRN2", target_bir_lowering=False, num_devices=1)
    ins, aps = {}, []
    for n in _INPUTS:
        a = np.ascontiguousarray(arrays[n])
        ins[n] = a
        aps.append(nc.dram_tensor(n, a.shape, mybir.dt.from_np(a.dtype), kind="ExternalInput").ap())
    out = nc.dram_tensor("out", (SEQ, D), F32, kind="ExternalOutput").ap()
    build(nc, *aps, out)
    r = run_bass_kernel_spmd(nc, [ins], core_ids=[0])
    return f(r.results[0]["out"]).reshape(1, SEQ, D)
```
